# Optimizing a Trainium2 kernel written in Bass

```python
import math
import jax, jax.numpy as jnp
from jax import lax
import numpy as np

D_MODEL = 1024
BATCH = 1
SEQ = 256
DEPTH = 2

N_MIXERS = 2
CONV_WIDTH = 3
HEAD_DIM = 64
N_Q_HEADS = D_MODEL // HEAD_DIM
N_KV_HEADS = 4
GROUP = N_Q_HEADS // N_KV_HEADS
WINDOW = 128
BLOCK = 128
D_FF = ((8 * D_MODEL // 3 + 255) // 256) * 256
QKV_WIDTH = (N_Q_HEADS + 2 * N_KV_HEADS) * HEAD_DIM
N_CONV_LAYERS = (DEPTH + 1) // 2
N_ATTN_LAYERS = DEPTH // 2
EPS = 1e-6


def rmsnorm(x, gain):
    xf = x.astype(jnp.float32)
    r = lax.rsqrt(jnp.mean(xf * xf, axis=-1, keepdims=True) + EPS)
    return (xf * r).astype(x.dtype) * gain

def alibi_slopes():
    h = jnp.arange(1, N_Q_HEADS + 1, dtype=jnp.float32)
    return jnp.exp2(-8.0 * h / N_Q_HEADS)

def short_conv_mixer(h, w_in, conv_w, w_out):
    d = h.shape[-1]
    bcx = h @ w_in
    b_gate, c_gate, xv = jnp.split(bcx, 3, axis=-1)
    u = b_gate * xv
    y = lax.conv_general_dilated(
        u, conv_w[:, None, :].astype(u.dtype),
        window_strides=(1,), padding=[(CONV_WIDTH - 1, 0)],
        dimension_numbers=('NWC', 'WIO', 'NWC'), feature_group_count=d)
    return (c_gate * y) @ w_out

def swa_sink_attention(h, w_qkv, q_gain, k_gain, sinks, w_o):
    bsz, s, _ = h.shape
    nb = s // BLOCK
    qkv = h @ w_qkv
    q_end = N_Q_HEADS * HEAD_DIM
    k_end = q_end + N_KV_HEADS * HEAD_DIM
    q = qkv[..., :q_end].reshape(bsz, s, N_KV_HEADS, GROUP, HEAD_DIM)
    k = qkv[..., q_end:k_end].reshape(bsz, s, N_KV_HEADS, HEAD_DIM)
    v = qkv[..., k_end:].reshape(bsz, s, N_KV_HEADS, HEAD_DIM)
    q = rmsnorm(q, q_gain)
    k = rmsnorm(k, k_gain)

    qb = q.reshape(bsz, nb, BLOCK, N_KV_HEADS, GROUP, HEAD_DIM)

    def band(t):
        tp = jnp.pad(t, ((0, 0), (BLOCK, 0), (0, 0), (0, 0)))
        tb = tp.reshape(bsz, nb + 1, BLOCK, N_KV_HEADS, HEAD_DIM)
        return jnp.concatenate([tb[:, :-1], tb[:, 1:]], axis=2)

    kw = band(k)
    vw = band(v)

    scale = 1.0 / math.sqrt(HEAD_DIM)
    scores = jnp.einsum('bnqkgd,bnskd->bnkgqs', qb, kw).astype(jnp.float32) * scale

    qi = jnp.arange(BLOCK)[:, None]
    kj = jnp.arange(2 * BLOCK)[None, :]
    dist = qi + BLOCK - kj
    key_pos = (jnp.arange(nb) * BLOCK - BLOCK)[:, None, None] + kj[None]
    mask = (dist >= 0)[None] & (dist < WINDOW)[None] & (key_pos >= 0)

    slopes = alibi_slopes().reshape(N_KV_HEADS, GROUP)
    alibi = -slopes[:, :, None, None] * dist.astype(jnp.float32)[None, None]
    scores = scores + alibi[None, None]
    scores = jnp.where(mask[None, :, None, None], scores, -jnp.inf)

    sink = sinks.astype(jnp.float32).reshape(N_KV_HEADS, GROUP)
    sink_col = jnp.broadcast_to(sink[None, None, :, :, None, None],
                                scores.shape[:-1] + (1,))
    logits = jnp.concatenate([scores, sink_col], axis=-1)
    p = jax.nn.softmax(logits, axis=-1)[..., :-1]

    out = jnp.einsum('bnkgqs,bnskd->bnqkgd', p.astype(vw.dtype), vw)
    out = out.reshape(bsz, s, N_Q_HEADS * HEAD_DIM)
    return out @ w_o

def swiglu_ffn(h, w_gate_up, w_down):
    gu = h @ w_gate_up
    g, u = jnp.split(gu, 2, axis=-1)
    return (jax.nn.silu(g) * u) @ w_down

def first_inputs(seed: int = 0) -> dict:
    key = jax.random.key(seed)
    ks = jax.random.split(key, 14)
    f32 = jnp.float32
    d = D_MODEL

    def w(k, shape, fan_in):
        return jax.random.normal(k, shape, f32) * (fan_in ** -0.5)

    return {
        "x": jax.random.normal(ks[0], (BATCH, SEQ, d), f32),
        "conv_w_in": w(ks[1], (N_CONV_LAYERS, d, 3 * d), d),
        "conv_w": w(ks[2], (N_CONV_LAYERS, CONV_WIDTH, d), CONV_WIDTH),
        "conv_w_out": w(ks[3], (N_CONV_LAYERS, d, d), d),
        "attn_w_qkv": w(ks[4], (N_ATTN_LAYERS, d, QKV_WIDTH), d),
        "attn_q_gain": 1.0 + 0.05 * jax.random.normal(ks[5], (N_ATTN_LAYERS, HEAD_DIM), f32),
        "attn_k_gain": 1.0 + 0.05 * jax.random.normal(ks[6], (N_ATTN_LAYERS, HEAD_DIM), f32),
        "attn_sinks": 0.5 * jax.random.normal(ks[7], (N_ATTN_LAYERS, N_Q_HEADS), f32),
        "attn_w_o": w(ks[8], (N_ATTN_LAYERS, N_Q_HEADS * HEAD_DIM, d), N_Q_HEADS * HEAD_DIM),
        "norm_mixer": 1.0 + 0.05 * jax.random.normal(ks[9], (DEPTH, d), f32),
        "norm_ffn": 1.0 + 0.05 * jax.random.normal(ks[10], (DEPTH, d), f32),
        "ffn_w_gate_up": w(ks[11], (DEPTH, d, 2 * D_FF), d),
        "ffn_w_down": w(ks[12], (DEPTH, D_FF, d), D_FF),
    }

def first_block(x, conv_w_in, conv_w, conv_w_out, attn_w_qkv, attn_q_gain, attn_k_gain,
              attn_sinks, attn_w_o, norm_mixer, norm_ffn, ffn_w_gate_up, ffn_w_down):
    for i in range(DEPTH):
        h = rmsnorm(x, norm_mixer[i])
        j = i // N_MIXERS
        if i % N_MIXERS == 0:
            mix = short_conv_mixer(h, conv_w_in[j], conv_w[j], conv_w_out[j])
        else:
            mix = swa_sink_attention(h, attn_w_qkv[j], attn_q_gain[j], attn_k_gain[j],
                                     attn_sinks[j], attn_w_o[j])
        x = x + mix
        h = rmsnorm(x, norm_ffn[i])
        x = x + swiglu_ffn(h, ffn_w_gate_up[i], ffn_w_down[i])
    return x


A_Q_HEADS = 8
A_KV_HEADS = 2
A_BLOCK = 128
ROPE_THETA = 10000.0
B_HEADS = 8
GRID_W = 64
NA_MAX_KH = 8
NA_KW = 16
NA_QBLOCK_W = 16
NA_SPAN_W = 2 * NA_KW
A_Q_DIM = A_Q_HEADS * HEAD_DIM
A_KV_DIM = A_KV_HEADS * HEAD_DIM
B_DIM = B_HEADS * HEAD_DIM
ATTN_IN = A_Q_DIM + 2 * A_KV_DIM + 3 * B_DIM
ATTN_OUT = A_Q_DIM + B_DIM
SSM_D_INNER = 2 * D_MODEL
SSM_HEAD_DIM = 64
SSM_HEADS = SSM_D_INNER // SSM_HEAD_DIM
SSM_GROUPS = 8
SSM_STATE = 128
SSM_CONV = 5
SSM_CHUNK = 128
SSM_CONV_DIM = SSM_D_INNER + 2 * SSM_GROUPS * SSM_STATE
SSM_IN = SSM_D_INNER + SSM_CONV_DIM + 2 * SSM_HEADS
D_FF_2 = 4 * D_MODEL
DN_ALPHA = (2 * DEPTH) ** 0.25
DN_BETA = (8 * DEPTH) ** -0.25
LN_EPS = 1e-5
RMS_EPS = 1e-5
NEG_INF = -1e30
N_ATTN_LAYERS_2 = (DEPTH + 1) // 2
N_SSM_LAYERS = DEPTH // 2


def layer_norm(x, g, b):
    xf = x.astype(jnp.float32)
    mu = jnp.mean(xf, -1, keepdims=True)
    var = jnp.mean(jnp.square(xf - mu), -1, keepdims=True)
    return ((xf - mu) * lax.rsqrt(var + LN_EPS)).astype(x.dtype) * g + b

def rope(x, pos):
    half = HEAD_DIM // 2
    inv = ROPE_THETA ** (-jnp.arange(half, dtype=jnp.float32) / half)
    ang = pos.astype(jnp.float32)[:, None] * inv[None, :]
    cos = jnp.cos(ang)[None, :, None, :].astype(x.dtype)
    sin = jnp.sin(ang)[None, :, None, :].astype(x.dtype)
    x1, x2 = x[..., :half], x[..., half:]
    return jnp.concatenate([x1 * cos - x2 * sin, x2 * cos + x1 * sin], axis=-1)

def windowed_gqa_sink(q, k, v, sink):
    bsz, t = q.shape[:2]
    nb = t // A_BLOCK
    rep = A_Q_HEADS // A_KV_HEADS
    qb = q.reshape(bsz, nb, A_BLOCK, A_KV_HEADS, rep, HEAD_DIM)

    def band(u):
        ub = u.reshape(bsz, nb, A_BLOCK, A_KV_HEADS, HEAD_DIM)
        up = jnp.pad(ub, ((0, 0), (1, 1), (0, 0), (0, 0), (0, 0)))
        return jnp.concatenate([up[:, :-2], up[:, 1:-1], up[:, 2:]], axis=2)

    kb, vb = band(k), band(v)
    s = jnp.einsum('bnqgrd,bnkgd->bngrqk', qb, kb).astype(jnp.float32) * (HEAD_DIM ** -0.5)
    qi = np.arange(A_BLOCK)[:, None] + A_BLOCK
    ki = np.arange(3 * A_BLOCK)[None, :]
    kabs = (np.arange(nb)[:, None, None] - 1) * A_BLOCK + ki[None]
    valid = (np.abs(qi - ki) <= WINDOW)[None] & (kabs >= 0) & (kabs < t)
    s = jnp.where(jnp.asarray(valid)[None, :, None, None], s, NEG_INF)
    sink_l = jnp.broadcast_to(sink.astype(jnp.float32).reshape(A_KV_HEADS, rep)[None, None, :, :, None, None],
                              s.shape[:-1] + (1,))
    p = jax.nn.softmax(jnp.concatenate([s, sink_l], axis=-1), axis=-1)[..., :-1]
    o = jnp.einsum('bngrqk,bnkgd->bnqgrd', p.astype(v.dtype), vb)
    return o.reshape(bsz, t, A_Q_DIM)

def _na_static():
    ncb = GRID_W // NA_QBLOCK_W
    starts = [min(max(j * NA_QBLOCK_W - NA_KW // 2, 0), GRID_W - NA_SPAN_W) for j in range(ncb)]
    c = np.arange(GRID_W).reshape(ncb, NA_QBLOCK_W)
    cs = np.clip(c - NA_KW // 2, 0, GRID_W - NA_KW)
    kc = np.array(starts)[:, None] + np.arange(NA_SPAN_W)[None, :]
    mask = (kc[:, None, :] >= cs[:, :, None]) & (kc[:, None, :] < cs[:, :, None] + NA_KW)
    dc = np.clip(kc[:, None, :] - c[:, :, None] + NA_KW - 1, 0, 2 * NA_KW - 2)
    return starts, mask, dc

def neighborhood_attention(q, k, v, rpb):
    bsz, t = q.shape[:2]
    rows = t // GRID_W
    kh = min(NA_MAX_KH, rows)
    ncb = GRID_W // NA_QBLOCK_W
    starts, mask, dc = _na_static()
    qg = q.reshape(bsz, rows, ncb, NA_QBLOCK_W, B_HEADS, HEAD_DIM)
    kg = k.reshape(bsz, rows, GRID_W, B_HEADS, HEAD_DIM)
    vg = v.reshape(bsz, rows, GRID_W, B_HEADS, HEAD_DIM)
    mask_j = jnp.asarray(mask)[:, :, None, :]
    scale = HEAD_DIM ** -0.5

    def row_step(r):
        rs = jnp.clip(r - kh // 2, 0, rows - kh)
        k_rows = lax.dynamic_slice_in_dim(kg, rs, kh, axis=1)
        v_rows = lax.dynamic_slice_in_dim(vg, rs, kh, axis=1)
        k_blk = jnp.stack([k_rows[:, :, s0:s0 + NA_SPAN_W] for s0 in starts], axis=1)
        v_blk = jnp.stack([v_rows[:, :, s0:s0 + NA_SPAN_W] for s0 in starts], axis=1)
        q_r = lax.dynamic_index_in_dim(qg, r, axis=1, keepdims=False)
        s = jnp.einsum('bjqhd,bjakhd->bhjqak', q_r, k_blk).astype(jnp.float32) * scale
        dr = rs + jnp.arange(kh) - r + NA_MAX_KH - 1
        bias = rpb[:, dr][:, :, dc].transpose(0, 2, 3, 1, 4)
        s = jnp.where(mask_j, s + bias.astype(jnp.float32), NEG_INF)
        p = jax.nn.softmax(s.reshape(s.shape[:-2] + (kh * NA_SPAN_W,)), axis=-1).reshape(s.shape)
        o = jnp.einsum('bhjqak,bjakhd->bjqhd', p.astype(v.dtype), v_blk)
        return o.reshape(bsz, GRID_W, B_DIM)

    out = lax.map(row_step, jnp.arange(rows))
    return out.transpose(1, 0, 2, 3).reshape(bsz, t, B_DIM)

def attention_mixer(x, w_in, sink, rpb, w_out):
    bsz, t, _ = x.shape
    h = x @ w_in
    qa, ka, va, qb, kb, vb = jnp.split(
        h, [A_Q_DIM, A_Q_DIM + A_KV_DIM, A_Q_DIM + 2 * A_KV_DIM,
            A_Q_DIM + 2 * A_KV_DIM + B_DIM, A_Q_DIM + 2 * A_KV_DIM + 2 * B_DIM], axis=-1)
    pos = jnp.arange(t)
    qa = rope(qa.reshape(bsz, t, A_Q_HEADS, HEAD_DIM), pos)
    ka = rope(ka.reshape(bsz, t, A_KV_HEADS, HEAD_DIM), pos)
    va = va.reshape(bsz, t, A_KV_HEADS, HEAD_DIM)
    oa = windowed_gqa_sink(qa, ka, va, sink)
    shp = (bsz, t, B_HEADS, HEAD_DIM)
    ob = neighborhood_attention(qb.reshape(shp), kb.reshape(shp), vb.reshape(shp), rpb)
    return jnp.concatenate([oa, ob], axis=-1) @ w_out

def depthwise_conv_centred(u, w, b):
    c = u.shape[-1]
    pad = SSM_CONV // 2
    out = lax.conv_general_dilated(u, w[:, None, :].astype(u.dtype), window_strides=(1,),
                                   padding=[(pad, pad)], dimension_numbers=('NWC', 'WIO', 'NWC'),
                                   feature_group_count=c)
    return out + b

def ssd_chunked(x, dt, a_neg, bm, cm):
    bsz, t = x.shape[:2]
    nc, L, G, R = t // SSM_CHUNK, SSM_CHUNK, SSM_GROUPS, SSM_HEADS // SSM_GROUPS
    x = x.astype(jnp.float32)
    dt = dt.astype(jnp.float32)
    xc = (x * dt[..., None]).reshape(bsz, nc, L, G, R, SSM_HEAD_DIM)
    a = (dt * a_neg.astype(jnp.float32)).reshape(bsz, nc, L, G, R).transpose(0, 1, 3, 4, 2)
    acum = jnp.cumsum(a, axis=-1)
    bc = bm.astype(jnp.float32).reshape(bsz, nc, L, G, SSM_STATE)
    cc = cm.astype(jnp.float32).reshape(bsz, nc, L, G, SSM_STATE)
    tri = jnp.tril(jnp.ones((L, L), dtype=bool))
    lmat = jnp.exp(jnp.where(tri, acum[..., :, None] - acum[..., None, :], -jnp.inf))
    cb = jnp.einsum('bclgn,bcsgn->bcgls', cc, bc)
    y_diag = jnp.einsum('bcgrls,bcsgrp->bclgrp', cb[:, :, :, None] * lmat, xc)
    decay_states = jnp.exp(acum[..., -1:] - acum)
    states = jnp.einsum('bcsgn,bcgrs,bcsgrp->bcgrpn', bc, decay_states, xc)
    chunk_decay = jnp.exp(acum[..., -1])

    def step(h, inp):
        st, dec = inp
        return h * dec[..., None, None] + st, h

    h0 = jnp.zeros((bsz, G, R, SSM_HEAD_DIM, SSM_STATE), jnp.float32)
    _, prev = lax.scan(step, h0, (jnp.moveaxis(states, 1, 0), jnp.moveaxis(chunk_decay, 1, 0)))
    prev = jnp.moveaxis(prev, 0, 1)
    y_off = jnp.einsum('bclgn,bcgrpn,bcgrl->bclgrp', cc, prev, jnp.exp(acum))
    return (y_diag + y_off).reshape(bsz, t, SSM_HEADS, SSM_HEAD_DIM)

def mamba2_bidir_mixer(x, w_in, conv_w, conv_b, dt_bias, a_log, d_skip, norm_w, w_out):
    bsz, t, _ = x.shape
    zxbcdt = x @ w_in
    z, xbc, dt = jnp.split(zxbcdt, [SSM_D_INNER, SSM_D_INNER + SSM_CONV_DIM], axis=-1)
    xbc = jax.nn.silu(depthwise_conv_centred(xbc, conv_w, conv_b))
    xs, bm, cm = jnp.split(xbc, [SSM_D_INNER, SSM_D_INNER + SSM_GROUPS * SSM_STATE], axis=-1)
    xs = xs.reshape(bsz, t, SSM_HEADS, SSM_HEAD_DIM)
    bm = bm.reshape(bsz, t, SSM_GROUPS, SSM_STATE)
    cm = cm.reshape(bsz, t, SSM_GROUPS, SSM_STATE)
    dt = jax.nn.softplus((dt + dt_bias).astype(jnp.float32))
    dt_f, dt_b = dt[..., :SSM_HEADS], dt[..., SSM_HEADS:]
    a_neg = -jnp.exp(a_log.astype(jnp.float32))
    y_f = ssd_chunked(xs, dt_f, a_neg[0], bm, cm)
    flip = lambda u: jnp.flip(u, axis=1)
    y_b = flip(ssd_chunked(flip(xs), flip(dt_b), a_neg[1], flip(bm), flip(cm)))
    y = (y_f + y_b).astype(x.dtype) + xs * d_skip[:, None]
    y = y.reshape(bsz, t, SSM_D_INNER) * jax.nn.silu(z)
    yg = y.astype(jnp.float32).reshape(bsz, t, SSM_GROUPS, SSM_D_INNER // SSM_GROUPS)
    yg = yg * lax.rsqrt(jnp.mean(jnp.square(yg), -1, keepdims=True) + RMS_EPS)
    y = yg.reshape(bsz, t, SSM_D_INNER).astype(x.dtype) * norm_w
    return y @ w_out

def squared_relu_mlp(x, w1, w2):
    return jnp.square(jax.nn.relu(x @ w1)) @ w2

def second_inputs(seed: int = 0) -> dict:
    key = jax.random.key(seed)
    ks = jax.random.split(key, 20)
    f32 = jnp.float32
    nrm = lambda k, shp, sc: jax.random.normal(k, shp, f32) * sc
    dt0 = jnp.exp(jax.random.uniform(ks[9], (N_SSM_LAYERS, 2 * SSM_HEADS), f32,
                                     jnp.log(1e-3), jnp.log(1e-1)))
    return {
        "x": nrm(ks[0], (BATCH, SEQ, D_MODEL), 1.0),
        "attn_w_in": nrm(ks[1], (N_ATTN_LAYERS_2, D_MODEL, ATTN_IN), D_MODEL ** -0.5),
        "attn_sink": nrm(ks[2], (N_ATTN_LAYERS_2, A_Q_HEADS), 1.0),
        "attn_rpb": nrm(ks[3], (N_ATTN_LAYERS_2, B_HEADS, 2 * NA_MAX_KH - 1, 2 * NA_KW - 1), 0.1),
        "attn_w_out": nrm(ks[4], (N_ATTN_LAYERS_2, ATTN_OUT, D_MODEL), ATTN_OUT ** -0.5 * DN_BETA),
        "ssm_w_in": nrm(ks[5], (N_SSM_LAYERS, D_MODEL, SSM_IN), D_MODEL ** -0.5),
        "ssm_conv_w": nrm(ks[6], (N_SSM_LAYERS, SSM_CONV, SSM_CONV_DIM), SSM_CONV ** -0.5),
        "ssm_conv_b": nrm(ks[7], (N_SSM_LAYERS, SSM_CONV_DIM), 0.02),
        "ssm_dt_bias": dt0 + jnp.log(-jnp.expm1(-dt0)),
        "ssm_A_log": jnp.log(jax.random.uniform(ks[10], (N_SSM_LAYERS, 2, SSM_HEADS), f32, 1.0, 16.0)),
        "ssm_D": 1.0 + nrm(ks[11], (N_SSM_LAYERS, SSM_HEADS), 0.05),
        "ssm_norm_w": 1.0 + nrm(ks[12], (N_SSM_LAYERS, SSM_D_INNER), 0.05),
        "ssm_w_out": nrm(ks[13], (N_SSM_LAYERS, SSM_D_INNER, D_MODEL), SSM_D_INNER ** -0.5 * DN_BETA),
        "mlp_w1": nrm(ks[14], (DEPTH, D_MODEL, D_FF_2), D_MODEL ** -0.5),
        "mlp_w2": nrm(ks[15], (DEPTH, D_FF_2, D_MODEL), D_FF_2 ** -0.5 * DN_BETA),
        "ln1_g": 1.0 + nrm(ks[16], (DEPTH, D_MODEL), 0.05),
        "ln1_b": nrm(ks[17], (DEPTH, D_MODEL), 0.02),
        "ln2_g": 1.0 + nrm(ks[18], (DEPTH, D_MODEL), 0.05),
        "ln2_b": nrm(ks[19], (DEPTH, D_MODEL), 0.02),
    }

def second_block(x, attn_w_in, attn_sink, attn_rpb, attn_w_out, ssm_w_in, ssm_conv_w, ssm_conv_b,
              ssm_dt_bias, ssm_A_log, ssm_D, ssm_norm_w, ssm_w_out, mlp_w1, mlp_w2,
              ln1_g, ln1_b, ln2_g, ln2_b):
    for i in range(DEPTH):
        j = i // 2
        if i % 2 == 0:
            mix = attention_mixer(x, attn_w_in[j], attn_sink[j], attn_rpb[j], attn_w_out[j])
        else:
            mix = mamba2_bidir_mixer(x, ssm_w_in[j], ssm_conv_w[j], ssm_conv_b[j], ssm_dt_bias[j],
                                     ssm_A_log[j], ssm_D[j], ssm_norm_w[j], ssm_w_out[j])
        x = layer_norm(DN_ALPHA * x + mix, ln1_g[i], ln1_b[i])
        x = layer_norm(DN_ALPHA * x + squared_relu_mlp(x, mlp_w1[i], mlp_w2[i]), ln2_g[i], ln2_b[i])
    return x


def setup_inputs(seed=0):
    out = dict(first_inputs(seed))
    for name, value in second_inputs(seed + 1).items():
        if name != "x":
            out[name + "_2"] = value
    return out


def reference(
    x, conv_w_in, conv_w, conv_w_out, attn_w_qkv, attn_q_gain, attn_k_gain, attn_sinks,
    attn_w_o, norm_mixer, norm_ffn, ffn_w_gate_up, ffn_w_down, attn_w_in_2, attn_sink_2,
    attn_rpb_2, attn_w_out_2, ssm_w_in_2, ssm_conv_w_2, ssm_conv_b_2, ssm_dt_bias_2,
    ssm_A_log_2, ssm_D_2, ssm_norm_w_2, ssm_w_out_2, mlp_w1_2, mlp_w2_2, ln1_g_2, ln1_b_2,
    ln2_g_2, ln2_b_2,
):
    x = first_block(
        x, conv_w_in, conv_w, conv_w_out, attn_w_qkv, attn_q_gain, attn_k_gain, attn_sinks,
        attn_w_o, norm_mixer, norm_ffn, ffn_w_gate_up, ffn_w_down,
    )
    return second_block(
        x, attn_w_in_2, attn_sink_2, attn_rpb_2, attn_w_out_2, ssm_w_in_2, ssm_conv_w_2,
        ssm_conv_b_2, ssm_dt_bias_2, ssm_A_log_2, ssm_D_2, ssm_norm_w_2, ssm_w_out_2, mlp_w1_2,
        mlp_w2_2, ln1_g_2, ln1_b_2, ln2_g_2, ln2_b_2,
    )


_drawn_inputs = setup_inputs


def setup_inputs(seed=0):
    import zlib

    import numpy as np

    out = dict(_drawn_inputs(seed))
    spreads = {}
    factors = {'attn_q_gain': 4.981,
     'attn_k_gain': 4.91,
     'attn_sinks': 24.669,
     'attn_sink_2': 56.764,
     'attn_rpb_2': 6.652,
     'ssm_conv_b_2': 5.511,
     'ssm_D_2': 6.99,
     'ssm_norm_w_2': 3.208}
    for name, (base, spread) in spreads.items():
        noise = np.random.default_rng([zlib.crc32(name.encode()), seed]).standard_normal(out[name].shape)
        drawn = base * np.exp(spread * noise) if base else spread * noise
        out[name] = __import__('jax').numpy.asarray(drawn.astype(out[name].dtype))
    for name, factor in factors.items():
        out[name] = (out[name] * factor).astype(out[name].dtype)
    return out
```

```python
import math
from contextlib import ExitStack

import numpy as np

import concourse.bass as bass
from concourse import mybir

F32 = mybir.dt.float32
F32R = mybir.dt.float32r
ALU = mybir.AluOpType
ACT = mybir.ActivationFunctionType
AX = mybir.AxisListType.X

P = 128
T = 256
MT = T // P
D = 1024
KT = D // P
SLOTS = 3
CHUNK = 2048
WIDE = CHUNK // KT
LEAD = 2
EPS = 1e-6
LN_EPS = 1e-5
HD = 64
D_FF = 2816
D_FF2 = 4096
QKV1 = 1536
QKV2 = 2304
ALPHA = 4 ** 0.25
SSM_IN = 6208
SSM_INNER = 2048
SSM_HEADS = 32
SSM_GROUPS = 8
SSM_TAPS = 5
TOP = 3
ACC = 4


class Loop:

    def __init__(self, trips):
        self.trips = trips


class Mark:

    def __init__(self, sem, base, stride=0, loop=None):
        self.sem, self.base, self.stride, self.loop = sem, base, stride, loop

    def back(self, trips=1):
        return Mark(self.sem, self.base - trips * self.stride, self.stride, self.loop)


class Later:

    def __init__(self):
        self.mark = None


class Queue:

    def __init__(self, sem):
        self.sem, self.count, self.ops, self.open, self.inner = sem, 0, [], None, []

    def add(self, fn, waits, inc):
        (self.ops if self.open is None else self.inner).append((fn, waits, inc))

    def do(self, fn, *waits):
        self.count += 1
        m = Mark(self.sem, self.count, 0, self.open)
        self.add(fn, waits, (self.sem, 1))
        if self.open is not None:
            self.inner_marks.append(m)
        return m

    def enter(self, loop):
        self.open, self.inner, self.inner_marks, self.at_entry = loop, [], [], self.count

    def leave(self):
        per_trip = self.count - self.at_entry
        for m in self.inner_marks:
            m.stride = per_trip
        self.count += per_trip * (self.open.trips - 1)
        if self.inner:
            self.ops.append((self.open, self.inner))
        self.open = None

    def emit(self, eng):
        known = {}

        def run(ops, loop, i):
            moving = {}
            for fn, waits, inc in ops:
                for w in waits:
                    if isinstance(w, Later):
                        w = w.mark
                    if w is None:
                        continue
                    key = id(w.sem)
                    if loop is not None and w.loop is loop and w.stride:
                        if moving.get(key, -1) >= w.base:
                            continue
                        moving[key] = w.base
                        assert w.base > 0
                        eng.wait_ge(w.sem, i * w.stride + w.base)
                    else:
                        value = w.base + (w.stride * (w.loop.trips - 1) if w.loop else 0)
                        if value <= 0 or known.get(key, 0) >= value:
                            continue
                        known[key] = value
                        eng.wait_ge(w.sem, value)
                ins = fn(eng, i)
                if inc is not None:
                    ins.then_inc(*inc)

        for op in self.ops:
            if isinstance(op[0], Loop):
                with eng.Fori(0, op[0].trips) as i:
                    run(op[1], op[0], i)
            else:
                run([op], None, 0)


def build(nc, A, stop_after=None):
    ctx = ExitStack()
    with ctx:
        sem = lambda name: ctx.enter_context(nc.semaphore(name))
        sp, act, dve, pe, pool = (Queue(sem(f"{n}_done")) for n in ("sp", "act", "dve", "pe", "pool"))
        queues = (sp, act, dve, pe, pool)
        raw_landed = [sem(f"raw_landed{s}") for s in range(SLOTS)]
        rounded = sem("chunks_rounded")
        split = sem("chunks_split")
        multiplied = sem("chunks_multiplied")

        at = [(nc.sbuf_base + 31) // 32 * 32]

        def place(name, shape, dtype=F32, offset=None):
            if offset is None:
                offset = at[0]
                at[0] += (int(np.prod(shape[1:])) * 4 + 31) // 32 * 32
            t = nc.alloc_sbuf_tensor_at(name, shape, dtype, offset=offset)
            return t, offset

        raw = [place(f"raw{s}", [P, CHUNK])[0] for s in range(SLOTS)]
        whi = [place(f"whi{s}", [P, CHUNK], F32R)[0] for s in range(SLOTS)]
        wlo = [place(f"wlo{s}", [P, CHUNK], F32R)[0] for s in range(SLOTS)]
        x, _ = place("x", [P, MT, D])
        h, h_at = place("h", [P, MT, D])
        acthi, act_at = place("acthi", [P, KT, T], F32R)
        actlo, _ = place("actlo", [P, KT, T], F32R)
        mixhi, mixhi_at = place("mixhi", [P, 2 * KT, T], F32R)
        mixlo, mixlo_at = place("mixlo", [P, 2 * KT, T], F32R)
        hidhi, hid_at = place("hidhi", [P, 3, 2, T], F32R)
        hidlo, _ = place("hidlo", [P, 3, 2, T], F32R)
        table, _ = place("table", [P, A["table"].shape[1]])
        params, _ = place("params", [P, A["params"].shape[1]])
        rows, _ = place("rows", [P, A["rows"].shape[1]])
        small, _ = place("small", [P, 896])
        lnrow, lnrow_at = place("lnrow", [P, 2, D])
        zero, zero_at = place("zero", [P, 256], F32R)
        strict, _ = place("strict", [P, 2, P], F32R)
        shared = at[0]
        ps = ctx.enter_context(nc.psum_tensor("ps", [P, 8, 512], F32))

        def bank2(b):
            return ps[:, b, :].rearrange("p (a n) -> p a n", a=2)

        def f32(ap):
            return ap.bitcast(F32)

        latest = {}
        noted, wanted = set(), {}

        def note(name, mark):
            latest[name] = mark
            noted.add(name)
            return mark

        def last(name):
            if chunk_no["loop"] is None or name in noted:
                return latest.get(name)
            return wanted.setdefault(name, Later())

        def loop_begin(trips):
            loop = Loop(trips)
            noted.clear()
            wanted.clear()
            for q in queues:
                q.enter(loop)
            chunk_no["loop"], chunk_no["entry"] = loop, chunk_no["n"]

        def loop_end():
            loop = chunk_no["loop"]
            per_trip = chunk_no["n"] - chunk_no["entry"]
            assert per_trip % SLOTS == 0
            for m, per_chunks in chunk_no["marks"]:
                m.stride = m.stride * per_trip // per_chunks
            chunk_no["marks"].clear()
            chunk_no["n"] += per_trip * (loop.trips - 1)
            chunk_no["loop"] = None
            for q in queues:
                q.leave()
            for name, later in wanted.items():
                m = latest.get(name)
                later.mark = m.back() if name in noted else m

        def bodies(n, body, peel_last=False):
            body(lambda i: 0)
            trips = n - 1 - peel_last
            if trips > 1:
                loop_begin(trips)
                body(lambda i: i + 1)
                loop_end()
            elif trips == 1:
                body(lambda i: 1)
            if peel_last and n > 1:
                body(lambda i: n - 1)

        consts = [sem(f"const_landed{n}") for n in range(6)]
        const_marks = [Mark(s, 16) for s in consts]
        for m in range(MT):
            sp.add(lambda e, i, m=m: e.dma_start(x[:, m, :], A["x"][0, m * P:(m + 1) * P, :]), (), (consts[m], 16))
        act.add(lambda e, i: e.dma_start(table[:, 0:P], A["table"][:, 0:P]), (), (consts[2], 16))
        act.add(lambda e, i: e.dma_start(params[:, :], A["params"]), (), (consts[3], 16))

        def load_later_constants(ready):
            act.add(lambda e, i: e.dma_start(table[:, P:], A["table"][:, P:]), (ready,), (consts[4], 16))
            act.add(lambda e, i: e.dma_start(rows[:, :], A["rows"].to_broadcast([P, A["rows"].shape[1]])), (), (consts[5], 16))
        *x_in, ident_in, params_in, table_in, rows_in = const_marks
        zeroed = pool.do(lambda e, i: e.memset(f32(zero[:, :]), 0.0))
        minus_half = small[:, 0:64]
        halved = pool.do(lambda e, i: e.memset(minus_half, -0.5))

        chunk_no = {"n": 0, "loop": None, "entry": 0, "marks": [], "total": TOTAL_CHUNKS if stop_after is None else STOPS[stop_after]}

        def chunk_mark(sem_, base, grows=1, per_chunks=1):
            loop = chunk_no["loop"]
            m = Mark(sem_, base, grows if loop else 0, loop)
            if loop is not None:
                chunk_no["marks"].append((m, per_chunks))
            return m

        def split_chunk(c):
            if chunk_no["loop"] is None and c >= chunk_no["total"]:
                return
            s = c % SLOTS
            landed = chunk_mark(raw_landed[s], 32 * (c // SLOTS + 1), 32, SLOTS)
            free = chunk_mark(multiplied, c - SLOTS + 1) if c >= SLOTS else None
            done = chunk_mark(rounded, c + 1)
            act.add(lambda e, i: e.activation(whi[s][:, :], raw[s][:, :], ACT.Copy),
                    (landed, free), (rounded, 1))
            dve.add(lambda e, i: e.tensor_tensor(wlo[s][:, :], raw[s][:, :], f32(whi[s][:, :]), ALU.subtract),
                    (done,), (split, 1))

        def chunk(src, products, *waits):
            c = chunk_no["n"]
            chunk_no["n"] += 1
            s = c % SLOTS
            for half in range(2):
                sp.add(lambda e, i, half=half: e.dma_start(*src(i, raw[s])[half]),
                       (chunk_mark(split, c - SLOTS + 1) if c >= SLOTS else None,), (raw_landed[s], 16))
            split_chunk(c + LEAD)
            pe.add(lambda e, i: products(e, i, s, whi[s], wlo[s]),
                   (chunk_mark(split, c + 1), last(f"bank {s}"), *waits), (multiplied, 1))
            return chunk_mark(multiplied, c + 1), s

        for c in range(LEAD):
            split_chunk(c)

        def columns(w, first):
            def src(i, slot):
                a = slot[:, :].rearrange("p (k n) -> p k n", k=KT)
                b = w.rearrange("(k p) n -> p k n", p=P)[:, :, bass.ds(first(i), WIDE)]
                return [(a[:, 0:4, :], b[:, 0:4, :]), (a[:, 4:8, :], b[:, 4:8, :])]
            return src

        def feature_major(xhi, xlo, k0=0):
            def mm(e, i, s, hi, lo):
                whi_, wlo_ = (w[:, :].rearrange("p (k n) -> p k n", k=KT) for w in (hi, lo))
                for f in range(2):
                    out = ps[:, s, f * T:(f + 1) * T]
                    for k in range(KT):
                        cols = slice(f * P, (f + 1) * P)
                        e.matmul(out, whi_[:, k, cols], xhi[:, k0 + k, :], start=k == 0, stop=False)
                        e.matmul(out, whi_[:, k, cols], xlo[:, k0 + k, :], start=False, stop=False)
                        last = e.matmul(out, wlo_[:, k, cols], xhi[:, k0 + k, :], start=False, stop=k == KT - 1)
                return last
            return mm

        def token_major(xhi, xlo, k0=0, first=True, last_k=True, cols=slice(0, WIDE)):
            def mm(e, i, s, hi, lo, bank=None):
                bank = s if bank is None else bank
                whi_, wlo_ = (w[:, :].rearrange("p (k n) -> p k n", k=KT)[:, :, cols] for w in (hi, lo))
                n = cols.stop - cols.start
                for m in range(MT):
                    out = ps[:, bank, m * T:m * T + n]
                    for k in range(KT):
                        xh, xl = (v[:, k0 + k, m * P:(m + 1) * P] for v in (xhi, xlo))
                        e.matmul(out, xh, whi_[:, k, :], start=k == 0, stop=False)
                        e.matmul(out, xh, wlo_[:, k, :], start=False, stop=False)
                        last = e.matmul(out, xl, whi_[:, k, :], start=False, stop=k == KT - 1)
                return last
            return mm

        ident = table[:, TAB["ident"]:TAB["ident"] + P]

        def to_features(ready, gain=None, rows_=None):
            turned = []
            rows_ = h if rows_ is None else rows_
            for m in range(MT):
                for k in range(KT):
                    out = ps[:, ACC + k // 2, (k % 2) * T + m * P:(k % 2) * T + (m + 1) * P]
                    turned.append(pe.do(lambda e, i, out=out, m=m, k=k: e.transpose(
                        out, rows_[:, m, k * P:(k + 1) * P], ident), ready[m], ident_in))
            done = {}
            for k in (0, 2, 4, 6, 1, 3, 5, 7):
                src = ps[:, ACC + k // 2, (k % 2) * T:(k % 2 + 1) * T]
                g = params[:, gain + k:gain + k + 1] if gain is not None else 1.0
                hi = act.do(lambda e, i, k=k, src=src, g=g: e.activation(acthi[:, k, :], src, ACT.Copy, scale=g),
                            turned[KT + k // 2 * 2 + 1], params_in, done.get(k - 1))
                done[k] = dve.do(lambda e, i, k=k, src=src, g=g: e.scalar_tensor_tensor(
                    out=actlo[:, k, :], in0=src, scalar=g, in1=f32(acthi[:, k, :]), op0=ALU.mult, op1=ALU.subtract), hi)
            return done[7]

        small_at = [64]

        def scratch(n):
            small_at[0] += n
            return small[:, small_at[0] - n:small_at[0]]

        def spread(ap, *dims):
            return bass.AP(ap.tensor, ap.offset, [list(ap.ap[0]), *[list(d) for d in dims]])

        def rsqrt(ready, total, n, count, eps):
            mean, out = scratch(count), scratch(count)
            ms = pool.do(lambda e, i: e.tensor_scalar(mean, total, 1.0 / n, eps, ALU.mult, ALU.add), ready, halved)
            return out, pool.do(lambda e, i: e.tensor_tensor(out, mean, minus_half[:, 0:count], ALU.pow), ms)

        def rms_norm(ready, gain):
            scaled = []
            for m in range(MT):
                total = scratch(1)
                sq = act.do(lambda e, i, m=m, total=total: e.activation(h[:, m, :], x[:, m, :], ACT.Square,
                                                                        accum_out=total), ready[m])
                rms, r = rsqrt(sq, total, D, 1, EPS)
                scaled.append(dve.do(lambda e, i, m=m, rms=rms: e.tensor_scalar(
                    h[:, m, :], x[:, m, :], rms, None, ALU.mult), r))
            return to_features(scaled, gain)

        def conv_layer(acts):
            b_sb, off = place("conv_b", [P, 2, T], offset=shared)
            u, _ = place("conv_u", [P, 2, T + 2], offset=shared + 2048)
            y, _ = place("conv_y", [P, 2, T], offset=shared + 2048 + 2112)
            cleared = pool.do(lambda e, i: e.memset(u[:, :, :], 0.0))
            w_in = A["conv_w_in"][0]

            def body(j):
                done, s = chunk(columns(w_in, lambda i: j(i) * WIDE), feature_major(acthi, actlo), acts)
                b_copied = note(f"bank {s}", act.do(lambda e, i, s=s: e.activation(b_sb[:, :, :], bank2(s), ACT.Copy),
                                                    done, last("b read")))
                done, s = chunk(columns(w_in, lambda i: j(i) * WIDE + 2 * D), feature_major(acthi, actlo))
                tap = note("b read", note(f"bank {s}", dve.do(lambda e, i, s=s: e.tensor_tensor(
                    u[:, :, 2:T + 2], bank2(s), b_sb[:, :, :], ALU.mult), done, b_copied, cleared)))
                for n in range(3):
                    for f in range(2):
                        def one(e, i, f=f, n=n):
                            w = params[:, bass.ds(j(i) * 2 + (PAR["conv_w"] + (2 - n) * KT + f), 1)]
                            src = u[:, f, 2 - n:2 - n + T]
                            if n == 0:
                                return e.tensor_scalar(y[:, f, :], src, w, None, ALU.mult)
                            return e.scalar_tensor_tensor(out=y[:, f, :], in0=src, scalar=w, in1=y[:, f, :],
                                                          op0=ALU.mult, op1=ALU.add)
                        note(f"tap {f}", dve.do(one, tap if n == 0 else last(f"tap {f}"), last("y read"), params_in))
                done, s = chunk(columns(w_in, lambda i: j(i) * WIDE + D), feature_major(acthi, actlo))
                gated = note(f"bank {s}", dve.do(lambda e, i, s=s: e.tensor_tensor(
                    y[:, :, :], bank2(s), y[:, :, :], ALU.mult), done, last("tap 0"), last("tap 1")))
                note("y read", split_mix(gated, lambda i: j(i) * 2, 2, y[:, :, :]))

            bodies(4, body)
            return last("y read")

        def split_mix(ready, first, n, src):
            hi = act.do(lambda e, i: e.activation(mixhi[:, bass.ds(first(i), n), :], src, ACT.Copy), ready)
            return dve.do(lambda e, i: e.tensor_tensor(mixlo[:, bass.ds(first(i), n), :], src,
                                                       f32(mixhi[:, bass.ds(first(i), n), :]), ALU.subtract), hi)

        def project(w, xhi, xlo, ready, add):
            for n in range(D // WIDE):
                done, s = chunk(columns(w, lambda i, n=n: n * WIDE), token_major(xhi, xlo), ready)
                m = note(f"bank {s}", add(done, bank2(s), slice(None), slice(n * WIDE, (n + 1) * WIDE)))
            return [m, m]

        def add_plain(done, src, tokens, cols):
            return dve.do(lambda e, i: e.tensor_tensor(x[:, tokens, cols], src, x[:, tokens, cols], ALU.add), done)

        def add_alpha(done, src, tokens, cols):
            return dve.do(lambda e, i: e.scalar_tensor_tensor(out=x[:, tokens, cols], in0=x[:, tokens, cols], scalar=ALPHA,
                                                              in1=src, op0=ALU.mult, op1=ALU.add), done)

        gate_sb, _ = place("gate_sb", [P, 2, T], offset=shared)
        prod_sb, _ = place("prod_sb", [P, 2, 2 * T], offset=shared + 2048)

        def feed_forward(acts, up_src, n_up, down, pairs, slots, hidden, add):

            def down_products(hs, final=False):
                def mm(e, i, s, hi, lo):
                    wh, wl = (w[:, :].rearrange("p (k n) -> p k n", k=2) for w in (hi, lo))
                    for k in range(2):
                        for m in range(MT):
                            xh, xl = (v[:, hs, k, m * P:(m + 1) * P] for v in (hidhi, hidlo))
                            for a, b in ((xh, wh), (xh, wl), (xl, wh)):
                                for n in range(2):
                                    mm_ = e.matmul(ps[:, ACC + 2 * m + n, :], a, b[:, k, n * 512:(n + 1) * 512],
                                                   start=False, stop=final and k == 1 and a is xl,
                                                   skip_group_check=True)
                    return mm_
                return mm

            def down_src(t):
                def src(i, slot):
                    a = slot[:, :].rearrange("p (k n) -> p k n", k=2)
                    return [(a[:, k, :], down[bass.ds(t(i) * 2 * P + k * P, P), :]) for k in range(2)]
                return src

            def up(t, hs):
                for q in range(n_up):
                    done, s = chunk(up_src(t, q), feature_major(acthi, actlo), acts)
                    hidden(done, s, hs, q)

            def open_accumulators(e, i):
                for b in range(4):
                    for half in range(2):
                        mm = e.matmul(ps[:, ACC + b, half * T:(half + 1) * T], zero[:, 0:P], zero[:, :],
                                      start=half == 0, stop=False, skip_group_check=True)
                return mm

            peel_last = chunk_no["n"] + pairs * (n_up + 1) == chunk_no["total"]
            pe.do(open_accumulators, zeroed, acts)
            up(lambda i: 0, 0)
            assert (pairs - 1) % slots == 0

            def body(j):
                for u in range(slots):
                    before = last("hidden")
                    up(lambda i, u=u: j(i) * slots + (u + 1), (u + 1) % slots)
                    chunk(down_src(lambda i, u=u: j(i) * slots + u), down_products(u), before)

            bodies((pairs - 1) // slots, body, peel_last)
            done, _ = chunk(down_src(lambda i: pairs - 1), down_products((pairs - 1) % slots, True), last("hidden"))
            return [add(done, ps[:, ACC + 2 * m:ACC + 2 * m + 2, :].rearrange("p a n -> p (a n)"), m, slice(0, D))
                    for m in range(MT)]

        def swiglu(layer):
            w = A["ffn_w_gate_up"][layer]

            def up_src(t, q):
                def src(i, slot):
                    a = slot[:, :].rearrange("p (k g n) -> p g k n", k=KT, g=2)
                    return [(a[:, g, :, :], w.rearrange("(k p) n -> p k n", p=P)[
                        :, :, bass.ds(t(i) * 2 * P + (q * P + g * D_FF), P)]) for g in range(2)]
                return src

            def hidden(done, s, hs, q):
                silu = act.do(lambda e, i: e.activation(gate_sb[:, q, :], ps[:, s, 0:T], ACT.Silu),
                              done, last(f"gate {q} read"))
                prod = dve.do(lambda e, i: e.tensor_tensor(prod_sb[:, q, 0:T], ps[:, s, T:2 * T], gate_sb[:, q, :],
                                                           ALU.mult), silu, last(f"prod {q} read"))
                note(f"bank {s}", prod)
                note(f"gate {q} read", prod)
                hi = act.do(lambda e, i: e.activation(hidhi[:, hs, q, :], prod_sb[:, q, 0:T], ACT.Copy), prod)
                lo = dve.do(lambda e, i: e.tensor_tensor(hidlo[:, hs, q, :], prod_sb[:, q, 0:T],
                                                         f32(hidhi[:, hs, q, :]), ALU.subtract), hi)
                note(f"prod {q} read", lo)
                note("hidden", lo)

            def run(acts):
                return feed_forward(acts, up_src, 2, A["ffn_w_down"][layer], D_FF // (2 * P), 2, hidden, add_plain)
            return run

        def squared_relu(layer):
            w = A["mlp_w1_2"][layer]

            def up_src(t, q):
                return columns(w, lambda i: t(i) * WIDE)

            def hidden(done, s, hs, q):
                relu = act.do(lambda e, i: e.activation(gate_sb[:, :, :], bank2(s), ACT.Relu), done, last("gate read"))
                note(f"bank {s}", relu)
                prod = prod_sb[:, 0, :].rearrange("p (a n) -> p a n", a=2)
                sq = dve.do(lambda e, i: e.tensor_tensor(prod, gate_sb[:, :, :], gate_sb[:, :, :], ALU.mult),
                            relu, last("prod read"))
                note("gate read", sq)
                hi = act.do(lambda e, i: e.activation(hidhi[:, hs, :, :], prod, ACT.Copy), sq)
                lo = dve.do(lambda e, i: e.tensor_tensor(hidlo[:, hs, :, :], prod, f32(hidhi[:, hs, :, :]),
                                                         ALU.subtract), hi)
                note("prod read", lo)
                note("hidden", lo)

            def run(acts):
                return feed_forward(acts, up_src, 1, A["mlp_w2_2"][layer], D_FF2 // (2 * P), 3, hidden, add_alpha)
            return run

        def layer_norm(ready, g, b):
            out = []
            ln_sem = sem(f"ln_landed{len(ln_sems)}")
            ln_sems.append(ln_sem)
            for n, v in enumerate((g, b)):
                act.add(lambda e, i, n=n, v=v: e.dma_start(lnrow[:, n, :], v.rearrange("(a d) -> a d", a=1).to_broadcast([P, D])),
                        (latest.get("lnrow"),), (ln_sem, 16))
            landed = Mark(ln_sem, 32)
            for m in range(MT):
                stats, mv = scratch(12), scratch(2)
                for n in range(2):
                    st = dve.do(lambda e, i, m=m, n=n, stats=stats: e.bn_stats(
                        stats[:, 6 * n:6 * n + 6], x[:, m, 512 * n:512 * (n + 1)]), ready[m])
                ag = dve.do(lambda e, i, mv=mv, stats=stats: e.bn_aggr(mv, stats), st)
                rstd, r = rsqrt(ag, mv[:, 1:2], 1, 1, LN_EPS)
                a = dve.do(lambda e, i, m=m, mv=mv: e.scalar_tensor_tensor(
                    out=x[:, m, :], in0=x[:, m, :], scalar=mv[:, 0:1], in1=lnrow[:, 0, :], op0=ALU.subtract,
                    op1=ALU.mult), ag, landed)
                out.append(dve.do(lambda e, i, m=m, rstd=rstd: e.scalar_tensor_tensor(
                    out=x[:, m, :], in0=x[:, m, :], scalar=rstd, in1=lnrow[:, 1, :], op0=ALU.mult,
                    op1=ALU.add), a, r))
            latest["lnrow"] = out[-1]
            return out
        ln_sems = []

        qkv, _ = place("qkv", [P, MT, QKV2], offset=shared)
        q_t = (place("q_hi", [P, 8, T], F32R, offset=shared + 18432)[0], place("q_lo", [P, 8, T], F32R, offset=act_at)[0])
        k_t = (place("k_hi", [P, 6, T], F32R, offset=shared + 26624)[0],
               place("k_lo", [P, 6, T], F32R, offset=act_at + 8192)[0])
        bias, _ = place("bias", [P, 2, 4, T], offset=lnrow_at)
        bias_more, _ = place("bias_more", [P, 2, 4, T], offset=mixlo_at + 8192)
        probs, _ = place("probs", [P, 2, 4, T], offset=h_at)
        probs_t, _ = place("probs_t", [P, 2, 2, 4, P], offset=mixhi_at + 8192)
        SCALE = HD ** -0.5
        HEADS = (0, 2, 1, 3)

        def wide_project(w, width, acts):
            def body(j):
                for u in range(3):
                    done, s = chunk(columns(w, lambda i, u=u: j(i) * 3 * WIDE + u * WIDE),
                                    token_major(acthi, actlo), acts)
                    note("qkv", note(f"bank {s}", act.do(lambda e, i, u=u, s=s: e.activation(
                        qkv[:, :, bass.ds(j(i) * 3 * WIDE + u * WIDE, WIDE)], bank2(s), ACT.Copy), done)))
            bodies(width // (3 * WIDE), body)
            return last("qkv")

        def turn_heads(ready, sources, dest, banks, gain=None):
            marks = []
            for n in range(0, len(sources), 2):
                b = banks[n // 2]
                for f, source in enumerate(sources[n:n + 2]):
                    for m in range(MT):
                        turned = pe.do(lambda e, i, b=b, f=f, m=m, source=source: e.transpose(
                            ps[:, b, f * T + m * P:f * T + (m + 1) * P], source(m), ident), ready[m])
                k = len(sources[n:n + 2])
                g = params[:, gain:gain + 1] if gain is not None else 1.0
                hi = act.do(lambda e, i, b=b, n=n, k=k, g=g: e.activation(
                    dest[0][:, n:n + k, :], bank2(b)[:, 0:k, :], ACT.Copy, scale=g), turned)
                marks.append(dve.do(lambda e, i, b=b, n=n, k=k, g=g: e.scalar_tensor_tensor(
                    out=dest[1][:, n:n + k, :], in0=bank2(b)[:, 0:k, :], scalar=g, in1=f32(dest[0][:, n:n + k, :]),
                    op0=ALU.mult, op1=ALU.subtract), hi))
            return marks[-1]

        def attend(ready, groups):
            N = len(groups)
            rows_of = [scratch(4 * 6) for _ in range(2)]
            scored, biased, exped, normed, turned, copied, mixed, split_ = ({} for _ in range(8))

            def score(n):
                if n >= N:
                    return
                g, b0, nk = groups[n], 2 * (n % 2), groups[n]["nk"] * P

                def mm(e, i):
                    for w, u in enumerate(HEADS):
                        base = (u % 2) * HD
                        for n_, (a, b) in enumerate(((0, 0), (0, 1), (1, 0))):
                            out = e.matmul(ps[:, b0 + w // 2, (w % 2) * T:(w % 2) * T + nk],
                                           q_t[a][base:base + HD, g["q"] + u // 2, g["m"] * P:(g["m"] + 1) * P],
                                           k_t[b][base:base + HD, g["k"](u), 0:nk], start=n_ == 0, stop=n_ == 2)
                    return out
                scored[n] = pe.do(mm, ready, biased.get(n - 2))

            def weigh(n):
                if n >= N:
                    return
                g, par, nk = groups[n], n % 2, groups[n]["nk"] * P
                r = rows_of[par]
                neg, den, sunk, es = (r[:, 4 * k:4 * k + 4] for k in range(4))
                p4 = probs[:, par, :, 0:nk]
                s4 = ps[:, 2 * par:2 * par + 2, :].rearrange("p a (b n) -> p (a b) n", b=2)[:, :, 0:nk]
                biased[n] = dve.do(lambda e, i: e.scalar_tensor_tensor(out=p4, in0=s4, scalar=SCALE, in1=g["bias"],
                                                                       op0=ALU.mult, op1=ALU.add),
                                   scored[n], g["bias_ready"], turned.get(n - 2))
                top = dve.do(lambda e, i: e.tensor_reduce(neg, p4, AX, ALU.max), biased[n], exped.get(n - 2))
                if g["sink"] is None:
                    top = dve.do(lambda e, i: e.tensor_scalar(neg, neg, -1.0, None, ALU.mult), top)
                else:
                    sink, minus_sink = (spread(v, [1, 2], [2, 2]) for v in g["sink"])
                    neg4, sunk4 = (spread(v, [2, 2], [1, 2]) for v in (neg, sunk))
                    top = dve.do(lambda e, i: e.scalar_tensor_tensor(out=neg4, in0=neg4, scalar=-1.0, in1=minus_sink,
                                                                     op0=ALU.mult, op1=ALU.min), top, sinks_ready)
                    sunk_ = dve.do(lambda e, i: e.tensor_tensor(sunk4, sink, neg4, ALU.add), top)
                for u in range(4):
                    exped[n] = act.do(lambda e, i, u=u: e.activation(p4[:, u, :], p4[:, u, :], ACT.Exp,
                                                                     bias=neg[:, u:u + 1], accum_out=den[:, u:u + 1]), top,
                                      normed.get(n - 2))
                if g["sink"] is not None:
                    exped[n] = act.do(lambda e, i: e.activation(es, sunk, ACT.Exp), sunk_)

            def normalise(n):
                g, par, nk = groups[n], n % 2, groups[n]["nk"] * P
                r = rows_of[par]
                den, es, inv = r[:, 4:8], r[:, 12:16], r[:, 16:20]
                p4 = probs[:, par, :, 0:nk]
                ready_ = exped[n]
                if g["sink"] is not None:
                    ready_ = dve.do(lambda e, i: e.tensor_tensor(den, den, es, ALU.add), ready_)
                ready_ = dve.do(lambda e, i: e.reciprocal(inv, den), ready_)
                normed[n] = dve.do(lambda e, i: e.tensor_tensor(p4, p4, spread(inv, [1, 4], [0, nk]), ALU.mult), ready_)

            def turn(n):
                g, par = groups[n], n % 2

                def mm(e, i):
                    for kt in range(g["nk"]):
                        for u in range(4):
                            out = e.transpose(ps[:, 4 + kt, u * P:(u + 1) * P], probs[:, par, u, kt * P:(kt + 1) * P], ident)
                    return out
                turned[n] = pe.do(mm, normed[n], copied.get(n - 1))
                copied[n] = act.do(lambda e, i: e.activation(
                    probs_t[:, par, 0:g["nk"], :, :].rearrange("p k u n -> p k (u n)"), ps[:, 4:4 + g["nk"], :], ACT.Copy),
                    turned[n], mixed.get(n - 2))

            def mix(n):
                g, par = groups[n], n % 2

                def mm(e, i):
                    for w, u in enumerate(HEADS):
                        base = (u % 2) * HD
                        for kt in range(g["nk"]):
                            v = qkv[:, kt, g["v"](u):g["v"](u) + HD]
                            out = e.matmul(ps[base:base + HD, 6 + par, (u // 2) * P:(u // 2 + 1) * P], v,
                                           probs_t[:, par, kt, w, :], start=kt == 0, stop=kt == g["nk"] - 1)
                    return out
                mixed[n] = pe.do(mm, copied[n], split_.get(n - 2))
                src = ps[:, 6 + par, 0:2 * P].rearrange("p (a n) -> p a n", a=2)
                tiles, tokens = slice(g["out"], g["out"] + 2), slice(g["m"] * P, (g["m"] + 1) * P)
                hi[n] = act.do(lambda e, i: e.activation(mixhi[:, tiles, tokens], src, ACT.Copy), mixed[n])

            def rest(n):
                g, par = groups[n], n % 2
                src = ps[:, 6 + par, 0:2 * P].rearrange("p (a n) -> p a n", a=2)
                tiles, tokens = slice(g["out"], g["out"] + 2), slice(g["m"] * P, (g["m"] + 1) * P)
                split_[n] = dve.do(lambda e, i: e.tensor_tensor(mixlo[:, tiles, tokens], src,
                                                                f32(mixhi[:, tiles, tokens]), ALU.subtract), hi[n])
            hi = {}
            score(0)
            score(1)
            weigh(0)
            for n in range(N):
                if "bias_make" in groups[min(n + 1, N - 1)] and n + 1 < N:
                    groups[n + 1]["bias_make"](biased.get(n - 1))
                weigh(n + 1)
                normalise(n)
                score(n + 2)
                turn(n)
                if n:
                    mix(n - 1)
                if n > 1:
                    rest(n - 2)
            mix(N - 1)
            rest(N - 2)
            rest(N - 1)
            latest["lnrow"] = split_[N - 1]
            return split_[N - 1]

        minus_sinks = rows_neg = None

        def swa_layer(acts):
            sinks_ready.mark = pool.do(lambda e, i: e.tensor_scalar(negated, rows[:, 0:24], -1.0, None, ALU.mult), rows_in)
            ready = wide_project(A["attn_w_qkv"][0], QKV1, acts)
            heads = 20
            scaled, prior = [], None
            for m in range(MT):
                total = scratch(heads)
                sq_buf = spread(h[:, 0, :], [1, heads * HD])
                sq = act.do(lambda e, i, m=m: e.activation(sq_buf, qkv[:, m, 0:heads * HD], ACT.Square), ready, prior)
                prior = dve.do(lambda e, i, total=total: e.tensor_reduce(
                    total, spread(h[:, 0, :], [HD, heads], [1, HD]), AX, ALU.add), sq)
                r, r_ready = rsqrt(prior, total, HD, heads, EPS)
                dve.do(lambda e, i, m=m, r=r: e.tensor_tensor(
                    spread(qkv[:, m, :], [HD, 16], [1, HD]), spread(qkv[:, m, :], [HD, 16], [1, HD]),
                    spread(r, [1, 16], [0, HD]), ALU.mult), r_ready)
                scaled.append(dve.do(lambda e, i, m=m, r=r: e.tensor_tensor(
                    spread(qkv[:, m, QKV1:], [2 * HD, 4], [HD, 2], [1, HD]), spread(qkv[:, m, D:], [HD, 4], [0, 2], [1, HD]),
                    spread(r[:, 16:20], [1, 4], [0, 2], [0, HD]), ALU.mult), r_ready))
            q_cols = lambda p: lambda m: qkv[:, m, p * P:(p + 1) * P]
            k_cols = lambda g: lambda m: qkv[:, m, QKV1 + g * P:QKV1 + (g + 1) * P]
            turn_heads(scaled, [q_cols(p) for p in range(8)], q_t, [4, 5, 6, 7], PAR["q_gain"])
            turned = turn_heads(scaled, [k_cols(g) for g in range(4)], k_t, [0, 1], PAR["k_gain"])
            groups = []
            for m in range(MT):
                for g in range(4):
                    n = len(groups)
                    nk = m + 1
                    sink = rows[:, ROW["sinks1"] + 4 * g:ROW["sinks1"] + 4 * g + 4]
                    msink = negated[:, ROW["sinks1"] + 4 * g:ROW["sinks1"] + 4 * g + 4]

                    def make(free, n=n, m=m, g=g, nk=nk):
                        for w, u in enumerate(HEADS):
                            slope = float(np.exp2(np.float32(-8.0 * (4 * g + u + 1) / 16)))
                            groups[n]["bias_ready"] = pool.do(lambda e, i, w=w, slope=slope: e.tensor_scalar(
                                bias[:, n % 2, w, 0:nk * P], table[:, TAB["dist"] + m * T:TAB["dist"] + m * T + nk * P],
                                -slope, None, ALU.mult), table_in, free)
                    groups.append(dict(m=m, nk=nk, q=2 * g, k=lambda u, g=g: g, v=lambda u, g=g: D + 256 + g * HD,
                                       out=2 * g, sink=(sink, msink), bias=bias[:, n % 2, :, 0:nk * P], bias_make=make))
            groups[0]["bias_make"](None)
            return attend(turned, groups)

        negated = scratch(24)
        sinks_ready = Later()

        rpb_sem = sem("rpb_landed")

        def rpb_tile(m, g):
            return (bias, bias_more)[m][:, g, :, :]

        def load_rpb(free):
            rpb = A["rpb"]
            (sh, _), (sr, _), _ = rpb.ap
            for m in range(MT):
                for head in range(8):
                    for rr in range(2):
                        off = head * sh + (7 - 2 * m - rr) * sr
                        src = bass.AP(rpb.tensor, off, [[1, 64], [sr, 4], [1, 64]])
                        dst = rpb_tile(m, head // 4)[64 * rr:64 * rr + 64, HEADS.index(head % 4), :].rearrange("p (a n) -> p a n", a=4)
                        pool.add(lambda e, i, dst=dst, src=src: e.dma_start(dst, src), (free,), (rpb_sem, 16))
            return Mark(rpb_sem, 16 * 32)

        biases = {}

        def flip_rpb(m, landed):
            for g in range(2):
                tile = rpb_tile(m, g).rearrange("p u n -> p (u n)")

                def mm(e, i, g=g, tile=tile):
                    for n in range(2):
                        out = e.matmul(ps[:, 2 * g + n, :], table[:, TAB["flip"]:TAB["flip"] + P],
                                       tile[:, 512 * n:512 * n + 512], start=True, stop=True)
                    return out
                flipped = pe.do(mm, landed, biases.get((m - 1, g)))
                near = spread(table[:, TAB["near"] + m * T:], [0, 4], [1, T])
                biases[m, g] = dve.do(lambda e, i, m=m, g=g, near=near: e.tensor_tensor(
                    rpb_tile(m, g), ps[:, 2 * g:2 * g + 2, :].rearrange("p a (b n) -> p (a b) n", b=2), near, ALU.add), flipped)
            for b in range(SLOTS):
                note(f"bank {b}", biases[m, 1])

        def na_layer(acts):
            ready = wide_project(A["attn_w_in_2"][0], QKV2, acts)
            half = HD // 2
            roped, prior = [], None
            for m in range(MT):
                v = qkv[:, m, :]
                first, second = spread(v, [HD, 10], [1, half]), spread(v[:, half:], [HD, 10], [1, half])
                both = spread(v, [HD, 10], [1, HD])
                cos = spread(table[:, TAB["cos"] + m * HD:], [0, 10], [1, HD])
                minus_sin = spread(table[:, TAB["sin"] + m * HD:], [0, 10], [1, half])
                plus_sin = spread(table[:, TAB["sin"] + m * HD + half:], [0, 10], [1, half])
                rot = probs[:, m, 0:3, :].rearrange("p a n -> p (a n)")
                rot_1, rot_2, rot_all = spread(rot, [HD, 10], [1, half]), spread(rot[:, half:], [HD, 10], [1, half]), \
                    spread(rot, [HD, 10], [1, HD])
                a = dve.do(lambda e, i, o=rot_1, x_=second, s_=minus_sin: e.tensor_tensor(o, x_, s_, ALU.mult), ready, table_in)
                b = dve.do(lambda e, i, o=rot_2, x_=first, s_=plus_sin: e.tensor_tensor(o, x_, s_, ALU.mult), ready)
                c = dve.do(lambda e, i, o=both, s_=cos: e.tensor_tensor(o, o, s_, ALU.mult), a, b)
                dve.do(lambda e, i, m=m, rot=rot, v=v: e.tensor_tensor(
                    spread(probs[:, m, 3, :], [2 * HD, 2], [HD, 2], [1, HD]), spread(v[:, 512:], [HD, 2], [0, 2], [1, HD]),
                    spread(rot[:, 512:], [HD, 2], [0, 2], [1, HD]), ALU.add), c)
                roped.append(dve.do(lambda e, i, v=v, rot=rot: e.tensor_tensor(v[:, 0:512], v[:, 0:512], rot[:, 0:512],
                                                                               ALU.add), c))
            cols = lambda c0: lambda m: qkv[:, m, c0:c0 + P]
            twice = lambda g: lambda m: probs[:, m, 3, g * P:(g + 1) * P]
            turn_heads(roped, [cols(p * P) for p in range(4)] + [cols(768 + p * P) for p in range(4)], q_t, [4, 5, 6, 7])
            turned = turn_heads(roped, [twice(0), twice(1)] + [cols(1280 + p * P) for p in range(4)], k_t, [0, 1, 2])
            groups = []
            for m in range(MT):
                window = spread(table[:, TAB["window"] + m * T:], [0, 4], [1, T])
                for g in range(2):
                    c = ROW["sinks2"] + 4 * g
                    groups.append(dict(m=m, nk=2, q=2 * g, k=lambda u, g=g: g, v=lambda u, g=g: 640 + g * HD, out=2 * g,
                                       sink=(rows[:, c:c + 4], negated[:, c:c + 4]), bias=window, bias_ready=table_in))
                for g in range(2):
                    groups.append(dict(m=m, nk=2, q=4 + 2 * g, k=lambda u, g=g: 2 + 2 * g + u // 2,
                                       v=lambda u, g=g: 1792 + (4 * g + u) * HD, out=4 + 2 * g, sink=None,
                                       bias=rpb_tile(m, g), bias_ready=biases[m, g]))
            return attend(turned, groups)

        z, _ = place("z", [P, MT, SSM_INNER], offset=shared)
        xs_t, _ = place("xs_t", [P, 16, T], offset=shared + 16384)
        y, _ = place("ssm_y", [P, MT, SSM_INNER], offset=shared + 16384)
        bc_t, _ = place("bc_t", [P, 16, T], offset=mixhi_at)
        xs, _ = place("xs", [P, MT, SSM_INNER], offset=mixlo_at)
        taps, _ = place("ssm_taps", [P, 2, 2, T], offset=hid_at)
        window, _ = place("ssm_window", [P, 2, 2, T + 4], offset=hid_at + 4096)
        cum = [[place(f"cum_{d}{n}", [P, 2, 4, P], F32R, offset=o)[0] for n, o in enumerate(os)]
               for d, os in (("f", (act_at, act_at + 4096)), ("b", (act_at + 8192, h_at)))]
        decay, _ = place("decay", [P, 2, 4, P], offset=act_at + 12288)
        weight, _ = place("weight", [P, 2, 4, P], offset=h_at + 4096)
        rounding, _ = place("rounding", [P, 128], F32R, offset=h_at + 4096)
        ssm_small, _ = place("ssm_small", [P, 5, 128], offset=shared + 32768)
        gram_f, _ = place("gram_f", [P, 2, MT, P], offset=hid_at)
        gram_b, _ = place("gram_b", [P, 2, MT, P], offset=hid_at + 2048)
        gram_x, _ = place("gram_x", [P, 2, MT, P], offset=hid_at + 4096)
        xdec, _ = place("xdec", [P, 2, 4, HD], offset=hid_at + 6144)
        skipped, _ = place("skipped", [P, 2, 4, HD], offset=hid_at + 8192)
        carried, _ = place("carried", [P, 2, 4, HD], offset=hid_at + 10240)

        def ssm_layer(acts):
            w_in = A["ssm_w_in_2"][0]
            le, ge, gt, lt = (table[:, TAB[n]:TAB[n] + P] for n in ("le", "ge", "gt", "lt"))
            done, s = chunk(columns(w_in, lambda i: SSM_IN - WIDE), token_major(acthi, actlo, cols=slice(WIDE - 64, WIDE)), acts)
            v, (dt, a, a_hi, a_lo, edge) = h[:, 0, 512:640], (ssm_small[:, n, :] for n in range(5))
            two = lambda ap: spread(ap, [64, 2], [1, 64])
            over_m = lambda ap: spread(ap, [0, 2], [1, 64])
            m_ = note(f"bank {s}", dve.do(lambda e, i: e.tensor_tensor(
                two(v), bank2(s)[:, :, 0:64], over_m(rows[:, ROW["dt_bias"]:]), ALU.add), done, rows_in))
            e_, u_, ln_, same = (h[:, 0, 128 * n:128 * n + 128] for n in range(4))
            m_ = dve.do(lambda e, i: e.scalar_tensor_tensor(out=e_, in0=v, scalar=-1.0, in1=v, op0=ALU.mult, op1=ALU.min), m_)
            exp_ = act.do(lambda e, i: e.activation(e_, e_, ACT.Exp), m_)
            m_ = dve.do(lambda e, i: e.tensor_scalar(u_, e_, 1.0, None, ALU.add), exp_)
            log = act.do(lambda e, i: e.activation(ln_, u_, ACT.Ln), m_)
            m_ = dve.do(lambda e, i: e.tensor_scalar(same, u_, 1.0, None, ALU.is_equal), m_)
            m_ = dve.do(lambda e, i: e.scalar_tensor_tensor(out=u_, in0=u_, scalar=-1.0, in1=same, op0=ALU.add, op1=ALU.add), m_, log)
            m_ = dve.do(lambda e, i: e.reciprocal(u_, u_), m_)
            m_ = dve.do(lambda e, i: e.tensor_tensor(u_, u_, ln_, ALU.mult), m_)
            m_ = dve.do(lambda e, i: e.tensor_tensor(u_, u_, same, ALU.add), m_)
            m_ = dve.do(lambda e, i: e.tensor_tensor(u_, u_, e_, ALU.mult), m_)
            dt_ready = dve.do(lambda e, i: e.scalar_tensor_tensor(out=dt, in0=v, scalar=0.0, in1=u_, op0=ALU.max, op1=ALU.add), m_)
            rate = scratch(64)
            rated = act.do(lambda e, i: e.activation(rate, rows[:, ROW["a_log"]:ROW["a_log"] + 64], ACT.Exp), rows_in)
            a_ready = dve.do(lambda e, i: e.scalar_tensor_tensor(out=two(a), in0=two(dt), scalar=-1.0, in1=over_m(rate),
                                                                 op0=ALU.mult, op1=ALU.mult), dt_ready, rated)

            act.do(lambda e, i: e.activation(strict[:, 0, :], gt, ACT.Copy), table_in)
            strict_ready = act.do(lambda e, i: e.activation(strict[:, 1, :], lt, ACT.Copy))
            hi = act.do(lambda e, i: e.activation(rounding[:, :], a, ACT.Copy), a_ready)
            dve.do(lambda e, i: e.tensor_copy(a_hi, f32(rounding[:, :])), hi)
            a_split = dve.do(lambda e, i: e.tensor_tensor(a_lo, a, f32(rounding[:, :]), ALU.subtract))

            edges = pool.do(lambda e, i: e.memset(window[:, :, :, :], 0.0), acts)

            def body_into(dest, first_tile, z_first):
                def body(j):
                    for q in range(2):
                        tile = lambda i, q=q: j(i) * 4 + (2 * q + first_tile)
                        done, s = chunk(columns(w_in, lambda i, q=q: j(i) * 2 * WIDE + (q * WIDE + first_tile * P + SSM_INNER)),
                                        feature_major(acthi, actlo), acts)
                        seen = act.do(lambda e, i, s=s, q=q: e.activation(window[:, q, :, 2:T + 2], bank2(s), ACT.Copy),
                                      done, edges, last(f"window {q} read"))
                        def w(i, tap, f, tile=tile):
                            return params[:, bass.ds(tile(i) + (PAR["ssm_conv_w"] + tap * 32 + f), 1)]
                        for f in range(2):
                            t = act.do(lambda e, i, s=s, q=q, f=f, w=w: e.activation(
                                taps[:, q, f, :], ps[:, s, f * T:(f + 1) * T], ACT.Copy, scale=w(i, 2, f)), done,
                                last(f"taps {q} read"), params_in)
                            note(f"tap {f}", t)
                        note(f"bank {s}", t)
                        for tap in (0, 1, 3, 4):
                            for f in range(2):
                                note(f"tap {f}", dve.do(lambda e, i, q=q, f=f, tap=tap, w=w: e.scalar_tensor_tensor(
                                    out=taps[:, q, f, :], in0=window[:, q, f, tap:tap + T], scalar=w(i, tap, f),
                                    in1=taps[:, q, f, :], op0=ALU.mult, op1=ALU.add), last(f"tap {f}"), seen))
                        note(f"window {q} read", last("tap 1"))
                        for f in range(2):
                            t = act.do(lambda e, i, q=q, f=f, tile=tile: e.activation(
                                dest[:, bass.ds(tile(i) - first_tile + f, 1), :].rearrange("p a n -> p (a n)"), taps[:, q, f, :],
                                ACT.Silu, bias=params[:, bass.ds(tile(i) + (PAR["ssm_conv_b"] + f), 1)]), last(f"tap {f}"))
                        note(f"taps {q} read", t)
                    done, s = chunk(columns(w_in, lambda i: j(i) * WIDE + z_first), token_major(acthi, actlo), acts)
                    note("z", note(f"bank {s}", act.do(lambda e, i, s=s: e.activation(
                        z[:, :, bass.ds(j(i) * WIDE + z_first, WIDE)], bank2(s), ACT.Silu), done)))
                bodies(4, body)

            body_into(xs_t, 0, 0)
            body_into(bc_t, 16, 4 * WIDE)
            conv_ready = last("z")

            filled, emptied = [], {}
            for n in range(8):
                m, t0 = n // 4, 4 * (n % 4)
                for t in range(4):
                    turned = pe.do(lambda e, i, n=n, m=m, t0=t0, t=t: e.transpose(
                        ps[:, ACC + n % 4, t * P:(t + 1) * P], xs_t[:, t0 + t, m * P:(m + 1) * P], ident),
                        conv_ready, emptied.get(n - 4))
                q = act if n % 2 else dve
                copy = (lambda e, i, n=n, m=m, t0=t0: e.activation(xs[:, m, t0 * P:(t0 + 4) * P], ps[:, ACC + n % 4, :], ACT.Copy)) \
                    if n % 2 else (lambda e, i, n=n, m=m, t0=t0: e.tensor_copy(xs[:, m, t0 * P:(t0 + 4) * P], ps[:, ACC + n % 4, :]))
                emptied[n] = q.do(copy, turned)
            xs_turned = turned
            xs_ready = (emptied[6], emptied[7])

            part = lambda ap, m, d: ap[:, 64 * m + 32 * d:64 * m + 32 * d + 32]
            sums = ((le, 1, 0), (gt, 0, 0), (ge, 0, 1), (lt, 1, 1))

            def border(e, i):
                for n, (mask, m, d) in enumerate(sums):
                    out = e.matmul(ps[:, TOP, 32 * n:32 * n + 32], mask, part(a, m, d), start=True, stop=True)
                return out
            summed = pe.do(border, a_ready, table_in)
            edged = act.do(lambda e, i: e.activation(edge, ps[:, TOP, 0:128], ACT.Exp), summed)
            out_f = dve.do(lambda e, i: e.tensor_tensor(edge[:, 32:64], edge[:, 32:64], part(dt, 0, 0), ALU.mult), edged)
            out_b = dve.do(lambda e, i: e.tensor_tensor(edge[:, 96:128], edge[:, 96:128], part(dt, 1, 1), ALU.mult), edged)

            gram, gram_masked, summed_to, exped, made, multiplied_, crossed, summed_y = ({} for _ in range(8))
            summed_over, xd, sk = {}, {}, {}
            totals = scratch(16)

            def make_gram(g):
                def mm(e, i):
                    for m in range(MT):
                        out = e.matmul(ps[:, TOP, m * T:(m + 1) * T], bc_t[:, g, m * P:(m + 1) * P], bc_t[:, 8 + g, :],
                                       start=True, stop=True)
                    return out
                gram[g] = pe.do(mm, conv_ready, edged if g == 0 else gram_masked[g - 1])
                diag = spread(ps[:, TOP, :], [T + P, 2], [1, P])
                par = g % 2
                free = (made.get((g - 2, 1)), crossed.get((g - 2, 1)))
                dve.do(lambda e, i: e.tensor_tensor(gram_f[:, par, :, :], diag, spread(le, [0, 2], [1, P]), ALU.mult),
                       gram[g], *free)
                dve.do(lambda e, i: e.tensor_tensor(gram_b[:, par, :, :], diag, spread(ge, [0, 2], [1, P]), ALU.mult))
                gram_masked[g] = dve.do(lambda e, i: e.tensor_copy(
                    gram_x[:, par, :, :].rearrange("p a n -> p (a n)"), ps[:, TOP, P:3 * P]))

            items = [(g, m) for g in range(SSM_GROUPS) for m in range(MT)]

            def head_cols(ap, m, d, g):
                return part(ap, m, d)[:, 4 * g:4 * g + 4]

            def prepare(n):
                if n >= len(items):
                    return
                g, m = items[n]
                par = n % 2
                for mask, d in ((le, 0), (ge, 1)):
                    for k, part_of_a in enumerate((a_hi, a_lo)):
                        summed_over[n] = pool.do(lambda e, i, mask=mask, d=d, k=k, v=part_of_a: e.tensor_tensor(
                            cum[d][k][:, par, :, :], spread(mask, [0, 4], [1, P]), spread(head_cols(v, m, d, g), [1, 4], [0, P]),
                            ALU.mult), a_split, summed_to.get(n - 2), conv_ready)
                src, c = (0, 32) if m == 1 else (1, 96)
                x4 = lambda m: spread(xs[:, m, 4 * HD * g:], [HD, 4], [1, HD])
                xd[n] = pool.do(lambda e, i: e.tensor_tensor(
                    xdec[:, par, :, :], x4(src), spread(edge[:, c + 4 * g:], [1, 4], [0, HD]), ALU.mult),
                    out_f, out_b, *xs_ready, crossed.get((items[n - 2]) if n >= 2 else None))
                sk[n] = pool.do(lambda e, i: e.tensor_tensor(
                    skipped[:, par, :, :], x4(m), spread(rows[:, ROW["skip"] + 4 * g:], [1, 4], [0, HD]), ALU.mult),
                    rows_in, summed_y.get(n - 2))

            def decays(n):
                if n >= len(items):
                    return
                g, m = items[n]
                par = n % 2

                def mm(e, i):
                    for d in range(2):
                        for k in range(2):
                            out = e.matmul(ps[:, par, :], strict[:, d, :], cum[d][k][:, par, :, :].rearrange("p u n -> p (u n)"),
                                           start=d == k == 0, stop=d == k == 1)
                    return out
                summed_to[n] = pe.do(mm, summed_over[n], exped.get(n - 2), strict_ready)
                exped[n] = act.do(lambda e, i: e.activation(decay[:, par, :, :].rearrange("p u n -> p (u n)"), ps[:, par, :],
                                                            ACT.Exp), summed_to[n], made.get((items[n - 2]) if n >= 2 else None))

            def weights(n):
                g, m = items[n]
                par, gp = n % 2, g % 2
                for u in range(4):
                    t = act.do(lambda e, i, u=u: e.activation(weight[:, par, u, :], gram_f[:, gp, m, :], ACT.Copy,
                                                              scale=head_cols(dt, m, 0, g)[:, u:u + 1]),
                               gram_masked[g], dt_ready, multiplied_.get(n - 2))
                for u in range(4):
                    t2 = dve.do(lambda e, i, u=u: e.scalar_tensor_tensor(
                        out=weight[:, par, u, :], in0=gram_b[:, gp, m, :], scalar=head_cols(dt, m, 1, g)[:, u:u + 1],
                        in1=weight[:, par, u, :], op0=ALU.mult, op1=ALU.add), t)
                made[g, m] = dve.do(lambda e, i: e.tensor_tensor(weight[:, par, :, :], weight[:, par, :, :], decay[:, par, :, :],
                                                                 ALU.mult), t2, exped[n])

            def outputs(n):
                g, m = items[n]
                par = n % 2

                def inner(e, i):
                    for u in range(4):
                        out = e.matmul(ps[:, 4 + par, u * HD:(u + 1) * HD], weight[:, par, u, :],
                                       xs[:, m, (4 * g + u) * HD:(4 * g + u + 1) * HD], start=True, stop=True)
                    return out

                def cross(e, i):
                    return e.matmul(ps[:, 6 + par, 0:4 * HD], gram_x[:, g % 2, 1 - m, :],
                                    xdec[:, par, :, :].rearrange("p u n -> p (u n)"), start=True, stop=True)
                crossed[g, m] = pe.do(cross, xd[n], gram_masked[g], summed_y.get(n - 2))
                multiplied_[n] = pe.do(inner, made[g, m], *xs_ready, summed_y.get(n - 2))
                c = 0 if m == 1 else 64
                yv = spread(y[:, m, 4 * HD * g:], [HD, 4], [1, HD])
                four = lambda ap: spread(ap, [HD, 4], [1, HD])
                t = dve.do(lambda e, i: e.tensor_tensor(carried[:, par, :, :], four(ps[:, 6 + par, :]),
                                                        spread(edge[:, c + 4 * g:], [1, 4], [0, HD]), ALU.mult),
                           crossed[g, m], edged, squared.get(n - 2))
                t = dve.do(lambda e, i: e.tensor_tensor(carried[:, par, :, :], carried[:, par, :, :], skipped[:, par, :, :],
                                                        ALU.add), t, sk[n])
                summed_y[n] = dve.do(lambda e, i: e.tensor_tensor(carried[:, par, :, :], four(ps[:, 4 + par, :]),
                                                                  carried[:, par, :, :], ALU.add), t, multiplied_[n])
                t = dve.do(lambda e, i: e.tensor_tensor(yv, carried[:, par, :, :], four(z[:, m, 4 * HD * g:]), ALU.mult),
                           summed_y[n], xs_turned, conv_ready)
                squared[n] = act.do(lambda e, i: e.activation(carried[:, par, :, :].rearrange("p u n -> p (u n)"),
                                                              y[:, m, 4 * HD * g:4 * HD * (g + 1)], ACT.Square,
                                                              accum_out=totals[:, 8 * m + g:8 * m + g + 1]), t)
            squared = {}
            prepare(0)
            prepare(1)
            decays(0)
            for n, (g, m) in enumerate(items):
                if m == 0:
                    make_gram(g)
                decays(n + 1)
                weights(n)
                outputs(n)
                prepare(n + 2)
            r, r_ready = rsqrt(squared[15], totals, 4 * HD, 16, 1e-5)
            scaled = [dve.do(lambda e, i, m=m: e.tensor_tensor(
                spread(y[:, m, :], [4 * HD, 8], [1, 4 * HD]), spread(y[:, m, :], [4 * HD, 8], [1, 4 * HD]),
                spread(r[:, 8 * m:], [1, 8], [0, 4 * HD]), ALU.mult), r_ready) for m in range(MT)]
            low = {}
            for k in range(16):
                b = (0, 1, 2, 4, 5, 6, 7)[k % 7]
                for m in range(MT):
                    turned = pe.do(lambda e, i, b=b, m=m, k=k: e.transpose(
                        ps[:, b, m * P:(m + 1) * P], y[:, m, k * P:(k + 1) * P], ident), scaled[1], low.get(k - 7))
                g_ = params[:, PAR["ssm_norm"] + k:PAR["ssm_norm"] + k + 1]
                hi = act.do(lambda e, i, b=b, k=k, g_=g_: e.activation(mixhi[:, k, :], ps[:, b, 0:T], ACT.Copy, scale=g_), turned)
                low[k] = dve.do(lambda e, i, b=b, k=k, g_=g_: e.scalar_tensor_tensor(
                    out=mixlo[:, k, :], in0=ps[:, b, 0:T], scalar=g_, in1=f32(mixhi[:, k, :]), op0=ALU.mult,
                    op1=ALU.subtract), hi)
            w_out = A["ssm_w_out_2"][0]
            marks = {}
            for n in range(4):
                b = ACC + 2 * (n % 2)
                for half in range(2):
                    def src(i, slot, n=n, half=half):
                        a_ = slot[:, :].rearrange("p (k n) -> p k n", k=KT)
                        b_ = w_out.rearrange("(k p) n -> p k n", p=P)[:, 8 * half:8 * half + 8, n * WIDE:(n + 1) * WIDE]
                        return [(a_[:, 0:4, :], b_[:, 0:4, :]), (a_[:, 4:8, :], b_[:, 4:8, :])]

                    def mm(e, i, s, hi, lo, b=b, half=half):
                        wh, wl = (w[:, :].rearrange("p (k n) -> p k n", k=KT) for w in (hi, lo))
                        for m in range(MT):
                            for k in range(KT):
                                xh, xl = (v[:, 8 * half + k, m * P:(m + 1) * P] for v in (mixhi, mixlo))
                                for q, (p_, w_) in enumerate(((xh, wh), (xh, wl), (xl, wh))):
                                    out = e.matmul(ps[:, b + m, 0:WIDE], p_, w_[:, k, :], start=half == k == q == 0,
                                                   stop=half == 1 and k == KT - 1 and q == 2, skip_group_check=True)
                        return out
                    done, _ = chunk(src, mm, low[15], marks.get(n - 2))
                marks[n] = add_alpha(done, ps[:, b:b + 2, 0:WIDE], slice(None), slice(n * WIDE, (n + 1) * WIDE))
            return [marks[3], marks[3]]

        def network():
            acts = rms_norm(x_in, PAR["norm_mixer0"])
            load_later_constants(acts)
            mixed = conv_layer(acts)
            yield project(A["conv_w_out"][0], mixhi, mixlo, mixed, add_plain)
            acts = rms_norm(latest_x[0], PAR["norm_ffn0"])
            yield swiglu(0)(acts)
            acts = rms_norm(latest_x[0], PAR["norm_mixer1"])
            mixed = swa_layer(acts)
            yield project(A["attn_w_o"][0], mixhi, mixlo, mixed, add_plain)
            acts = rms_norm(latest_x[0], PAR["norm_ffn1"])
            landed = load_rpb(mixed)
            yield swiglu(1)(acts)
            for m in range(MT):
                flip_rpb(m, landed)
            acts = to_features(latest_x[0], rows_=x)
            mixed = na_layer(acts)
            added = project(A["attn_w_out_2"][0], mixhi, mixlo, mixed, add_alpha)
            yield layer_norm(added, A["ln1_g_2"][0], A["ln1_b_2"][0])
            acts = to_features(latest_x[0], rows_=x)
            added = squared_relu(0)(acts)
            yield layer_norm(added, A["ln2_g_2"][0], A["ln2_b_2"][0])
            acts = to_features(latest_x[0], rows_=x)
            added = ssm_layer(acts)
            yield layer_norm(added, A["ln1_g_2"][1], A["ln1_b_2"][1])
            acts = to_features(latest_x[0], rows_=x)
            added = squared_relu(1)(acts)
            yield layer_norm(added, A["ln2_g_2"][1], A["ln2_b_2"][1])

        latest_x = [None]
        for n, ready in enumerate(network()):
            latest_x[0] = ready
            if n == stop_after:
                break
        out_landed = sem("out_landed")
        sp.add(lambda e, i: e.dma_start(A["out"].rearrange("b (m p) d -> p (b m) d", p=P), x[:, :, :]), tuple(ready),
               (out_landed, 16))

        block = ctx.enter_context(nc.Block())

        @block.sync
        def _(eng):
            sp.emit(eng)
            for landed in (*consts, out_landed):
                eng.wait_ge(landed, 16)

        @block.scalar
        def _(eng):
            act.emit(eng)

        @block.vector
        def _(eng):
            dve.emit(eng)

        @block.tensor
        def _(eng):
            pe.emit(eng)

        @block.gpsimd
        def _(eng):
            pool.emit(eng)


def spans(sizes):
    out, n = {}, 0
    for name, size in sizes:
        out[name] = n
        n += size
    return out, n


TAB, TAB_N = spans([("ident", P), ("le", P), ("ge", P), ("gt", P), ("lt", P), ("flip", P), ("dist", 2 * T), ("window", 2 * T),
                    ("near", 2 * T), ("cos", 2 * HD), ("sin", 2 * HD)])
PAR, PAR_N = spans([("norm_mixer0", KT), ("norm_ffn0", KT), ("norm_mixer1", KT), ("norm_ffn1", KT),
                    ("conv_w", 3 * KT), ("q_gain", 1), ("k_gain", 1), ("ssm_conv_w", SSM_TAPS * 32),
                    ("ssm_conv_b", 32), ("ssm_norm", 16)])
ROW, ROW_N = spans([("sinks1", 16), ("sinks2", 8), ("dt_bias", 64), ("a_log", 64), ("skip", 32)])

TOTAL_CHUNKS = 202
STOPS = [16, 49, 59, 92, 105, 137, 170, 202]


def shape_tables():
    t = np.arange(T)
    a, b = np.arange(P)[:, None], np.arange(P)[None, :]
    out = np.zeros((P, TAB_N), np.float32)

    def put(name, v):
        out[:, TAB[name]:TAB[name] + v.shape[1]] = v

    put("ident", a == b)
    put("le", a <= b)
    put("ge", a >= b)
    put("gt", a > b)
    put("lt", a < b)
    put("flip", a == b // 64 * 64 + 63 - b % 64)
    far = np.float32(1e30)
    rows = lambda v: v.reshape(MT, P, -1).transpose(1, 0, 2).reshape(P, -1)
    dist = (t[:, None] - t[None, :]).astype(np.float32)
    put("dist", rows(np.where((dist >= 0) & (dist < 128), dist, far)))
    put("window", rows(np.where(np.abs(dist) <= 128, np.float32(0), -far)))
    c = t % 64
    start = np.clip(c - 8, 0, 48)
    near = (c[None, :] >= start[:, None]) & (c[None, :] < start[:, None] + 16)
    put("near", rows(np.where(near, np.float32(0), -far)))
    half = HD // 2
    inv = np.float32(10000.0) ** (-np.arange(half, dtype=np.float32) / np.float32(half))
    ang = t.astype(np.float32)[:, None] * inv[None, :].astype(np.float32)
    cos, sin = np.cos(ang).astype(np.float32), np.sin(ang).astype(np.float32)
    put("cos", rows(np.concatenate([cos, cos], 1)))
    put("sin", rows(np.concatenate([-sin, sin], 1)))
    return out


_WEIGHTS = ["x", "conv_w_in", "conv_w_out", "attn_w_qkv", "attn_w_o", "ffn_w_gate_up", "ffn_w_down", "attn_w_in_2",
            "attn_w_out_2", "ssm_w_in_2", "ssm_w_out_2", "mlp_w1_2", "mlp_w2_2", "ln1_g_2", "ln1_b_2", "ln2_g_2",
            "ln2_b_2"]


def kernel(**inputs):
    import concourse.bacc as bacc
    from concourse.bass_utils import run_bass_kernel_spmd

    get = {k: np.asarray(v) for k, v in inputs.items()}

    def by_feature(v):
        return v.reshape(-1, P).T

    arrays = {name: np.ascontiguousarray(get[name]) for name in _WEIGHTS}
    arrays["table"] = shape_tables()
    arrays["params"] = np.ascontiguousarray(np.concatenate([
        by_feature(get["norm_mixer"][0]), by_feature(get["norm_ffn"][0]), by_feature(get["norm_mixer"][1]),
        by_feature(get["norm_ffn"][1]), by_feature(get["conv_w"][0]), by_feature(np.tile(get["attn_q_gain"][0], 2)),
        by_feature(np.tile(get["attn_k_gain"][0], 2)), by_feature(get["ssm_conv_w_2"][0]),
        by_feature(get["ssm_conv_b_2"][0]), by_feature(get["ssm_norm_w_2"][0])], 1))
    arrays["rows"] = np.concatenate([get["attn_sinks"][0], get["attn_sink_2"][0], get["ssm_dt_bias_2"][0],
                                     get["ssm_A_log_2"][0].reshape(-1), get["ssm_D_2"][0]])[None, :]
    rpb = get["attn_rpb_2"][0]
    arrays["rpb"] = np.pad(rpb, ((0, 0), (0, 0), (48, 48)))

    nc = bacc.Bacc("TRN2", target_bir_lowering=False, num_devices=1)
    A = {name: nc.dram_tensor(f"in_{name}", a.shape, mybir.dt.from_np(a.dtype), kind="ExternalInput").ap()
         for name, a in arrays.items()}
    A["out"] = nc.dram_tensor("out", get["x"].shape, F32, kind="ExternalOutput").ap()
    build(nc, A, STOP)
    r = run_bass_kernel_spmd(nc, [{f"in_{n}": a for n, a in arrays.items()}], core_ids=[0])
    return r.results[0]["out"]


STOP = None
```

```python
import math
from contextlib import ExitStack

import numpy as np

import concourse.bass as bass
from concourse import mybir

F32 = mybir.dt.float32
F32R = mybir.dt.float32r
ALU = mybir.AluOpType
ACT = mybir.ActivationFunctionType
AX = mybir.AxisListType.X

P = 128
T = 256
MT = T // P
D = 1024
KT = D // P
SLOTS = 3
CHUNK = 2048
WIDE = CHUNK // KT
LEAD = 2
EPS = 1e-6
LN_EPS = 1e-5
HD = 64
D_FF = 2816
D_FF2 = 4096
QKV1 = 1536
QKV2 = 2304
ALPHA = 4 ** 0.25
SSM_IN = 6208
SSM_INNER = 2048
SSM_HEADS = 32
SSM_GROUPS = 8
SSM_TAPS = 5
TOP = 3
ACC = 4


class Loop:

    def __init__(self, trips):
        self.trips = trips


class Mark:

    def __init__(self, sem, base, stride=0, loop=None):
        self.sem, self.base, self.stride, self.loop = sem, base, stride, loop

    def back(self, trips=1):
        return Mark(self.sem, self.base - trips * self.stride, self.stride, self.loop)


class Later:

    def __init__(self):
        self.mark = None


class Queue:

    def __init__(self, sem):
        self.sem, self.count, self.ops, self.open, self.inner = sem, 0, [], None, []

    def add(self, fn, waits, inc):
        (self.ops if self.open is None else self.inner).append((fn, waits, inc))

    def do(self, fn, *waits):
        self.count += 1
        m = Mark(self.sem, self.count, 0, self.open)
        self.add(fn, waits, (self.sem, 1))
        if self.open is not None:
            self.inner_marks.append(m)
        return m

    def enter(self, loop):
        self.open, self.inner, self.inner_marks, self.at_entry = loop, [], [], self.count

    def leave(self):
        per_trip = self.count - self.at_entry
        for m in self.inner_marks:
            m.stride = per_trip
        self.count += per_trip * (self.open.trips - 1)
        if self.inner:
            self.ops.append((self.open, self.inner))
        self.open = None

    def emit(self, eng):
        known = {}

        def run(ops, loop, i):
            moving = {}
            for fn, waits, inc in ops:
                for w in waits:
                    if isinstance(w, Later):
                        w = w.mark
                    if w is None:
                        continue
                    key = id(w.sem)
                    if loop is not None and w.loop is loop and w.stride:
                        if moving.get(key, -1) >= w.base:
                            continue
                        moving[key] = w.base
                        assert w.base > 0
                        eng.wait_ge(w.sem, i * w.stride + w.base)
                    else:
                        value = w.base + (w.stride * (w.loop.trips - 1) if w.loop else 0)
                        if value <= 0 or known.get(key, 0) >= value:
                            continue
                        known[key] = value
                        eng.wait_ge(w.sem, value)
                ins = fn(eng, i)
                if inc is not None:
                    ins.then_inc(*inc)

        for op in self.ops:
            if isinstance(op[0], Loop):
                with eng.Fori(0, op[0].trips) as i:
                    run(op[1], op[0], i)
            else:
                run([op], None, 0)


def build(nc, A, stop_after=None):
    ctx = ExitStack()
    with ctx:
        sem = lambda name: ctx.enter_context(nc.semaphore(name))
        sp, act, dve, pe, pool = (Queue(sem(f"{n}_done")) for n in ("sp", "act", "dve", "pe", "pool"))
        queues = (sp, act, dve, pe, pool)
        raw_landed = [sem(f"raw_landed{s}") for s in range(SLOTS)]
        rounded = sem("chunks_rounded")
        split = sem("chunks_split")
        multiplied = sem("chunks_multiplied")

        at = [(nc.sbuf_base + 31) // 32 * 32]

        def place(name, shape, dtype=F32, offset=None):
            if offset is None:
                offset = at[0]
                at[0] += (int(np.prod(shape[1:])) * 4 + 31) // 32 * 32
            t = nc.alloc_sbuf_tensor_at(name, shape, dtype, offset=offset)
            return t, offset

        raw = [place(f"raw{s}", [P, CHUNK])[0] for s in range(SLOTS)]
        whi = [place(f"whi{s}", [P, CHUNK], F32R)[0] for s in range(SLOTS)]
        wlo = [place(f"wlo{s}", [P, CHUNK], F32R)[0] for s in range(SLOTS)]
        x, _ = place("x", [P, MT, D])
        h, h_at = place("h", [P, MT, D])
        acthi, act_at = place("acthi", [P, KT, T], F32R)
        actlo, _ = place("actlo", [P, KT, T], F32R)
        mixhi, mixhi_at = place("mixhi", [P, 2 * KT, T], F32R)
        mixlo, mixlo_at = place("mixlo", [P, 2 * KT, T], F32R)
        hidhi, hid_at = place("hidhi", [P, 3, 2, T], F32R)
        hidlo, _ = place("hidlo", [P, 3, 2, T], F32R)
        table, _ = place("table", [P, A["table"].shape[1]])
        params, _ = place("params", [P, A["params"].shape[1]])
        rows, _ = place("rows", [P, A["rows"].shape[1]])
        small, _ = place("small", [P, 896])
        lnrow, lnrow_at = place("lnrow", [P, 2, D])
        zero, zero_at = place("zero", [P, 256], F32R)
        strict, _ = place("strict", [P, 2, P], F32R)
        shared = at[0]
        ps = ctx.enter_context(nc.psum_tensor("ps", [P, 8, 512], F32))

        def bank2(b):
            return ps[:, b, :].rearrange("p (a n) -> p a n", a=2)

        def f32(ap):
            return ap.bitcast(F32)

        latest = {}
        noted, wanted = set(), {}

        def note(name, mark):
            latest[name] = mark
            noted.add(name)
            return mark

        def last(name):
            if chunk_no["loop"] is None or name in noted:
                return latest.get(name)
            return wanted.setdefault(name, Later())

        def loop_begin(trips):
            loop = Loop(trips)
            noted.clear()
            wanted.clear()
            for q in queues:
                q.enter(loop)
            chunk_no["loop"], chunk_no["entry"] = loop, chunk_no["n"]

        def loop_end():
            loop = chunk_no["loop"]
            per_trip = chunk_no["n"] - chunk_no["entry"]
            assert per_trip % SLOTS == 0
            for m, per_chunks in chunk_no["marks"]:
                m.stride = m.stride * per_trip // per_chunks
            chunk_no["marks"].clear()
            chunk_no["n"] += per_trip * (loop.trips - 1)
            chunk_no["loop"] = None
            for q in queues:
                q.leave()
            for name, later in wanted.items():
                m = latest.get(name)
                later.mark = m.back() if name in noted else m

        def bodies(n, body, peel_last=False):
            body(lambda i: 0)
            trips = n - 1 - peel_last
            if trips > 1:
                loop_begin(trips)
                body(lambda i: i + 1)
                loop_end()
            elif trips == 1:
                body(lambda i: 1)
            if peel_last and n > 1:
                body(lambda i: n - 1)

        consts = [sem(f"const_landed{n}") for n in range(6)]
        const_marks = [Mark(s, 16) for s in consts]
        for m in range(MT):
            sp.add(lambda e, i, m=m: e.dma_start(x[:, m, :], A["x"][0, m * P:(m + 1) * P, :]), (), (consts[m], 16))
        act.add(lambda e, i: e.dma_start(table[:, 0:P], A["table"][:, 0:P]), (), (consts[2], 16))
        act.add(lambda e, i: e.dma_start(params[:, :], A["params"]), (), (consts[3], 16))

        def load_later_constants(ready):
            act.add(lambda e, i: e.dma_start(table[:, P:], A["table"][:, P:]), (ready,), (consts[4], 16))
            act.add(lambda e, i: e.dma_start(rows[:, :], A["rows"].to_broadcast([P, A["rows"].shape[1]])), (), (consts[5], 16))
        *x_in, ident_in, params_in, table_in, rows_in = const_marks
        zeroed = pool.do(lambda e, i: e.memset(f32(zero[:, :]), 0.0))
        minus_half = small[:, 0:64]
        halved = pool.do(lambda e, i: e.memset(minus_half, -0.5))

        chunk_no = {"n": 0, "loop": None, "entry": 0, "marks": [], "total": TOTAL_CHUNKS if stop_after is None else STOPS[stop_after]}

        def chunk_mark(sem_, base, grows=1, per_chunks=1):
            loop = chunk_no["loop"]
            m = Mark(sem_, base, grows if loop else 0, loop)
            if loop is not None:
                chunk_no["marks"].append((m, per_chunks))
            return m

        def split_chunk(c):
            if chunk_no["loop"] is None and c >= chunk_no["total"]:
                return
            s = c % SLOTS
            landed = chunk_mark(raw_landed[s], 32 * (c // SLOTS + 1), 32, SLOTS)
            free = chunk_mark(multiplied, c - SLOTS + 1) if c >= SLOTS else None
            done = chunk_mark(rounded, c + 1)
            act.add(lambda e, i: e.activation(whi[s][:, :], raw[s][:, :], ACT.Copy),
                    (landed, free), (rounded, 1))
            dve.add(lambda e, i: e.tensor_tensor(wlo[s][:, :], raw[s][:, :], f32(whi[s][:, :]), ALU.subtract),
                    (done,), (split, 1))

        def chunk(src, products, *waits):
            c = chunk_no["n"]
            chunk_no["n"] += 1
            s = c % SLOTS
            for half in range(2):
                sp.add(lambda e, i, half=half: e.dma_start(*src(i, raw[s])[half]),
                       (chunk_mark(split, c - SLOTS + 1) if c >= SLOTS else None,), (raw_landed[s], 16))
            split_chunk(c + LEAD)
            pe.add(lambda e, i: products(e, i, s, whi[s], wlo[s]),
                   (chunk_mark(split, c + 1), last(f"bank {s}"), *waits), (multiplied, 1))
            return chunk_mark(multiplied, c + 1), s

        for c in range(LEAD):
            split_chunk(c)

        def columns(w, first):
            def src(i, slot):
                a = slot[:, :].rearrange("p (k n) -> p k n", k=KT)
                b = w.rearrange("(k p) n -> p k n", p=P)[:, :, bass.ds(first(i), WIDE)]
                return [(a[:, 0:4, :], b[:, 0:4, :]), (a[:, 4:8, :], b[:, 4:8, :])]
            return src

        def feature_major(xhi, xlo, k0=0):
            def mm(e, i, s, hi, lo):
                whi_, wlo_ = (w[:, :].rearrange("p (k n) -> p k n", k=KT) for w in (hi, lo))
                for f in range(2):
                    out = ps[:, s, f * T:(f + 1) * T]
                    for k in range(KT):
                        cols = slice(f * P, (f + 1) * P)
                        e.matmul(out, whi_[:, k, cols], xhi[:, k0 + k, :], start=k == 0, stop=False)
                        e.matmul(out, whi_[:, k, cols], xlo[:, k0 + k, :], start=False, stop=False)
                        last = e.matmul(out, wlo_[:, k, cols], xhi[:, k0 + k, :], start=False, stop=k == KT - 1)
                return last
            return mm

        def token_major(xhi, xlo, k0=0, first=True, last_k=True, cols=slice(0, WIDE)):
            def mm(e, i, s, hi, lo, bank=None):
                bank = s if bank is None else bank
                whi_, wlo_ = (w[:, :].rearrange("p (k n) -> p k n", k=KT)[:, :, cols] for w in (hi, lo))
                n = cols.stop - cols.start
                for m in range(MT):
                    out = ps[:, bank, m * T:m * T + n]
                    for k in range(KT):
                        xh, xl = (v[:, k0 + k, m * P:(m + 1) * P] for v in (xhi, xlo))
                        e.matmul(out, xh, whi_[:, k, :], start=k == 0, stop=False)
                        e.matmul(out, xh, wlo_[:, k, :], start=False, stop=False)
                        last = e.matmul(out, xl, whi_[:, k, :], start=False, stop=k == KT - 1)
                return last
            return mm

        ident = table[:, TAB["ident"]:TAB["ident"] + P]

        def to_features(ready, gain=None, rows_=None):
            turned = []
            rows_ = h if rows_ is None else rows_
            for m in range(MT):
                for k in range(KT):
                    out = ps[:, ACC + k // 2, (k % 2) * T + m * P:(k % 2) * T + (m + 1) * P]
                    turned.append(pe.do(lambda e, i, out=out, m=m, k=k: e.transpose(
                        out, rows_[:, m, k * P:(k + 1) * P], ident), ready[m], ident_in))
            done = {}
            for k in (0, 2, 4, 6, 1, 3, 5, 7):
                src = ps[:, ACC + k // 2, (k % 2) * T:(k % 2 + 1) * T]
                g = params[:, gain + k:gain + k + 1] if gain is not None else 1.0
                hi = act.do(lambda e, i, k=k, src=src, g=g: e.activation(acthi[:, k, :], src, ACT.Copy, scale=g),
                            turned[KT + k // 2 * 2 + 1], params_in, done.get(k - 1))
                done[k] = dve.do(lambda e, i, k=k, src=src, g=g: e.scalar_tensor_tensor(
                    out=actlo[:, k, :], in0=src, scalar=g, in1=f32(acthi[:, k, :]), op0=ALU.mult, op1=ALU.subtract), hi)
            return done[7]

        small_at = [64]

        def scratch(n):
            small_at[0] += n
            return small[:, small_at[0] - n:small_at[0]]

        def spread(ap, *dims):
            return bass.AP(ap.tensor, ap.offset, [list(ap.ap[0]), *[list(d) for d in dims]])

        def rsqrt(ready, total, n, count, eps):
            mean, out = scratch(count), scratch(count)
            ms = pool.do(lambda e, i: e.tensor_scalar(mean, total, 1.0 / n, eps, ALU.mult, ALU.add), ready, halved)
            return out, pool.do(lambda e, i: e.tensor_tensor(out, mean, minus_half[:, 0:count], ALU.pow), ms)

        def rms_norm(ready, gain):
            scaled = []
            for m in range(MT):
                total = scratch(1)
                sq = act.do(lambda e, i, m=m, total=total: e.activation(h[:, m, :], x[:, m, :], ACT.Square,
                                                                        accum_out=total), ready[m])
                rms, r = rsqrt(sq, total, D, 1, EPS)
                scaled.append(dve.do(lambda e, i, m=m, rms=rms: e.tensor_scalar(
                    h[:, m, :], x[:, m, :], rms, None, ALU.mult), r))
            return to_features(scaled, gain)

        def conv_layer(acts):
            b_sb, off = place("conv_b", [P, 2, T], offset=shared)
            u, _ = place("conv_u", [P, 2, T + 2], offset=shared + 2048)
            y, _ = place("conv_y", [P, 2, T], offset=shared + 2048 + 2112)
            cleared = pool.do(lambda e, i: e.memset(u[:, :, :], 0.0))
            w_in = A["conv_w_in"][0]

            def body(j):
                done, s = chunk(columns(w_in, lambda i: j(i) * WIDE), feature_major(acthi, actlo), acts)
                b_copied = note(f"bank {s}", act.do(lambda e, i, s=s: e.activation(b_sb[:, :, :], bank2(s), ACT.Copy),
                                                    done, last("b read")))
                done, s = chunk(columns(w_in, lambda i: j(i) * WIDE + 2 * D), feature_major(acthi, actlo))
                tap = note("b read", note(f"bank {s}", dve.do(lambda e, i, s=s: e.tensor_tensor(
                    u[:, :, 2:T + 2], bank2(s), b_sb[:, :, :], ALU.mult), done, b_copied, cleared)))
                for n in range(3):
                    for f in range(2):
                        def one(e, i, f=f, n=n):
                            w = params[:, bass.ds(j(i) * 2 + (PAR["conv_w"] + (2 - n) * KT + f), 1)]
                            src = u[:, f, 2 - n:2 - n + T]
                            if n == 0:
                                return e.tensor_scalar(y[:, f, :], src, w, None, ALU.mult)
                            return e.scalar_tensor_tensor(out=y[:, f, :], in0=src, scalar=w, in1=y[:, f, :],
                                                          op0=ALU.mult, op1=ALU.add)
                        note(f"tap {f}", dve.do(one, tap if n == 0 else last(f"tap {f}"), last("y read"), params_in))
                done, s = chunk(columns(w_in, lambda i: j(i) * WIDE + D), feature_major(acthi, actlo))
                gated = note(f"bank {s}", dve.do(lambda e, i, s=s: e.tensor_tensor(
                    y[:, :, :], bank2(s), y[:, :, :], ALU.mult), done, last("tap 0"), last("tap 1")))
                note("y read", split_mix(gated, lambda i: j(i) * 2, 2, y[:, :, :]))

            bodies(4, body)
            return last("y read")

        def split_mix(ready, first, n, src):
            hi = act.do(lambda e, i: e.activation(mixhi[:, bass.ds(first(i), n), :], src, ACT.Copy), ready)
            return dve.do(lambda e, i: e.tensor_tensor(mixlo[:, bass.ds(first(i), n), :], src,
                                                       f32(mixhi[:, bass.ds(first(i), n), :]), ALU.subtract), hi)

        def project(w, xhi, xlo, ready, add):
            for n in range(D // WIDE):
                done, s = chunk(columns(w, lambda i, n=n: n * WIDE), token_major(xhi, xlo), ready)
                m = note(f"bank {s}", add(done, bank2(s), slice(None), slice(n * WIDE, (n + 1) * WIDE)))
            return [m, m]

        def add_plain(done, src, tokens, cols):
            return dve.do(lambda e, i: e.tensor_tensor(x[:, tokens, cols], src, x[:, tokens, cols], ALU.add), done)

        def add_alpha(done, src, tokens, cols):
            return dve.do(lambda e, i: e.scalar_tensor_tensor(out=x[:, tokens, cols], in0=x[:, tokens, cols], scalar=ALPHA,
                                                              in1=src, op0=ALU.mult, op1=ALU.add), done)

        gate_sb, _ = place("gate_sb", [P, 2, T], offset=shared)
        prod_sb, _ = place("prod_sb", [P, 2, 2 * T], offset=shared + 2048)

        def feed_forward(acts, up_src, n_up, down, pairs, slots, hidden, add):

            def down_products(hs, final=False):
                def mm(e, i, s, hi, lo):
                    wh, wl = (w[:, :].rearrange("p (k n) -> p k n", k=2) for w in (hi, lo))
                    for k in range(2):
                        for m in range(MT):
                            xh, xl = (v[:, hs, k, m * P:(m + 1) * P] for v in (hidhi, hidlo))
                            for a, b in ((xh, wh), (xh, wl), (xl, wh)):
                                for n in range(2):
                                    mm_ = e.matmul(ps[:, ACC + 2 * m + n, :], a, b[:, k, n * 512:(n + 1) * 512],
                                                   start=False, stop=final and k == 1 and a is xl,
                                                   skip_group_check=True)
                    return mm_
                return mm

            def down_src(t):
                def src(i, slot):
                    a = slot[:, :].rearrange("p (k n) -> p k n", k=2)
                    return [(a[:, k, :], down[bass.ds(t(i) * 2 * P + k * P, P), :]) for k in range(2)]
                return src

            def up(t, hs):
                for q in range(n_up):
                    done, s = chunk(up_src(t, q), feature_major(acthi, actlo), acts)
                    hidden(done, s, hs, q)

            def open_accumulators(e, i):
                for b in range(4):
                    for half in range(2):
                        mm = e.matmul(ps[:, ACC + b, half * T:(half + 1) * T], zero[:, 0:P], zero[:, :],
                                      start=half == 0, stop=False, skip_group_check=True)
                return mm

            peel_last = chunk_no["n"] + pairs * (n_up + 1) == chunk_no["total"]
            pe.do(open_accumulators, zeroed, acts)
            up(lambda i: 0, 0)
            assert (pairs - 1) % slots == 0

            def body(j):
                for u in range(slots):
                    before = last("hidden")
                    up(lambda i, u=u: j(i) * slots + (u + 1), (u + 1) % slots)
                    chunk(down_src(lambda i, u=u: j(i) * slots + u), down_products(u), before)

            bodies((pairs - 1) // slots, body, peel_last)
            done, _ = chunk(down_src(lambda i: pairs - 1), down_products((pairs - 1) % slots, True), last("hidden"))
            return [add(done, ps[:, ACC + 2 * m:ACC + 2 * m + 2, :].rearrange("p a n -> p (a n)"), m, slice(0, D))
                    for m in range(MT)]

        def swiglu(layer):
            w = A["ffn_w_gate_up"][layer]

            def up_src(t, q):
                def src(i, slot):
                    a = slot[:, :].rearrange("p (k g n) -> p g k n", k=KT, g=2)
                    return [(a[:, g, :, :], w.rearrange("(k p) n -> p k n", p=P)[
                        :, :, bass.ds(t(i) * 2 * P + (q * P + g * D_FF), P)]) for g in range(2)]
                return src

            def hidden(done, s, hs, q):
                silu = act.do(lambda e, i: e.activation(gate_sb[:, q, :], ps[:, s, 0:T], ACT.Silu),
                              done, last(f"gate {q} read"))
                prod = dve.do(lambda e, i: e.tensor_tensor(prod_sb[:, q, 0:T], ps[:, s, T:2 * T], gate_sb[:, q, :],
                                                           ALU.mult), silu, last(f"prod {q} read"))
                note(f"bank {s}", prod)
                note(f"gate {q} read", prod)
                hi = act.do(lambda e, i: e.activation(hidhi[:, hs, q, :], prod_sb[:, q, 0:T], ACT.Copy), prod)
                lo = dve.do(lambda e, i: e.tensor_tensor(hidlo[:, hs, q, :], prod_sb[:, q, 0:T],
                                                         f32(hidhi[:, hs, q, :]), ALU.subtract), hi)
                note(f"prod {q} read", lo)
                note("hidden", lo)

            def run(acts):
                return feed_forward(acts, up_src, 2, A["ffn_w_down"][layer], D_FF // (2 * P), 2, hidden, add_plain)
            return run

        def squared_relu(layer):
            w = A["mlp_w1_2"][layer]

            def up_src(t, q):
                return columns(w, lambda i: t(i) * WIDE)

            def hidden(done, s, hs, q):
                relu = act.do(lambda e, i: e.activation(gate_sb[:, :, :], bank2(s), ACT.Relu), done, last("gate read"))
                note(f"bank {s}", relu)
                prod = prod_sb[:, 0, :].rearrange("p (a n) -> p a n", a=2)
                sq = dve.do(lambda e, i: e.tensor_tensor(prod, gate_sb[:, :, :], gate_sb[:, :, :], ALU.mult),
                            relu, last("prod read"))
                note("gate read", sq)
                hi = act.do(lambda e, i: e.activation(hidhi[:, hs, :, :], prod, ACT.Copy), sq)
                lo = dve.do(lambda e, i: e.tensor_tensor(hidlo[:, hs, :, :], prod, f32(hidhi[:, hs, :, :]),
                                                         ALU.subtract), hi)
                note("prod read", lo)
                note("hidden", lo)

            def run(acts):
                return feed_forward(acts, up_src, 1, A["mlp_w2_2"][layer], D_FF2 // (2 * P), 3, hidden, add_alpha)
            return run

        def layer_norm(ready, g, b):
            out = []
            ln_sem = sem(f"ln_landed{len(ln_sems)}")
            ln_sems.append(ln_sem)
            for n, v in enumerate((g, b)):
                act.add(lambda e, i, n=n, v=v: e.dma_start(lnrow[:, n, :], v.rearrange("(a d) -> a d", a=1).to_broadcast([P, D])),
                        (latest.get("lnrow"),), (ln_sem, 16))
            landed = Mark(ln_sem, 32)
            for m in range(MT):
                stats, mv = scratch(12), scratch(2)
                for n in range(2):
                    st = dve.do(lambda e, i, m=m, n=n, stats=stats: e.bn_stats(
                        stats[:, 6 * n:6 * n + 6], x[:, m, 512 * n:512 * (n + 1)]), ready[m])
                ag = dve.do(lambda e, i, mv=mv, stats=stats: e.bn_aggr(mv, stats), st)
                rstd, r = rsqrt(ag, mv[:, 1:2], 1, 1, LN_EPS)
                a = dve.do(lambda e, i, m=m, mv=mv: e.scalar_tensor_tensor(
                    out=x[:, m, :], in0=x[:, m, :], scalar=mv[:, 0:1], in1=lnrow[:, 0, :], op0=ALU.subtract,
                    op1=ALU.mult), ag, landed)
                out.append(dve.do(lambda e, i, m=m, rstd=rstd: e.scalar_tensor_tensor(
                    out=x[:, m, :], in0=x[:, m, :], scalar=rstd, in1=lnrow[:, 1, :], op0=ALU.mult,
                    op1=ALU.add), a, r))
            latest["lnrow"] = out[-1]
            return out
        ln_sems = []

        qkv, _ = place("qkv", [P, MT, QKV2], offset=shared)
        q_t = (place("q_hi", [P, 8, T], F32R, offset=shared + 18432)[0], place("q_lo", [P, 8, T], F32R, offset=act_at)[0])
        k_t = (place("k_hi", [P, 6, T], F32R, offset=shared + 26624)[0],
               place("k_lo", [P, 6, T], F32R, offset=act_at + 8192)[0])
        bias, _ = place("bias", [P, 2, 4, T], offset=lnrow_at)
        bias_more, _ = place("bias_more", [P, 2, 4, T], offset=mixlo_at + 8192)
        probs, _ = place("probs", [P, 2, 4, T], offset=h_at)
        probs_t, _ = place("probs_t", [P, 2, 2, 4, P], offset=mixhi_at + 8192)
        SCALE = HD ** -0.5
        HEADS = (0, 2, 1, 3)

        def wide_project(w, width, acts):
            def body(j):
                for u in range(3):
                    done, s = chunk(columns(w, lambda i, u=u: j(i) * 3 * WIDE + u * WIDE),
                                    token_major(acthi, actlo), acts)
                    note("qkv", note(f"bank {s}", act.do(lambda e, i, u=u, s=s: e.activation(
                        qkv[:, :, bass.ds(j(i) * 3 * WIDE + u * WIDE, WIDE)], bank2(s), ACT.Copy), done)))
            bodies(width // (3 * WIDE), body)
            return last("qkv")

        def turn_heads(ready, sources, dest, banks, gain=None):
            marks = []
            for n in range(0, len(sources), 2):
                b = banks[n // 2]
                for f, source in enumerate(sources[n:n + 2]):
                    for m in range(MT):
                        turned = pe.do(lambda e, i, b=b, f=f, m=m, source=source: e.transpose(
                            ps[:, b, f * T + m * P:f * T + (m + 1) * P], source(m), ident), ready[m])
                k = len(sources[n:n + 2])
                g = params[:, gain:gain + 1] if gain is not None else 1.0
                hi = act.do(lambda e, i, b=b, n=n, k=k, g=g: e.activation(
                    dest[0][:, n:n + k, :], bank2(b)[:, 0:k, :], ACT.Copy, scale=g), turned)
                marks.append(dve.do(lambda e, i, b=b, n=n, k=k, g=g: e.scalar_tensor_tensor(
                    out=dest[1][:, n:n + k, :], in0=bank2(b)[:, 0:k, :], scalar=g, in1=f32(dest[0][:, n:n + k, :]),
                    op0=ALU.mult, op1=ALU.subtract), hi))
            return marks[-1]

        def attend(ready, groups):
            N = len(groups)
            rows_of = [scratch(4 * 6) for _ in range(2)]
            scored, biased, exped, normed, turned, copied, mixed, split_ = ({} for _ in range(8))

            def score(n):
                if n >= N:
                    return
                g, b0, nk = groups[n], 2 * (n % 2), groups[n]["nk"] * P

                def mm(e, i):
                    for w, u in enumerate(HEADS):
                        base = (u % 2) * HD
                        for n_, (a, b) in enumerate(((0, 0), (0, 1), (1, 0))):
                            out = e.matmul(ps[:, b0 + w // 2, (w % 2) * T:(w % 2) * T + nk],
                                           q_t[a][base:base + HD, g["q"] + u // 2, g["m"] * P:(g["m"] + 1) * P],
                                           k_t[b][base:base + HD, g["k"](u), 0:nk], start=n_ == 0, stop=n_ == 2)
                    return out
                scored[n] = pe.do(mm, ready, biased.get(n - 2))

            def weigh(n):
                if n >= N:
                    return
                g, par, nk = groups[n], n % 2, groups[n]["nk"] * P
                r = rows_of[par]
                neg, den, sunk, es = (r[:, 4 * k:4 * k + 4] for k in range(4))
                p4 = probs[:, par, :, 0:nk]
                s4 = ps[:, 2 * par:2 * par + 2, :].rearrange("p a (b n) -> p (a b) n", b=2)[:, :, 0:nk]
                biased[n] = dve.do(lambda e, i: e.scalar_tensor_tensor(out=p4, in0=s4, scalar=SCALE, in1=g["bias"],
                                                                       op0=ALU.mult, op1=ALU.add),
                                   scored[n], g["bias_ready"], turned.get(n - 2))
                top = dve.do(lambda e, i: e.tensor_reduce(neg, p4, AX, ALU.max), biased[n], exped.get(n - 2))
                if g["sink"] is None:
                    top = dve.do(lambda e, i: e.tensor_scalar(neg, neg, -1.0, None, ALU.mult), top)
                else:
                    sink, minus_sink = (spread(v, [1, 2], [2, 2]) for v in g["sink"])
                    neg4, sunk4 = (spread(v, [2, 2], [1, 2]) for v in (neg, sunk))
                    top = dve.do(lambda e, i: e.scalar_tensor_tensor(out=neg4, in0=neg4, scalar=-1.0, in1=minus_sink,
                                                                     op0=ALU.mult, op1=ALU.min), top, sinks_ready)
                    sunk_ = dve.do(lambda e, i: e.tensor_tensor(sunk4, sink, neg4, ALU.add), top)
                for u in range(4):
                    exped[n] = act.do(lambda e, i, u=u: e.activation(p4[:, u, :], p4[:, u, :], ACT.Exp,
                                                                     bias=neg[:, u:u + 1], accum_out=den[:, u:u + 1]), top,
                                      normed.get(n - 2))
                if g["sink"] is not None:
                    exped[n] = act.do(lambda e, i: e.activation(es, sunk, ACT.Exp), sunk_)

            def normalise(n):
                g, par, nk = groups[n], n % 2, groups[n]["nk"] * P
                r = rows_of[par]
                den, es, inv = r[:, 4:8], r[:, 12:16], r[:, 16:20]
                p4 = probs[:, par, :, 0:nk]
                ready_ = exped[n]
                if g["sink"] is not None:
                    ready_ = dve.do(lambda e, i: e.tensor_tensor(den, den, es, ALU.add), ready_)
                ready_ = dve.do(lambda e, i: e.reciprocal(inv, den), ready_)
                normed[n] = dve.do(lambda e, i: e.tensor_tensor(p4, p4, spread(inv, [1, 4], [0, nk]), ALU.mult), ready_)

            def turn(n):
                g, par = groups[n], n % 2

                def mm(e, i):
                    for kt in range(g["nk"]):
                        for u in range(4):
                            out = e.transpose(ps[:, 4 + kt, u * P:(u + 1) * P], probs[:, par, u, kt * P:(kt + 1) * P], ident)
                    return out
                turned[n] = pe.do(mm, normed[n], copied.get(n - 1))
                copied[n] = act.do(lambda e, i: e.activation(
                    probs_t[:, par, 0:g["nk"], :, :].rearrange("p k u n -> p k (u n)"), ps[:, 4:4 + g["nk"], :], ACT.Copy),
                    turned[n], mixed.get(n - 2))

            def mix(n):
                g, par = groups[n], n % 2

                def mm(e, i):
                    for w, u in enumerate(HEADS):
                        base = (u % 2) * HD
                        for kt in range(g["nk"]):
                            v = qkv[:, kt, g["v"](u):g["v"](u) + HD]
                            out = e.matmul(ps[base:base + HD, 6 + par, (u // 2) * P:(u // 2 + 1) * P], v,
                                           probs_t[:, par, kt, w, :], start=kt == 0, stop=kt == g["nk"] - 1)
                    return out
                mixed[n] = pe.do(mm, copied[n], split_.get(n - 2))
                src = ps[:, 6 + par, 0:2 * P].rearrange("p (a n) -> p a n", a=2)
                tiles, tokens = slice(g["out"], g["out"] + 2), slice(g["m"] * P, (g["m"] + 1) * P)
                hi[n] = act.do(lambda e, i: e.activation(mixhi[:, tiles, tokens], src, ACT.Copy), mixed[n])

            def rest(n):
                g, par = groups[n], n % 2
                src = ps[:, 6 + par, 0:2 * P].rearrange("p (a n) -> p a n", a=2)
                tiles, tokens = slice(g["out"], g["out"] + 2), slice(g["m"] * P, (g["m"] + 1) * P)
                split_[n] = dve.do(lambda e, i: e.tensor_tensor(mixlo[:, tiles, tokens], src,
                                                                f32(mixhi[:, tiles, tokens]), ALU.subtract), hi[n])
            hi = {}
            score(0)
            score(1)
            weigh(0)
            for n in range(N):
                if "bias_make" in groups[min(n + 1, N - 1)] and n + 1 < N:
                    groups[n + 1]["bias_make"](biased.get(n - 1))
                weigh(n + 1)
                normalise(n)
                score(n + 2)
                turn(n)
                if n:
                    mix(n - 1)
                if n > 1:
                    rest(n - 2)
            mix(N - 1)
            rest(N - 2)
            rest(N - 1)
            latest["lnrow"] = split_[N - 1]
            return split_[N - 1]

        minus_sinks = rows_neg = None

        def swa_layer(acts):
            sinks_ready.mark = pool.do(lambda e, i: e.tensor_scalar(negated, rows[:, 0:24], -1.0, None, ALU.mult), rows_in)
            ready = wide_project(A["attn_w_qkv"][0], QKV1, acts)
            heads = 20
            scaled, prior = [], None
            for m in range(MT):
                total = scratch(heads)
                sq_buf = spread(h[:, 0, :], [1, heads * HD])
                sq = act.do(lambda e, i, m=m: e.activation(sq_buf, qkv[:, m, 0:heads * HD], ACT.Square), ready, prior)
                prior = dve.do(lambda e, i, total=total: e.tensor_reduce(
                    total, spread(h[:, 0, :], [HD, heads], [1, HD]), AX, ALU.add), sq)
                r, r_ready = rsqrt(prior, total, HD, heads, EPS)
                dve.do(lambda e, i, m=m, r=r: e.tensor_tensor(
                    spread(qkv[:, m, :], [HD, 16], [1, HD]), spread(qkv[:, m, :], [HD, 16], [1, HD]),
                    spread(r, [1, 16], [0, HD]), ALU.mult), r_ready)
                scaled.append(dve.do(lambda e, i, m=m, r=r: e.tensor_tensor(
                    spread(qkv[:, m, QKV1:], [2 * HD, 4], [HD, 2], [1, HD]), spread(qkv[:, m, D:], [HD, 4], [0, 2], [1, HD]),
                    spread(r[:, 16:20], [1, 4], [0, 2], [0, HD]), ALU.mult), r_ready))
            q_cols = lambda p: lambda m: qkv[:, m, p * P:(p + 1) * P]
            k_cols = lambda g: lambda m: qkv[:, m, QKV1 + g * P:QKV1 + (g + 1) * P]
            turn_heads(scaled, [q_cols(p) for p in range(8)], q_t, [4, 5, 6, 7], PAR["q_gain"])
            turned = turn_heads(scaled, [k_cols(g) for g in range(4)], k_t, [0, 1], PAR["k_gain"])
            groups = []
            for m in range(MT):
                for g in range(4):
                    n = len(groups)
                    nk = m + 1
                    sink = rows[:, ROW["sinks1"] + 4 * g:ROW["sinks1"] + 4 * g + 4]
                    msink = negated[:, ROW["sinks1"] + 4 * g:ROW["sinks1"] + 4 * g + 4]

                    def make(free, n=n, m=m, g=g, nk=nk):
                        for w, u in enumerate(HEADS):
                            slope = float(np.exp2(np.float32(-8.0 * (4 * g + u + 1) / 16)))
                            groups[n]["bias_ready"] = pool.do(lambda e, i, w=w, slope=slope: e.tensor_scalar(
                                bias[:, n % 2, w, 0:nk * P], table[:, TAB["dist"] + m * T:TAB["dist"] + m * T + nk * P],
                                -slope, None, ALU.mult), table_in, free)
                    groups.append(dict(m=m, nk=nk, q=2 * g, k=lambda u, g=g: g, v=lambda u, g=g: D + 256 + g * HD,
                                       out=2 * g, sink=(sink, msink), bias=bias[:, n % 2, :, 0:nk * P], bias_make=make))
            groups[0]["bias_make"](None)
            return attend(turned, groups)

        negated = scratch(24)
        sinks_ready = Later()

        rpb_sem = sem("rpb_landed")

        def rpb_tile(m, g):
            return (bias, bias_more)[m][:, g, :, :]

        def load_rpb(free):
            rpb = A["rpb"]
            (sh, _), (sr, _), _ = rpb.ap
            for m in range(MT):
                for head in range(8):
                    for rr in range(2):
                        off = head * sh + (7 - 2 * m - rr) * sr
                        src = bass.AP(rpb.tensor, off, [[1, 64], [sr, 4], [1, 64]])
                        dst = rpb_tile(m, head // 4)[64 * rr:64 * rr + 64, HEADS.index(head % 4), :].rearrange("p (a n) -> p a n", a=4)
                        pool.add(lambda e, i, dst=dst, src=src: e.dma_start(dst, src), (free,), (rpb_sem, 16))
            return Mark(rpb_sem, 16 * 32)

        biases = {}

        def flip_rpb(m, landed):
            for g in range(2):
                tile = rpb_tile(m, g).rearrange("p u n -> p (u n)")

                def mm(e, i, g=g, tile=tile):
                    for n in range(2):
                        out = e.matmul(ps[:, 2 * g + n, :], table[:, TAB["flip"]:TAB["flip"] + P],
                                       tile[:, 512 * n:512 * n + 512], start=True, stop=True)
                    return out
                flipped = pe.do(mm, landed, biases.get((m - 1, g)))
                near = spread(table[:, TAB["near"] + m * T:], [0, 4], [1, T])
                biases[m, g] = dve.do(lambda e, i, m=m, g=g, near=near: e.tensor_tensor(
                    rpb_tile(m, g), ps[:, 2 * g:2 * g + 2, :].rearrange("p a (b n) -> p (a b) n", b=2), near, ALU.add), flipped)
            for b in range(SLOTS):
                note(f"bank {b}", biases[m, 1])

        def na_layer(acts):
            ready = wide_project(A["attn_w_in_2"][0], QKV2, acts)
            half = HD // 2
            roped, prior = [], None
            for m in range(MT):
                v = qkv[:, m, :]
                first, second = spread(v, [HD, 10], [1, half]), spread(v[:, half:], [HD, 10], [1, half])
                both = spread(v, [HD, 10], [1, HD])
                cos = spread(table[:, TAB["cos"] + m * HD:], [0, 10], [1, HD])
                minus_sin = spread(table[:, TAB["sin"] + m * HD:], [0, 10], [1, half])
                plus_sin = spread(table[:, TAB["sin"] + m * HD + half:], [0, 10], [1, half])
                rot = probs[:, m, 0:3, :].rearrange("p a n -> p (a n)")
                rot_1, rot_2, rot_all = spread(rot, [HD, 10], [1, half]), spread(rot[:, half:], [HD, 10], [1, half]), \
                    spread(rot, [HD, 10], [1, HD])
                a = dve.do(lambda e, i, o=rot_1, x_=second, s_=minus_sin: e.tensor_tensor(o, x_, s_, ALU.mult), ready, table_in)
                b = dve.do(lambda e, i, o=rot_2, x_=first, s_=plus_sin: e.tensor_tensor(o, x_, s_, ALU.mult), ready)
                c = dve.do(lambda e, i, o=both, s_=cos: e.tensor_tensor(o, o, s_, ALU.mult), a, b)
                dve.do(lambda e, i, m=m, rot=rot, v=v: e.tensor_tensor(
                    spread(probs[:, m, 3, :], [2 * HD, 2], [HD, 2], [1, HD]), spread(v[:, 512:], [HD, 2], [0, 2], [1, HD]),
                    spread(rot[:, 512:], [HD, 2], [0, 2], [1, HD]), ALU.add), c)
                roped.append(dve.do(lambda e, i, v=v, rot=rot: e.tensor_tensor(v[:, 0:512], v[:, 0:512], rot[:, 0:512],
                                                                               ALU.add), c))
            cols = lambda c0: lambda m: qkv[:, m, c0:c0 + P]
            twice = lambda g: lambda m: probs[:, m, 3, g * P:(g + 1) * P]
            turn_heads(roped, [cols(p * P) for p in range(4)] + [cols(768 + p * P) for p in range(4)], q_t, [4, 5, 6, 7])
            turned = turn_heads(roped, [twice(0), twice(1)] + [cols(1280 + p * P) for p in range(4)], k_t, [0, 1, 2])
            groups = []
            for m in range(MT):
                window = spread(table[:, TAB["window"] + m * T:], [0, 4], [1, T])
                for g in range(2):
                    c = ROW["sinks2"] + 4 * g
                    groups.append(dict(m=m, nk=2, q=2 * g, k=lambda u, g=g: g, v=lambda u, g=g: 640 + g * HD, out=2 * g,
                                       sink=(rows[:, c:c + 4], negated[:, c:c + 4]), bias=window, bias_ready=table_in))
                for g in range(2):
                    groups.append(dict(m=m, nk=2, q=4 + 2 * g, k=lambda u, g=g: 2 + 2 * g + u // 2,
                                       v=lambda u, g=g: 1792 + (4 * g + u) * HD, out=4 + 2 * g, sink=None,
                                       bias=rpb_tile(m, g), bias_ready=biases[m, g]))
            return attend(turned, groups)

        y, _ = place("ssm_y", [P, MT, SSM_INNER], offset=shared)
        z, _ = place("z", [P, 2, MT, 4 * P], offset=shared + 16384)
        ssm_small, _ = place("ssm_small", [P, 5, 128], offset=shared + 24576)
        bc_t, _ = place("bc_t", [P, 4, T], offset=mixhi_at)
        xs_t, _ = place("xs_t", [P, 2, 4, T], offset=mixhi_at + 4096)
        gram_f, _ = place("gram_f", [P, 2, MT, P], offset=mixhi_at + 12288)
        gram_b, _ = place("gram_b", [P, 2, MT, P], offset=mixhi_at + 14336)
        xs, _ = place("xs", [P, 2, MT, 4 * P], offset=mixlo_at)
        gram_x, _ = place("gram_x", [P, 2, MT, P], offset=mixlo_at + 8192)
        xdec, _ = place("xdec", [P, 2, 4, HD], offset=mixlo_at + 10240)
        skipped, _ = place("skipped", [P, 2, 4, HD], offset=mixlo_at + 12288)
        carried, _ = place("carried", [P, 2, 4, HD], offset=mixlo_at + 14336)
        taps, _ = place("ssm_taps", [P, 2, 2, T], offset=hid_at)
        window, _ = place("ssm_window", [P, 2, 2, T + 4], offset=hid_at + 4096)
        cum = [[place(f"cum_{d}{n}", [P, 4, P], F32R, offset=lnrow_at + 4096 * d + 2048 * n)[0] for n in range(2)]
               for d in range(2)]
        decay, _ = place("decay", [P, 2, 4, P], offset=h_at)
        weight, _ = place("weight", [P, 2, 4, P], offset=h_at + 4096)
        rounding, _ = place("rounding", [P, 128], F32R, offset=h_at + 4096)

        def ssm_layer(acts):
            w_in = A["ssm_w_in_2"][0]
            le, ge, gt, lt = (table[:, TAB[n]:TAB[n] + P] for n in ("le", "ge", "gt", "lt"))
            done, s = chunk(columns(w_in, lambda i: SSM_IN - WIDE), token_major(acthi, actlo, cols=slice(WIDE - 64, WIDE)), acts)
            v, (dt, a, a_hi, a_lo, edge) = h[:, 0, 512:640], (ssm_small[:, n, :] for n in range(5))
            two = lambda ap: spread(ap, [64, 2], [1, 64])
            over_m = lambda ap: spread(ap, [0, 2], [1, 64])
            m_ = note(f"bank {s}", dve.do(lambda e, i: e.tensor_tensor(
                two(v), bank2(s)[:, :, 0:64], over_m(rows[:, ROW["dt_bias"]:]), ALU.add), done, rows_in))
            e_, u_, ln_, same = (h[:, 0, 128 * n:128 * n + 128] for n in range(4))
            m_ = dve.do(lambda e, i: e.scalar_tensor_tensor(out=e_, in0=v, scalar=-1.0, in1=v, op0=ALU.mult, op1=ALU.min), m_)
            exp_ = act.do(lambda e, i: e.activation(e_, e_, ACT.Exp), m_)
            m_ = dve.do(lambda e, i: e.tensor_scalar(u_, e_, 1.0, None, ALU.add), exp_)
            log = act.do(lambda e, i: e.activation(ln_, u_, ACT.Ln), m_)
            m_ = dve.do(lambda e, i: e.tensor_scalar(same, u_, 1.0, None, ALU.is_equal), m_)
            m_ = dve.do(lambda e, i: e.scalar_tensor_tensor(out=u_, in0=u_, scalar=-1.0, in1=same, op0=ALU.add, op1=ALU.add), m_, log)
            m_ = dve.do(lambda e, i: e.reciprocal(u_, u_), m_)
            m_ = dve.do(lambda e, i: e.tensor_tensor(u_, u_, ln_, ALU.mult), m_)
            m_ = dve.do(lambda e, i: e.tensor_tensor(u_, u_, same, ALU.add), m_)
            m_ = dve.do(lambda e, i: e.tensor_tensor(u_, u_, e_, ALU.mult), m_)
            dt_ready = dve.do(lambda e, i: e.scalar_tensor_tensor(out=dt, in0=v, scalar=0.0, in1=u_, op0=ALU.max, op1=ALU.add), m_)
            rate = scratch(64)
            rated = act.do(lambda e, i: e.activation(rate, rows[:, ROW["a_log"]:ROW["a_log"] + 64], ACT.Exp), rows_in)
            a_ready = dve.do(lambda e, i: e.scalar_tensor_tensor(out=two(a), in0=two(dt), scalar=-1.0, in1=over_m(rate),
                                                                 op0=ALU.mult, op1=ALU.mult), dt_ready, rated)

            act.do(lambda e, i: e.activation(strict[:, 0, :], gt, ACT.Copy), table_in)
            strict_ready = act.do(lambda e, i: e.activation(strict[:, 1, :], lt, ACT.Copy))
            hi = act.do(lambda e, i: e.activation(rounding[:, :], a, ACT.Copy), a_ready)
            dve.do(lambda e, i: e.tensor_copy(a_hi, f32(rounding[:, :])), hi)
            a_split = dve.do(lambda e, i: e.tensor_tensor(a_lo, a, f32(rounding[:, :]), ALU.subtract))

            edges = pool.do(lambda e, i: e.memset(window[:, :, :, :], 0.0), acts)
            strict_set = (strict_ready,)
            conved, gated, xs_ready, xs_turned = {}, {}, {}, {}
            ring = [0]

            later = []

            def run_later():
                for op in later:
                    op()
                later.clear()

            def conv_chunk(key, first_tile, dest, free):
                q = ring[0] % 2
                ring[0] += 1
                done, s = chunk(columns(w_in, lambda i: SSM_INNER + first_tile * P), feature_major(acthi, actlo), acts)
                seen = act.do(lambda e, i: e.activation(window[:, q, :, 2:T + 2], bank2(s), ACT.Copy),
                              done, edges, latest.get(f"window {q} read"))
                w = lambda tap, f: params[:, PAR["ssm_conv_w"] + tap * 32 + first_tile + f:][:, 0:1]
                for f in range(2):
                    t = act.do(lambda e, i, f=f: e.activation(taps[:, q, f, :], ps[:, s, f * T:(f + 1) * T], ACT.Copy,
                                                              scale=w(2, f)), latest.get(f"taps {q} read"), params_in)
                note(f"bank {s}", t)
                for tap in (0, 1, 3, 4):
                    prior = t
                    for f in range(2):
                        t = dve.do(lambda e, i, f=f, tap=tap: e.scalar_tensor_tensor(
                            out=taps[:, q, f, :], in0=window[:, q, f, tap:tap + T], scalar=w(tap, f),
                            in1=taps[:, q, f, :], op0=ALU.mult, op1=ALU.add), prior, seen)
                note(f"window {q} read", t)

                def silu():
                    for f in range(2):
                        t2 = act.do(lambda e, i, f=f: e.activation(
                            dest[:, f, :], taps[:, q, f, :], ACT.Silu,
                            bias=params[:, PAR["ssm_conv_b"] + first_tile + f:][:, 0:1]), t, *free())
                    conved[key] = note(f"taps {q} read", t2)
                later.append(silu)

            def z_chunk(n):
                done, s = chunk(columns(w_in, lambda i: n * WIDE), token_major(acthi, actlo), acts)
                gated[n] = note(f"bank {s}", act.do(lambda e, i: e.activation(
                    z[:, n // 2 % 2, :, n % 2 * WIDE:(n % 2 + 1) * WIDE], bank2(s), ACT.Silu), done,
                    gated_read.get((n - 4, 1))))
            gated_read = {}

            def turn_xs(G):
                for m in range(MT):
                    for t in range(4):
                        turned = pe.do(lambda e, i, m=m, t=t: e.transpose(
                            ps[:, 5, t * P:(t + 1) * P], xs_t[:, G % 2, t, m * P:(m + 1) * P], ident),
                            conved[G, 0], conved[G, 1], latest.get("turn bank"))
                    xs_ready[G] = note("turn bank", act.do(lambda e, i, m=m: e.activation(
                        xs[:, G % 2, m, :], ps[:, 5, :], ACT.Copy), turned, skip_made.get(4 * G - 5), multiplied_.get(4 * G - 5)))
                xs_turned[G] = turned

            part = lambda ap, m, d: ap[:, 64 * m + 32 * d:64 * m + 32 * d + 32]
            sums = ((le, 1, 0), (gt, 0, 0), (ge, 0, 1), (lt, 1, 1))

            def border(e, i):
                for n, (mask, m, d) in enumerate(sums):
                    out = e.matmul(ps[:, TOP, 32 * n:32 * n + 32], mask, part(a, m, d), start=True, stop=True)
                return out
            summed = pe.do(border, a_ready, table_in)
            edged = act.do(lambda e, i: e.activation(edge, ps[:, TOP, 0:128], ACT.Exp), summed)
            out_f = dve.do(lambda e, i: e.tensor_tensor(edge[:, 32:64], edge[:, 32:64], part(dt, 0, 0), ALU.mult), edged)
            out_b = dve.do(lambda e, i: e.tensor_tensor(edge[:, 96:128], edge[:, 96:128], part(dt, 1, 1), ALU.mult), edged)

            gram, gram_masked, summed_to, exped, made, multiplied_, crossed, summed_y, squared = ({} for _ in range(9))
            summed_over, xd, skip_made = {}, {}, {}
            totals = scratch(16)

            def make_gram(g):
                q = g % 2

                def mm(e, i):
                    for m in range(MT):
                        out = e.matmul(ps[:, TOP, m * T:(m + 1) * T], bc_t[:, q, m * P:(m + 1) * P], bc_t[:, 2 + q, :],
                                       start=True, stop=True)
                    return out
                gram[g] = pe.do(mm, conved[g // 2, 2], conved[g // 2, 3], gram_masked.get(g - 1, edged))
                diag = spread(ps[:, TOP, :], [T + P, 2], [1, P])
                dve.do(lambda e, i: e.tensor_tensor(gram_f[:, q, :, :], diag, spread(le, [0, 2], [1, P]), ALU.mult),
                       gram[g], made.get((g - 2, 1)), crossed.get((g - 2, 1)))
                dve.do(lambda e, i: e.tensor_tensor(gram_b[:, q, :, :], diag, spread(ge, [0, 2], [1, P]), ALU.mult))
                gram_masked[g] = dve.do(lambda e, i: e.tensor_copy(
                    gram_x[:, q, :, :].rearrange("p a n -> p (a n)"), ps[:, TOP, P:3 * P]))

            items = [(g, m) for g in range(SSM_GROUPS) for m in range(MT)]

            def head_cols(ap, m, d, g):
                return part(ap, m, d)[:, 4 * g:4 * g + 4]

            def group_cols(ring_, g, m):
                return spread(ring_[:, g // 2 % 2, m, 4 * HD * (g % 2):], [HD, 4], [1, HD])

            def prepare(n):
                if n >= len(items):
                    return
                g, m = items[n]
                par = n % 2
                for mask, d in ((le, 0), (ge, 1)):
                    for k, v in enumerate((a_hi, a_lo)):
                        summed_over[n] = pool.do(lambda e, i, mask=mask, d=d, k=k, v=v: e.tensor_tensor(
                            cum[d][k][:, :, :], spread(mask, [0, 4], [1, P]), spread(head_cols(v, m, d, g), [1, 4], [0, P]),
                            ALU.mult), a_split, summed_to.get(n - 1), acts)
                src, c = (0, 32) if m == 1 else (1, 96)
                xd[n] = pool.do(lambda e, i: e.tensor_tensor(
                    xdec[:, par, :, :], group_cols(xs, g, src), spread(edge[:, c + 4 * g:], [1, 4], [0, HD]), ALU.mult),
                    out_f, out_b, xs_ready[g // 2], crossed.get(items[n - 2] if n >= 2 else None))
                skip_made[n] = pool.do(lambda e, i: e.tensor_tensor(
                    skipped[:, par, :, :], group_cols(xs, g, m), spread(rows[:, ROW["skip"] + 4 * g:], [1, 4], [0, HD]),
                    ALU.mult), rows_in, summed_y.get(n - 2))

            def decays(n):
                g, m = items[n]
                par, gp = n % 2, g % 2

                def mm(e, i):
                    for d in range(2):
                        for k in range(2):
                            out = e.matmul(ps[:, 4, :], strict[:, d, :], cum[d][k][:, :, :].rearrange("p u n -> p (u n)"),
                                           start=d == k == 0, stop=d == k == 1)
                    return out
                summed_to[n] = pe.do(mm, summed_over[n], exped.get(n - 1), *strict_set)
                for u in range(4):
                    t = act.do(lambda e, i, u=u: e.activation(weight[:, par, u, :], gram_f[:, gp, m, :], ACT.Copy,
                                                              scale=head_cols(dt, m, 0, g)[:, u:u + 1]),
                               gram_masked[g], dt_ready, multiplied_.get(n - 2))
                exped[n] = act.do(lambda e, i: e.activation(decay[:, par, :, :].rearrange("p u n -> p (u n)"), ps[:, 4, :],
                                                            ACT.Exp), summed_to[n], made.get(items[n - 2] if n >= 2 else None))
                for u in range(4):
                    t2 = dve.do(lambda e, i, u=u: e.scalar_tensor_tensor(
                        out=weight[:, par, u, :], in0=gram_b[:, gp, m, :], scalar=head_cols(dt, m, 1, g)[:, u:u + 1],
                        in1=weight[:, par, u, :], op0=ALU.mult, op1=ALU.add), t)
                made[g, m] = dve.do(lambda e, i: e.tensor_tensor(weight[:, par, :, :], weight[:, par, :, :], decay[:, par, :, :],
                                                                 ALU.mult), t2, exped[n])

            def outputs(n):
                g, m = items[n]
                par = n % 2
                bank = 6 + par

                def inner(e, i):
                    for u in range(4):
                        out = e.matmul(ps[:, bank, u * HD:(u + 1) * HD], weight[:, par, u, :],
                                       xs[:, g // 2 % 2, m, (4 * (g % 2) + u) * HD:(4 * (g % 2) + u + 1) * HD],
                                       start=True, stop=True)
                    return out

                def cross(e, i):
                    return e.matmul(ps[:, bank, 4 * HD:8 * HD], gram_x[:, g % 2, 1 - m, :],
                                    xdec[:, par, :, :].rearrange("p u n -> p (u n)"), start=True, stop=True)
                crossed[g, m] = pe.do(cross, xd[n], gram_masked[g], summed_y.get(n - 2))
                multiplied_[n] = pe.do(inner, made[g, m], xs_ready[g // 2])
                c = 0 if m == 1 else 64
                yv = spread(y[:, m, 4 * HD * g:], [HD, 4], [1, HD])
                half = lambda k: spread(ps[:, bank, 4 * HD * k:], [HD, 4], [1, HD])
                t = dve.do(lambda e, i: e.tensor_tensor(carried[:, par, :, :], half(1),
                                                        spread(edge[:, c + 4 * g:], [1, 4], [0, HD]), ALU.mult),
                           multiplied_[n], edged, squared.get(n - 2))
                t = dve.do(lambda e, i: e.tensor_tensor(carried[:, par, :, :], carried[:, par, :, :], skipped[:, par, :, :],
                                                        ALU.add), t, skip_made[n])
                summed_y[n] = dve.do(lambda e, i: e.tensor_tensor(carried[:, par, :, :], half(0),
                                                                  carried[:, par, :, :], ALU.add), t)
                t = gated_read[g, m] = pool.do(lambda e, i: e.tensor_tensor(
                    yv, carried[:, par, :, :], group_cols(z, g, m), ALU.mult), summed_y[n], gated[g], acts)

                def square():
                    squared[n] = act.do(lambda e, i: e.activation(
                        carried[:, par, :, :].rearrange("p u n -> p (u n)"), y[:, m, 4 * HD * g:4 * HD * (g + 1)],
                        ACT.Square, accum_out=totals[:, 2 * g + m:2 * g + m + 1]), t)
                later.append(square)

            scaled = {}

            def norm_pair(G):
                r, r_ready = rsqrt(squared[4 * G + 3], totals[:, 4 * G:4 * G + 4], 4 * HD, 4, 1e-5)
                for m in range(MT):
                    v = spread(y[:, m, 8 * HD * G:], [4 * HD, 2], [1, 4 * HD])
                    scaled[G] = pool.do(lambda e, i, v=v, m=m: e.tensor_tensor(
                        v, v, spread(r[:, m:], [2, 2], [0, 4 * HD]), ALU.mult), r_ready)

            def turn_y(half, hi_part, lo_part, banks, low, *waits):
                for k in range(KT):
                    b = banks[k % 4]
                    for m in range(MT):
                        turned = pe.do(lambda e, i, b=b, m=m, k=k: e.transpose(
                            ps[:, b, m * P:(m + 1) * P], y[:, m, (KT * half + k) * P:(KT * half + k + 1) * P], ident),
                            scaled[2 * half + 1], low.get(k - 4), *waits)
                    g_ = params[:, PAR["ssm_norm"] + KT * half + k:][:, 0:1]
                    hi = act.do(lambda e, i, b=b, k=k, g_=g_: e.activation(hi_part[:, k, :], ps[:, b, 0:T], ACT.Copy, scale=g_),
                                turned)
                    low[k] = dve.do(lambda e, i, b=b, k=k, g_=g_: e.scalar_tensor_tensor(
                        out=lo_part[:, k, :], in0=ps[:, b, 0:T], scalar=g_, in1=f32(hi_part[:, k, :]), op0=ALU.mult,
                        op1=ALU.subtract), hi)
                return low[KT - 1]

            w_out = A["ssm_w_out_2"][0]

            def out_chunk(half, n, hi_part, lo_part, ready):
                def src(i, slot):
                    a_ = slot[:, :].rearrange("p (k n) -> p k n", k=KT)
                    b_ = w_out.rearrange("(k p) n -> p k n", p=P)[:, KT * half:KT * (half + 1), n * WIDE:(n + 1) * WIDE]
                    return [(a_[:, 0:4, :], b_[:, 0:4, :]), (a_[:, 4:8, :], b_[:, 4:8, :])]

                def mm(e, i, s, hi, lo):
                    wh, wl = (w[:, :].rearrange("p (k n) -> p k n", k=KT) for w in (hi, lo))
                    for m in range(MT):
                        for k in range(KT):
                            xh, xl = (v[:, k, m * P:(m + 1) * P] for v in (hi_part, lo_part))
                            for q, (p_, w_) in enumerate(((xh, wh), (xh, wl), (xl, wh))):
                                out = e.matmul(ps[:, out_banks[n], m * T:(m + 1) * T], p_, w_[:, k, :],
                                               start=half == m == k == q == 0,
                                               stop=half == 1 and k == KT - 1 and q == 2, skip_group_check=True)
                    return out
                return chunk(src, mm, ready)[0]
            out_banks = (0, 1, 2, 5)

            for G in range(4):
                steps = [lambda: conv_chunk((G, 0), 4 * G, xs_t[:, G % 2, 0:2, :], lambda: (xs_turned.get(G - 2),)),
                         lambda: conv_chunk((G, 1), 4 * G + 2, xs_t[:, G % 2, 2:4, :], lambda: ()),
                         lambda: z_chunk(2 * G),
                         lambda: conv_chunk((G, 2), 16 + 2 * G, bc_t[:, 0:2, :], lambda: (gram.get(2 * G - 1),)),
                         lambda: conv_chunk((G, 3), 24 + 2 * G, bc_t[:, 2:4, :], lambda: (gram.get(2 * G - 1),)),
                         lambda: z_chunk(2 * G + 1)]
                first = 4 * (G - 1)
                for k in range(6):
                    n = first + {1: 0, 2: 1, 4: 2, 5: 3}[k] if G > 0 and k in (1, 2, 4, 5) else None
                    if n is not None:
                        decays(n)
                        prepare(n + 1)
                    if k in (0, 3) and G > 0:
                        make_gram(2 * G - 2 + k // 3)
                    if k == 3 and G > 1:
                        norm_pair(G - 2)
                    former = list(later)
                    later.clear()
                    steps[k]()
                    for op in former:
                        op()
                    if n is not None:
                        outputs(n)
                    if k == 3:
                        turn_xs(G)
                        if G == 0:
                            prepare(0)
            z_read = gated[7]
            low_first = {}
            run_later()
            make_gram(6)
            decays(12)
            prepare(13)
            norm_pair(2)
            first_half = turn_y(0, acthi, actlo, out_banks, low_first, z_read, xs_ready[3])
            for k in range(4):
                if k > 0:
                    decays(12 + k)
                    prepare(12 + k + 1)
                done = out_chunk(0, k, acthi, actlo, first_half)
                if k == 0:
                    make_gram(7)
                run_later()
                outputs(12 + k)
            run_later()
            norm_pair(3)
            latest["lnrow"] = summed_to[15]
            second_half = turn_y(1, mixhi, mixlo, (TOP, 4, 6, 7), {})
            for n in range(4):
                done = out_chunk(1, n, mixhi, mixlo, second_half)
                added = add_alpha(done, bank2(out_banks[n]), slice(None), slice(n * WIDE, (n + 1) * WIDE))
                if n < SLOTS:
                    note(f"bank {n}", added)
            return [added, added]

        def network():
            acts = rms_norm(x_in, PAR["norm_mixer0"])
            load_later_constants(acts)
            mixed = conv_layer(acts)
            yield project(A["conv_w_out"][0], mixhi, mixlo, mixed, add_plain)
            acts = rms_norm(latest_x[0], PAR["norm_ffn0"])
            yield swiglu(0)(acts)
            acts = rms_norm(latest_x[0], PAR["norm_mixer1"])
            mixed = swa_layer(acts)
            yield project(A["attn_w_o"][0], mixhi, mixlo, mixed, add_plain)
            acts = rms_norm(latest_x[0], PAR["norm_ffn1"])
            landed = load_rpb(mixed)
            yield swiglu(1)(acts)
            for m in range(MT):
                flip_rpb(m, landed)
            acts = to_features(latest_x[0], rows_=x)
            mixed = na_layer(acts)
            added = project(A["attn_w_out_2"][0], mixhi, mixlo, mixed, add_alpha)
            yield layer_norm(added, A["ln1_g_2"][0], A["ln1_b_2"][0])
            acts = to_features(latest_x[0], rows_=x)
            added = squared_relu(0)(acts)
            yield layer_norm(added, A["ln2_g_2"][0], A["ln2_b_2"][0])
            acts = to_features(latest_x[0], rows_=x)
            added = ssm_layer(acts)
            yield layer_norm(added, A["ln1_g_2"][1], A["ln1_b_2"][1])
            acts = to_features(latest_x[0], rows_=x)
            added = squared_relu(1)(acts)
            yield layer_norm(added, A["ln2_g_2"][1], A["ln2_b_2"][1])

        latest_x = [None]
        for n, ready in enumerate(network()):
            latest_x[0] = ready
            if n == stop_after:
                break
        out_landed = sem("out_landed")
        sp.add(lambda e, i: e.dma_start(A["out"].rearrange("b (m p) d -> p (b m) d", p=P), x[:, :, :]), tuple(ready),
               (out_landed, 16))

        block = ctx.enter_context(nc.Block())

        @block.sync
        def _(eng):
            sp.emit(eng)
            for landed in (*consts, out_landed):
                eng.wait_ge(landed, 16)

        @block.scalar
        def _(eng):
            act.emit(eng)

        @block.vector
        def _(eng):
            dve.emit(eng)

        @block.tensor
        def _(eng):
            pe.emit(eng)

        @block.gpsimd
        def _(eng):
            pool.emit(eng)


def spans(sizes):
    out, n = {}, 0
    for name, size in sizes:
        out[name] = n
        n += size
    return out, n


TAB, TAB_N = spans([("ident", P), ("le", P), ("ge", P), ("gt", P), ("lt", P), ("flip", P), ("dist", 2 * T), ("window", 2 * T),
                    ("near", 2 * T), ("cos", 2 * HD), ("sin", 2 * HD)])
PAR, PAR_N = spans([("norm_mixer0", KT), ("norm_ffn0", KT), ("norm_mixer1", KT), ("norm_ffn1", KT),
                    ("conv_w", 3 * KT), ("q_gain", 1), ("k_gain", 1), ("ssm_conv_w", SSM_TAPS * 32),
                    ("ssm_conv_b", 32), ("ssm_norm", 16)])
ROW, ROW_N = spans([("sinks1", 16), ("sinks2", 8), ("dt_bias", 64), ("a_log", 64), ("skip", 32)])

TOTAL_CHUNKS = 202
STOPS = [16, 49, 59, 92, 105, 137, 170, 202]


def shape_tables():
    t = np.arange(T)
    a, b = np.arange(P)[:, None], np.arange(P)[None, :]
    out = np.zeros((P, TAB_N), np.float32)

    def put(name, v):
        out[:, TAB[name]:TAB[name] + v.shape[1]] = v

    put("ident", a == b)
    put("le", a <= b)
    put("ge", a >= b)
    put("gt", a > b)
    put("lt", a < b)
    put("flip", a == b // 64 * 64 + 63 - b % 64)
    far = np.float32(1e30)
    rows = lambda v: v.reshape(MT, P, -1).transpose(1, 0, 2).reshape(P, -1)
    dist = (t[:, None] - t[None, :]).astype(np.float32)
    put("dist", rows(np.where((dist >= 0) & (dist < 128), dist, far)))
    put("window", rows(np.where(np.abs(dist) <= 128, np.float32(0), -far)))
    c = t % 64
    start = np.clip(c - 8, 0, 48)
    near = (c[None, :] >= start[:, None]) & (c[None, :] < start[:, None] + 16)
    put("near", rows(np.where(near, np.float32(0), -far)))
    half = HD // 2
    inv = np.float32(10000.0) ** (-np.arange(half, dtype=np.float32) / np.float32(half))
    ang = t.astype(np.float32)[:, None] * inv[None, :].astype(np.float32)
    cos, sin = np.cos(ang).astype(np.float32), np.sin(ang).astype(np.float32)
    put("cos", rows(np.concatenate([cos, cos], 1)))
    put("sin", rows(np.concatenate([-sin, sin], 1)))
    return out


_WEIGHTS = ["x", "conv_w_in", "conv_w_out", "attn_w_qkv", "attn_w_o", "ffn_w_gate_up", "ffn_w_down", "attn_w_in_2",
            "attn_w_out_2", "ssm_w_in_2", "ssm_w_out_2", "mlp_w1_2", "mlp_w2_2", "ln1_g_2", "ln1_b_2", "ln2_g_2",
            "ln2_b_2"]


def kernel(**inputs):
    import concourse.bacc as bacc
    from concourse.bass_utils import run_bass_kernel_spmd

    get = {k: np.asarray(v) for k, v in inputs.items()}

    def by_feature(v):
        return v.reshape(-1, P).T

    arrays = {name: np.ascontiguousarray(get[name]) for name in _WEIGHTS}
    arrays["table"] = shape_tables()
    arrays["params"] = np.ascontiguousarray(np.concatenate([
        by_feature(get["norm_mixer"][0]), by_feature(get["norm_ffn"][0]), by_feature(get["norm_mixer"][1]),
        by_feature(get["norm_ffn"][1]), by_feature(get["conv_w"][0]), by_feature(np.tile(get["attn_q_gain"][0], 2)),
        by_feature(np.tile(get["attn_k_gain"][0], 2)), by_feature(get["ssm_conv_w_2"][0]),
        by_feature(get["ssm_conv_b_2"][0]), by_feature(get["ssm_norm_w_2"][0])], 1))
    arrays["rows"] = np.concatenate([get["attn_sinks"][0], get["attn_sink_2"][0], get["ssm_dt_bias_2"][0],
                                     get["ssm_A_log_2"][0].reshape(-1), get["ssm_D_2"][0]])[None, :]
    rpb = get["attn_rpb_2"][0]
    arrays["rpb"] = np.pad(rpb, ((0, 0), (0, 0), (48, 48)))

    nc = bacc.Bacc("TRN2", target_bir_lowering=False, num_devices=1)
    A = {name: nc.dram_tensor(f"in_{name}", a.shape, mybir.dt.from_np(a.dtype), kind="ExternalInput").ap()
         for name, a in arrays.items()}
    A["out"] = nc.dram_tensor("out", get["x"].shape, F32, kind="ExternalOutput").ap()
    build(nc, A, STOP)
    r = run_bass_kernel_spmd(nc, [{f"in_{n}": a for n, a in arrays.items()}], core_ids=[0])
    return r.results[0]["out"]


STOP = None
```

```python
import math
from contextlib import ExitStack

import numpy as np

import concourse.bass as bass
from concourse import mybir

F32 = mybir.dt.float32
F32R = mybir.dt.float32r
ALU = mybir.AluOpType
ACT = mybir.ActivationFunctionType
AX = mybir.AxisListType.X

P = 128
T = 256
MT = T // P
D = 1024
KT = D // P
SLOTS = 3
CHUNK = 2048
WIDE = CHUNK // KT
LEAD = 2
EPS = 1e-6
LN_EPS = 1e-5
HD = 64
D_FF = 2816
D_FF2 = 4096
QKV1 = 1536
QKV2 = 2304
ALPHA = 4 ** 0.25
SSM_IN = 6208
SSM_INNER = 2048
SSM_HEADS = 32
SSM_GROUPS = 8
SSM_TAPS = 5
TOP = 3
ACC = 4


class Loop:

    def __init__(self, trips):
        self.trips = trips


class Mark:

    def __init__(self, sem, base, stride=0, loop=None):
        self.sem, self.base, self.stride, self.loop = sem, base, stride, loop

    def back(self, trips=1):
        return Mark(self.sem, self.base - trips * self.stride, self.stride, self.loop)


class Later:

    def __init__(self):
        self.mark = None


class Queue:

    def __init__(self, sem):
        self.sem, self.count, self.ops, self.open, self.inner = sem, 0, [], None, []

    def add(self, fn, waits, inc):
        (self.ops if self.open is None else self.inner).append((fn, waits, inc))

    def do(self, fn, *waits):
        self.count += 1
        m = Mark(self.sem, self.count, 0, self.open)
        self.add(fn, waits, (self.sem, 1))
        if self.open is not None:
            self.inner_marks.append(m)
        return m

    def enter(self, loop):
        self.open, self.inner, self.inner_marks, self.at_entry = loop, [], [], self.count

    def leave(self):
        per_trip = self.count - self.at_entry
        for m in self.inner_marks:
            m.stride = per_trip
        self.count += per_trip * (self.open.trips - 1)
        if self.inner:
            self.ops.append((self.open, self.inner))
        self.open = None

    def emit(self, eng):
        known = {}

        def run(ops, loop, i):
            moving = {}
            for fn, waits, inc in ops:
                for w in waits:
                    if isinstance(w, Later):
                        w = w.mark
                    if w is None:
                        continue
                    key = id(w.sem)
                    if loop is not None and w.loop is loop and w.stride:
                        if moving.get(key, -1) >= w.base:
                            continue
                        moving[key] = w.base
                        assert w.base > 0
                        eng.wait_ge(w.sem, i * w.stride + w.base)
                    else:
                        value = w.base + (w.stride * (w.loop.trips - 1) if w.loop else 0)
                        if value <= 0 or known.get(key, 0) >= value:
                            continue
                        known[key] = value
                        eng.wait_ge(w.sem, value)
                ins = fn(eng, i)
                if inc is not None:
                    ins.then_inc(*inc)

        for op in self.ops:
            if isinstance(op[0], Loop):
                with eng.Fori(0, op[0].trips) as i:
                    run(op[1], op[0], i)
            else:
                run([op], None, 0)


def build(nc, A, stop_after=None):
    ctx = ExitStack()
    with ctx:
        sem = lambda name: ctx.enter_context(nc.semaphore(name))
        sp, act, dve, pe, pool = (Queue(sem(f"{n}_done")) for n in ("sp", "act", "dve", "pe", "pool"))
        queues = (sp, act, dve, pe, pool)
        raw_landed = [sem(f"raw_landed{s}") for s in range(SLOTS)]
        rounded = sem("chunks_rounded")
        split = sem("chunks_split")
        multiplied = sem("chunks_multiplied")

        at = [(nc.sbuf_base + 31) // 32 * 32]

        def place(name, shape, dtype=F32, offset=None):
            if offset is None:
                offset = at[0]
                at[0] += (int(np.prod(shape[1:])) * 4 + 31) // 32 * 32
            t = nc.alloc_sbuf_tensor_at(name, shape, dtype, offset=offset)
            return t, offset

        raw = [place(f"raw{s}", [P, CHUNK])[0] for s in range(SLOTS)]
        whi = [place(f"whi{s}", [P, CHUNK], F32R)[0] for s in range(SLOTS)]
        wlo = [place(f"wlo{s}", [P, CHUNK], F32R)[0] for s in range(SLOTS)]
        x, _ = place("x", [P, MT, D])
        h, h_at = place("h", [P, MT, D])
        acthi, act_at = place("acthi", [P, KT, T], F32R)
        actlo, _ = place("actlo", [P, KT, T], F32R)
        mixhi, mixhi_at = place("mixhi", [P, 2 * KT, T], F32R)
        mixlo, mixlo_at = place("mixlo", [P, 2 * KT, T], F32R)
        hidhi, hid_at = place("hidhi", [P, 3, 2, T], F32R)
        hidlo, _ = place("hidlo", [P, 3, 2, T], F32R)
        table, _ = place("table", [P, A["table"].shape[1]])
        params, _ = place("params", [P, A["params"].shape[1]])
        rows, _ = place("rows", [P, A["rows"].shape[1]])
        small, _ = place("small", [P, 896])
        lnrow, lnrow_at = place("lnrow", [P, 2, D])
        zero, _ = place("zero", [P, 256], F32R)
        strict, _ = place("strict", [P, 2, P], F32R)
        shared = at[0]
        ps = ctx.enter_context(nc.psum_tensor("ps", [P, 8, 512], F32))

        def bank2(b):
            return ps[:, b, :].rearrange("p (a n) -> p a n", a=2)

        def f32(ap):
            return ap.bitcast(F32)

        latest = {}
        noted, wanted = set(), {}

        def note(name, mark):
            latest[name] = mark
            noted.add(name)
            return mark

        def last(name):
            if chunk_no["loop"] is None or name in noted:
                return latest.get(name)
            return wanted.setdefault(name, Later())

        def loop_begin(trips):
            loop = Loop(trips)
            noted.clear()
            wanted.clear()
            for q in queues:
                q.enter(loop)
            chunk_no["loop"], chunk_no["entry"] = loop, chunk_no["n"]

        def loop_end():
            loop = chunk_no["loop"]
            per_trip = chunk_no["n"] - chunk_no["entry"]
            assert per_trip % SLOTS == 0
            for m, per_chunks in chunk_no["marks"]:
                m.stride = m.stride * per_trip // per_chunks
            chunk_no["marks"].clear()
            chunk_no["n"] += per_trip * (loop.trips - 1)
            chunk_no["loop"] = None
            for q in queues:
                q.leave()
            for name, later in wanted.items():
                m = latest.get(name)
                later.mark = m.back() if name in noted else m

        def bodies(n, body, peel_last=False):
            body(lambda i: 0)
            trips = n - 1 - peel_last
            if trips > 1:
                loop_begin(trips)
                body(lambda i: i + 1)
                loop_end()
            elif trips == 1:
                body(lambda i: 1)
            if peel_last and n > 1:
                body(lambda i: n - 1)

        consts = [sem(f"const_landed{n}") for n in range(6)]
        const_marks = [Mark(s, 16) for s in consts]
        for m in range(MT):
            sp.add(lambda e, i, m=m: e.dma_start(x[:, m, :], A["x"][0, m * P:(m + 1) * P, :]), (), (consts[m], 16))
        act.add(lambda e, i: e.dma_start(table[:, 0:P], A["table"][:, 0:P]), (), (consts[2], 16))
        act.add(lambda e, i: e.dma_start(params[:, :], A["params"]), (), (consts[3], 16))

        def load_later_constants(ready):
            act.add(lambda e, i: e.dma_start(table[:, P:], A["table"][:, P:]), (ready,), (consts[4], 16))
            act.add(lambda e, i: e.dma_start(rows[:, :], A["rows"].to_broadcast([P, A["rows"].shape[1]])), (), (consts[5], 16))
        *x_in, ident_in, params_in, table_in, rows_in = const_marks
        zeroed = pool.do(lambda e, i: e.memset(f32(zero[:, :]), 0.0))
        minus_half = small[:, 0:64]
        halved = pool.do(lambda e, i: e.memset(minus_half, -0.5))

        chunk_no = {"n": 0, "loop": None, "entry": 0, "marks": [], "total": TOTAL_CHUNKS if stop_after is None else STOPS[stop_after]}

        def chunk_mark(sem_, base, grows=1, per_chunks=1):
            loop = chunk_no["loop"]
            m = Mark(sem_, base, grows if loop else 0, loop)
            if loop is not None:
                chunk_no["marks"].append((m, per_chunks))
            return m

        def split_chunk(c, hold=False):
            if chunk_no["loop"] is None and c >= chunk_no["total"]:
                return
            s = c % SLOTS
            landed = chunk_mark(raw_landed[s], 32 * (c // SLOTS + 1), 32, SLOTS)
            free = chunk_mark(multiplied, c - SLOTS + 1) if c >= SLOTS else None
            done = chunk_mark(rounded, c + 1)
            act.add(lambda e, i: e.activation(whi[s][:, :], raw[s][:, :], ACT.Copy),
                    (landed, free), (rounded, 1))

            def rest():
                dve.add(lambda e, i: e.tensor_tensor(wlo[s][:, :], raw[s][:, :], f32(whi[s][:, :]), ALU.subtract),
                        (done,), (split, 1))
            held.append(rest)
            if not hold:
                run_held()

        held = []

        def run_held():
            while held:
                held.pop(0)()

        def chunk(src, products, *waits, early=(), hold=False):
            c = chunk_no["n"]
            products_of = products
            chunk_no["n"] += 1
            s = c % SLOTS
            for half in range(2):
                sp.add(lambda e, i, half=half: e.dma_start(*src(i, raw[s])[half]),
                       (chunk_mark(split, c - SLOTS + 1) if c >= SLOTS else None,), (raw_landed[s], 16))
            split_chunk(c + LEAD, hold)
            early_done.clear()
            needs = [(*waits,)] * (len(early) + 1)
            if pair_ready:
                *early, products = (lambda *a, k=k: products_of(*a, ks=(k, k + 1)) for k in range(0, KT, 2))
                needs = [(ready,) for ready in pair_ready]
                pair_ready.clear()
            for part, need in zip(early, needs):
                early_done.append(pe.do(lambda e, i, part=part: part(e, i, s, whi[s], wlo[s]),
                                        chunk_mark(split, c + 1), last(f"bank {s}"), *need))
            pe.add(lambda e, i: products(e, i, s, whi[s], wlo[s]),
                   (chunk_mark(split, c + 1), last(f"bank {s}"), *waits, *needs[-1]), (multiplied, 1))
            return chunk_mark(multiplied, c + 1), s

        early_done, pair_ready, turned = [], [], {}

        def columns(w, first):
            def src(i, slot):
                a = slot[:, :].rearrange("p (k n) -> p k n", k=KT)
                b = w.rearrange("(k p) n -> p k n", p=P)[:, :, bass.ds(first(i), WIDE)]
                return [(a[:, 0:4, :], b[:, 0:4, :]), (a[:, 4:8, :], b[:, 4:8, :])]
            return src

        def feature_major(xhi, xlo):
            def mm(e, i, s, hi, lo, ks=None):
                whi_, wlo_ = (w[:, :].rearrange("p (k n) -> p k n", k=KT) for w in (hi, lo))
                for f in range(2):
                    out, cols = ps[:, s, f * T:(f + 1) * T], slice(f * P, (f + 1) * P)
                    for k in ks or range(KT):
                        start = k == 0 and (f == 0 or ks is None)
                        e.matmul(out, whi_[:, k, cols], xhi[:, k, :], start=start, stop=False, skip_group_check=True)
                        e.matmul(out, whi_[:, k, cols], xlo[:, k, :], start=False, stop=False, skip_group_check=True)
                        last = e.matmul(out, wlo_[:, k, cols], xhi[:, k, :], start=False, stop=k == KT - 1,
                                        skip_group_check=True)
                return last
            return mm

        def token_major(xhi, xlo, cols=slice(0, WIDE)):
            def mm(e, i, s, hi, lo, ks=None, tokens=range(MT)):
                whi_, wlo_ = (w[:, :].rearrange("p (k n) -> p k n", k=KT)[:, :, cols] for w in (hi, lo))
                n = cols.stop - cols.start
                for m in tokens:
                    out = ps[:, s, m * T:m * T + n]
                    for k in ks or range(KT):
                        xh, xl = (v[:, k, m * P:(m + 1) * P] for v in (xhi, xlo))
                        start = k == 0 and (m == 0 or ks is None)
                        e.matmul(out, xh, whi_[:, k, :], start=start, stop=False, skip_group_check=True)
                        e.matmul(out, xh, wlo_[:, k, :], start=False, stop=False, skip_group_check=True)
                        last = e.matmul(out, xl, whi_[:, k, :], start=False, stop=k == KT - 1, skip_group_check=True)
                return last
            return mm

        ident = table[:, TAB["ident"]:TAB["ident"] + P]

        def keep_warm(n, *waits):
            def mm(e, i):
                for _ in range(n):
                    out = e.matmul(ps[:, TOP, 0:T], zero[:, 0:P], zero[:, :], start=True, stop=True)
                return out
            pe.do(mm, zeroed, *waits)

        def to_features(ready, gain=None, rows_=None, shift=None):
            rows_ = h if rows_ is None else rows_
            column = lambda first, k: params[:, first + k:first + k + 1]
            full = h[:, :, :].rearrange("p m (k n) -> p (m k) n", n=T)
            pair = lambda b: slice(2 * b, 2 * b + 2)
            made, hi, lo = {}, {}, {}
            run_held()
            if gain is not None:
                keep_warm(24)
            for b in range(4):
                for k in (2 * b, 2 * b + 1):
                    for m in range(MT):
                        out = ps[:, ACC + b, (k % 2) * T + m * P:(k % 2) * T + (m + 1) * P]
                        turned[b] = pe.do(lambda e, i, out=out, m=m, k=k: e.transpose(
                            out, rows_[:, m, k * P:(k + 1) * P], ident), ready[m], ident_in)

            def make_full(b):
                for k in (2 * b, 2 * b + 1):
                    src = ps[:, ACC + b, (k % 2) * T:(k % 2 + 1) * T]
                    if b % 2 == 0:
                        made[b] = act.do(lambda e, i, k=k, src=src: e.activation(
                            full[:, k, :], src, ACT.Identity, scale=column(gain, k), bias=column(shift, k)),
                            turned[b], params_in)
                    else:
                        made[b] = dve.do(lambda e, i, k=k, src=src: e.tensor_scalar(
                            full[:, k, :], src, column(gain, k), column(shift, k), ALU.mult, ALU.add),
                            turned[b], params_in)

            if shift is not None:
                make_full(0)
                make_full(1)
            for b in range(4):
                if shift is not None:
                    hi[b] = act.do(lambda e, i, b=b: e.activation(acthi[:, pair(b), :], full[:, pair(b), :], ACT.Copy), made[b])
                    if b == 0:
                        make_full(2)
                    lo[b] = dve.do(lambda e, i, b=b: e.tensor_tensor(
                        actlo[:, pair(b), :], full[:, pair(b), :], f32(acthi[:, pair(b), :]), ALU.subtract), hi[b])
                    if b == 0:
                        make_full(3)
                elif gain is not None:
                    for k in (2 * b, 2 * b + 1):
                        hi[b] = act.do(lambda e, i, k=k, b=b: e.activation(
                            acthi[:, k, :], bank2(ACC + b)[:, k % 2, :], ACT.Copy, scale=column(gain, k)), turned[b], params_in)
                    for k in (2 * b, 2 * b + 1):
                        lo[b] = dve.do(lambda e, i, k=k, b=b: e.scalar_tensor_tensor(
                            out=actlo[:, k, :], in0=bank2(ACC + b)[:, k % 2, :], scalar=column(gain, k),
                            in1=f32(acthi[:, k, :]), op0=ALU.mult, op1=ALU.subtract), hi[b])
                else:
                    hi[b] = act.do(lambda e, i, b=b: e.activation(acthi[:, pair(b), :], bank2(ACC + b), ACT.Copy), turned[b])
                    lo[b] = dve.do(lambda e, i, b=b: e.tensor_tensor(
                        actlo[:, pair(b), :], bank2(ACC + b), f32(acthi[:, pair(b), :]), ALU.subtract), hi[b])
            pair_ready.extend(lo[b] for b in range(4))
            return lo[3]

        small_at = [64]

        def scratch(n):
            small_at[0] += n
            return small[:, small_at[0] - n:small_at[0]]

        def spread(ap, *dims):
            return bass.AP(ap.tensor, ap.offset, [list(ap.ap[0]), *[list(d) for d in dims]])

        def rsqrt(ready, total, n, count, eps):
            mean, out = scratch(count), scratch(count)
            ready = ready if isinstance(ready, (list, tuple)) else (ready,)
            ms = pool.do(lambda e, i: e.tensor_scalar(mean, total, 1.0 / n, eps, ALU.mult, ALU.add), *ready, halved)
            return out, pool.do(lambda e, i: e.tensor_tensor(out, mean, minus_half[:, 0:count], ALU.pow), ms)

        class Residual:

            def __init__(self, kind, pieces):
                self.kind, self.pieces = kind, pieces
                self.stats = scratch(MT * pieces * 6) if kind == "ln" else scratch(MT * pieces) if kind == "rms" else None
                self.ready = [None] * MT

            def add(self, alpha, done, src, m, piece):
                n = D // self.pieces
                cols = slice(piece * n, (piece + 1) * n)
                v = x[:, m, cols]
                if alpha:
                    added = dve.do(lambda e, i: e.scalar_tensor_tensor(out=v, in0=v, scalar=ALPHA, in1=src, op0=ALU.mult,
                                                                       op1=ALU.add), done)
                else:
                    added = dve.do(lambda e, i: e.tensor_tensor(v, src, v, ALU.add), done)
                self.ready[m] = added
                self.take(m, piece, added)
                return added

            def take(self, m, piece, added):
                n = D // self.pieces
                v, at_ = x[:, m, piece * n:(piece + 1) * n], m * self.pieces + piece
                if self.kind == "rms":
                    self.ready[m] = act.do(lambda e, i: e.activation(h[:, m, piece * n:(piece + 1) * n], v, ACT.Square,
                                                                     accum_out=self.stats[:, at_:at_ + 1]), added)
                elif self.kind == "ln":
                    self.ready[m] = dve.do(lambda e, i: e.bn_stats(self.stats[:, 6 * at_:6 * at_ + 6], v), added)

        def rms_norm(res, gain):
            total = res.stats
            ready = res.ready
            if res.pieces > 1:
                total = scratch(MT)
                ready = [dve.do(lambda e, i: e.tensor_reduce(total, res.stats.rearrange("p (m n) -> p m n", m=MT), AX, ALU.add),
                                *res.ready)]
            rms, r = rsqrt(ready, total, D, MT, EPS)
            scaled = [dve.do(lambda e, i, m=m: e.tensor_scalar(h[:, m, :], x[:, m, :], rms[:, m:m + 1], None, ALU.mult), r)
                      for m in range(MT)]
            return to_features(scaled, gain)

        def conv_layer(acts):
            b_sb, off = place("conv_b", [P, 2, T], offset=shared)
            u, _ = place("conv_u", [P, 2, T + 2], offset=shared + 2048)
            y, _ = place("conv_y", [P, 2, T], offset=shared + 2048 + 2112)
            cleared = pool.do(lambda e, i: e.memset(u[:, :, :], 0.0))
            w_in = A["conv_w_in"][0]

            def body(j):
                done, s = chunk(columns(w_in, lambda i: j(i) * WIDE), feature_major(acthi, actlo), acts)
                b_copied = note(f"bank {s}", act.do(lambda e, i, s=s: e.activation(b_sb[:, :, :], bank2(s), ACT.Copy),
                                                    done, last("b read")))
                done, s = chunk(columns(w_in, lambda i: j(i) * WIDE + 2 * D), feature_major(acthi, actlo))
                tap = note("b read", note(f"bank {s}", dve.do(lambda e, i, s=s: e.tensor_tensor(
                    u[:, :, 2:T + 2], bank2(s), b_sb[:, :, :], ALU.mult), done, b_copied, cleared)))
                for n in range(3):
                    for f in range(2):
                        def one(e, i, f=f, n=n):
                            w = params[:, bass.ds(j(i) * 2 + (PAR["conv_w"] + (2 - n) * KT + f), 1)]
                            src = u[:, f, 2 - n:2 - n + T]
                            if n == 0:
                                return e.tensor_scalar(y[:, f, :], src, w, None, ALU.mult)
                            return e.scalar_tensor_tensor(out=y[:, f, :], in0=src, scalar=w, in1=y[:, f, :],
                                                          op0=ALU.mult, op1=ALU.add)
                        note(f"tap {f}", dve.do(one, tap if n == 0 else last(f"tap {f}"), last("y read"), params_in))
                done, s = chunk(columns(w_in, lambda i: j(i) * WIDE + D), feature_major(acthi, actlo))
                gated = note(f"bank {s}", dve.do(lambda e, i, s=s: e.tensor_tensor(
                    y[:, :, :], bank2(s), y[:, :, :], ALU.mult), done, last("tap 0"), last("tap 1")))
                note("y read", split_mix(gated, lambda i: j(i) * 2, 2, y[:, :, :]))

            bodies(4, body)
            pair_ready.extend([last("y read").back()] * 3 + [last("y read")])
            return last("y read")

        def split_mix(ready, first, n, src):
            hi = act.do(lambda e, i: e.activation(mixhi[:, bass.ds(first(i), n), :], src, ACT.Copy), ready)
            return dve.do(lambda e, i: e.tensor_tensor(mixlo[:, bass.ds(first(i), n), :], src,
                                                       f32(mixhi[:, bass.ds(first(i), n), :]), ALU.subtract), hi)

        def project(w, xhi, xlo, ready, alpha, res):
            for n in range(D // WIDE):
                if n < D // WIDE - 1:
                    done, s = chunk(columns(w, lambda i, n=n: n * WIDE), token_major(xhi, xlo), ready)
                    for m in range(MT):
                        note(f"bank {s}", res.add(alpha, done, bank2(s)[:, m, :], m, n))
                else:
                    one = lambda m: (lambda e, i, s, hi, lo: token_major(xhi, xlo)(
                        e, i, (s, ACC + 3)[m], hi, lo, tokens=(m,)))
                    done, s = chunk(columns(w, lambda i, n=n: n * WIDE), one(1), ready, early=(one(0),), hold=True)
                    note(f"bank {s}", res.add(alpha, early_done[0], bank2(s)[:, 0, :], 0, n))
                    res.add(alpha, done, bank2(ACC + 3)[:, 1, :], 1, n)
            return res

        gate_sb, _ = place("gate_sb", [P, 2, T], offset=shared)
        prod_sb, _ = place("prod_sb", [P, 2, 2 * T], offset=shared + 2048)

        def feed_forward(acts, up_src, n_up, down, pairs, slots, hidden, alpha, res):

            def down_products(hs):
                def mm(e, i, s, hi, lo):
                    wh, wl = (w[:, :].rearrange("p (k n) -> p k n", k=2) for w in (hi, lo))
                    for k in range(2):
                        for m in range(MT):
                            xh, xl = (v[:, hs, k, m * P:(m + 1) * P] for v in (hidhi, hidlo))
                            for a, b in ((xh, wh), (xh, wl), (xl, wh)):
                                for n in range(2):
                                    mm_ = e.matmul(ps[:, ACC + 2 * m + n, :], a, b[:, k, n * 512:(n + 1) * 512],
                                                   start=False, stop=False, skip_group_check=True)
                    return mm_
                return mm

            def down_src(t):
                def src(i, slot):
                    a = slot[:, :].rearrange("p (k n) -> p k n", k=2)
                    return [(a[:, k, :], down[bass.ds(t(i) * 2 * P + k * P, P), :]) for k in range(2)]
                return src

            def up(t, hs):
                for q in range(n_up):
                    done, s = chunk(up_src(t, q), feature_major(acthi, actlo), acts)
                    hidden(done, s, hs, q)

            def open_accumulators(e, i):
                for b in range(4):
                    for half in range(2):
                        mm = e.matmul(ps[:, ACC + b, half * T:(half + 1) * T], zero[:, 0:P], zero[:, :],
                                      start=half == 0, stop=False, skip_group_check=True)
                return mm

            peel_last = chunk_no["n"] + pairs * (n_up + 1) == chunk_no["total"]
            up(lambda i: 0, 0)
            pe.do(open_accumulators, zeroed, acts)
            assert (pairs - 1) % slots == 0

            def body(j):
                for u in range(slots):
                    before = last("hidden")
                    up(lambda i, u=u: j(i) * slots + (u + 1), (u + 1) % slots)
                    chunk(down_src(lambda i, u=u: j(i) * slots + u), down_products(u), before)

            bodies((pairs - 1) // slots, body, peel_last)

            def last_products(m, n):
                def mm(e, i, s, hi, lo):
                    wh, wl = (w[:, :].rearrange("p (k n) -> p k n", k=2) for w in (hi, lo))
                    hs = (pairs - 1) % slots
                    for k in range(2):
                        xh, xl = (v[:, hs, k, m * P:(m + 1) * P] for v in (hidhi, hidlo))
                        for a, b in ((xh, wh), (xh, wl), (xl, wh)):
                            mm_ = e.matmul(ps[:, ACC + 2 * m + n, :], a, b[:, k, n * 512:(n + 1) * 512],
                                           start=False, stop=k == 1 and a is xl, skip_group_check=True)
                    return mm_
                return mm
            banks = [(m, n) for m in range(MT) for n in range(2)]
            done, _ = chunk(down_src(lambda i: pairs - 1), last_products(*banks[-1]), last("hidden"),
                            early=[last_products(*b) for b in banks[:-1]], hold=True)
            for (m, n), finished in zip(banks, [*early_done, done]):
                res.add(alpha, finished, ps[:, ACC + 2 * m + n, :], m, n)
            return res

        def swiglu(layer):
            w = A["ffn_w_gate_up"][layer]

            def up_src(t, q):
                def src(i, slot):
                    a = slot[:, :].rearrange("p (k g n) -> p g k n", k=KT, g=2)
                    return [(a[:, g, :, :], w.rearrange("(k p) n -> p k n", p=P)[
                        :, :, bass.ds(t(i) * 2 * P + (q * P + g * D_FF), P)]) for g in range(2)]
                return src

            def hidden(done, s, hs, q):
                silu = act.do(lambda e, i: e.activation(gate_sb[:, q, :], ps[:, s, 0:T], ACT.Silu),
                              done, last(f"gate {q} read"))
                prod = dve.do(lambda e, i: e.tensor_tensor(prod_sb[:, q, 0:T], ps[:, s, T:2 * T], gate_sb[:, q, :],
                                                           ALU.mult), silu, last(f"prod {q} read"))
                note(f"bank {s}", prod)
                note(f"gate {q} read", prod)
                hi = act.do(lambda e, i: e.activation(hidhi[:, hs, q, :], prod_sb[:, q, 0:T], ACT.Copy), prod)
                lo = dve.do(lambda e, i: e.tensor_tensor(hidlo[:, hs, q, :], prod_sb[:, q, 0:T],
                                                         f32(hidhi[:, hs, q, :]), ALU.subtract), hi)
                note(f"prod {q} read", lo)
                note("hidden", lo)

            def run(acts, res):
                return feed_forward(acts, up_src, 2, A["ffn_w_down"][layer], D_FF // (2 * P), 2, hidden, False, res)
            return run

        def squared_relu(layer):
            w = A["mlp_w1_2"][layer]

            def up_src(t, q):
                return columns(w, lambda i: t(i) * WIDE)

            def hidden(done, s, hs, q):
                relu = act.do(lambda e, i: e.activation(gate_sb[:, :, :], bank2(s), ACT.Relu), done, last("gate read"))
                note(f"bank {s}", relu)
                prod = prod_sb[:, 0, :].rearrange("p (a n) -> p a n", a=2)
                sq = dve.do(lambda e, i: e.tensor_tensor(prod, gate_sb[:, :, :], gate_sb[:, :, :], ALU.mult),
                            relu, last("prod read"))
                note("gate read", sq)
                hi = act.do(lambda e, i: e.activation(hidhi[:, hs, :, :], prod, ACT.Copy), sq)
                lo = dve.do(lambda e, i: e.tensor_tensor(hidlo[:, hs, :, :], prod, f32(hidhi[:, hs, :, :]),
                                                         ALU.subtract), hi)
                note("prod read", lo)
                note("hidden", lo)

            def run(acts, res):
                return feed_forward(acts, up_src, 1, A["mlp_w2_2"][layer], D_FF2 // (2 * P), 3, hidden, True, res)
            return run

        def layer_norm(res, g, b, columns_at=None):
            ln_sem = sem(f"ln_landed{len(ln_sems)}")
            ln_sems.append(ln_sem)
            for n, v in enumerate((g, b)):
                act.add(lambda e, i, n=n, v=v: e.dma_start(lnrow[:, n, :], v.rearrange("(a d) -> a d", a=1).to_broadcast([P, D])),
                        (latest.get("lnrow"),), (ln_sem, 16))
            landed = Mark(ln_sem, 32)
            mv = scratch(2 * MT)
            for m in range(MT):
                width = 6 * res.pieces
                ag = dve.do(lambda e, i, m=m: e.bn_aggr(mv[:, 2 * m:2 * m + 2], res.stats[:, m * width:(m + 1) * width]),
                            res.ready[m])
            rstd, r = rsqrt(ag, spread(mv[:, 1:], [2, MT]), 1, MT, LN_EPS)
            if columns_at is None:
                centred = [dve.do(lambda e, i, m=m: e.scalar_tensor_tensor(
                    out=x[:, m, :], in0=x[:, m, :], scalar=mv[:, 2 * m:2 * m + 1], in1=lnrow[:, 0, :], op0=ALU.subtract,
                    op1=ALU.mult), ag, landed) for m in range(MT)]
                return [dve.do(lambda e, i, m=m: e.scalar_tensor_tensor(
                    out=x[:, m, :], in0=x[:, m, :], scalar=rstd[:, m:m + 1], in1=lnrow[:, 1, :], op0=ALU.mult,
                    op1=ALU.add), centred[m], r) for m in range(MT)], None
            ready = [dve.do(lambda e, i, m=m: e.tensor_scalar(
                x[:, m, :], x[:, m, :], mv[:, 2 * m:2 * m + 1], rstd[:, m:m + 1], ALU.subtract, ALU.mult), r) for m in range(MT)]
            acts = to_features(ready, columns_at, x, columns_at + KT)
            ready = [turned[3]] * MT
            for m in range(MT):
                scaled = dve.do(lambda e, i, m=m: e.tensor_tensor(x[:, m, :], x[:, m, :], lnrow[:, 0, :], ALU.mult),
                                ready[m], landed)
                ready[m] = dve.do(lambda e, i, m=m: e.tensor_tensor(x[:, m, :], x[:, m, :], lnrow[:, 1, :], ALU.add), scaled)
            latest["lnrow"] = ready[-1]
            return ready, acts
        ln_sems = []

        qkv, _ = place("qkv", [P, MT, QKV2], offset=shared)
        q_t = (place("q_hi", [P, 8, T], F32R, offset=shared + 18432)[0], place("q_lo", [P, 8, T], F32R, offset=act_at)[0])
        k_t = (place("k_hi", [P, 6, T], F32R, offset=shared + 26624)[0],
               place("k_lo", [P, 6, T], F32R, offset=act_at + 8192)[0])
        bias, _ = place("bias", [P, 2, 4, T], offset=lnrow_at)
        bias_more, _ = place("bias_more", [P, 2, 4, T], offset=mixlo_at + 8192)
        probs, _ = place("probs", [P, 2, 4, T], offset=h_at)
        probs_ring = [probs[:, 0, :, :], probs[:, 1, :, :], place("probs_more", [P, 4, T], offset=hid_at)[0][:, :, :]]
        probs_t, _ = place("probs_t", [P, 2, 2, 4, P], offset=mixhi_at + 8192)
        SCALE = HD ** -0.5
        HEADS = (0, 2, 1, 3)

        def wide_project(w, width, acts, beside):
            def body(j):
                for u in range(3):
                    done, s = chunk(columns(w, lambda i, u=u: j(i) * 3 * WIDE + u * WIDE),
                                    token_major(acthi, actlo), acts)
                    note("qkv", note(f"bank {s}", act.do(lambda e, i, u=u, s=s: e.activation(
                        qkv[:, :, bass.ds(j(i) * 3 * WIDE + u * WIDE, WIDE)], bank2(s), ACT.Copy), done)))
                if chunk_no["loop"] is None:
                    beside(last("qkv"))
            bodies(width // (3 * WIDE), body)
            return last("qkv")

        def turn_heads(ready, n, sources, dest, b, gain=None):
            for f, source in enumerate(sources):
                for m in range(MT):
                    turned = pe.do(lambda e, i, f=f, m=m, source=source: e.transpose(
                        ps[:, b, f * T + m * P:f * T + (m + 1) * P], source(m), ident), *ready)
            k = len(sources)
            g = params[:, gain:gain + 1] if gain is not None else 1.0
            hi = act.do(lambda e, i: e.activation(dest[0][:, n:n + k, :], bank2(b)[:, 0:k, :], ACT.Copy, scale=g), turned)
            return dve.do(lambda e, i: e.scalar_tensor_tensor(
                out=dest[1][:, n:n + k, :], in0=bank2(b)[:, 0:k, :], scalar=g, in1=f32(dest[0][:, n:n + k, :]),
                op0=ALU.mult, op1=ALU.subtract), hi)

        def attend(banks_free, groups):
            N = len(groups)
            rows_of = [scratch(4 * 6) for _ in range(2)]
            scored, biased, exped, normed, turned, copied, mixed, split_ = ({} for _ in range(8))

            def score(n):
                if n >= N:
                    return
                g, b0, nk = groups[n], 2 * (n % 2), groups[n]["nk"] * P

                def mm(e, i):
                    for w, u in enumerate(HEADS):
                        base = (u % 2) * HD
                        for n_, (a, b) in enumerate(((0, 0), (0, 1), (1, 0))):
                            out = e.matmul(ps[:, b0 + w // 2, (w % 2) * T:(w % 2) * T + nk],
                                           q_t[a][base:base + HD, g["q"] + u // 2, g["m"] * P:(g["m"] + 1) * P],
                                           k_t[b][base:base + HD, g["k"](u), 0:nk], start=n_ == 0, stop=n_ == 2)
                    return out
                scored[n] = pe.do(mm, *g["ready"], *banks_free.get(n, ()), biased.get(n - 2))

            def weigh(n):
                if n >= N:
                    return
                g, par, nk = groups[n], n % 2, groups[n]["nk"] * P
                r = rows_of[par]
                neg, den, sunk, es = (r[:, 4 * k:4 * k + 4] for k in range(4))
                p4 = probs_ring[n % 3][:, :, 0:nk]
                s4 = ps[:, 2 * par:2 * par + 2, :].rearrange("p a (b n) -> p (a b) n", b=2)[:, :, 0:nk]
                biased[n] = dve.do(lambda e, i: e.scalar_tensor_tensor(out=p4, in0=s4, scalar=SCALE, in1=g["bias"],
                                                                       op0=ALU.mult, op1=ALU.add),
                                   scored[n], g["bias_ready"], turned.get(n - 3))
                top = dve.do(lambda e, i: e.tensor_reduce(neg, p4, AX, ALU.max), biased[n], exped.get(n - 2))
                if g["sink"] is None:
                    top = dve.do(lambda e, i: e.tensor_scalar(neg, neg, -1.0, None, ALU.mult), top)
                else:
                    sink, minus_sink = (spread(v, [1, 2], [2, 2]) for v in g["sink"])
                    neg4, sunk4 = (spread(v, [2, 2], [1, 2]) for v in (neg, sunk))
                    top = dve.do(lambda e, i: e.scalar_tensor_tensor(out=neg4, in0=neg4, scalar=-1.0, in1=minus_sink,
                                                                     op0=ALU.mult, op1=ALU.min), top, sinks_ready)
                    sunk_ = dve.do(lambda e, i: e.tensor_tensor(sunk4, sink, neg4, ALU.add), top)
                for u in range(4):
                    exped[n] = act.do(lambda e, i, u=u: e.activation(p4[:, u, :], p4[:, u, :], ACT.Exp,
                                                                     bias=neg[:, u:u + 1], accum_out=den[:, u:u + 1]), top,
                                      normed.get(n - 2))
                if g["sink"] is not None:
                    exped[n] = act.do(lambda e, i: e.activation(es, sunk, ACT.Exp), sunk_)

            def normalise(n):
                g, par, nk = groups[n], n % 2, groups[n]["nk"] * P
                r = rows_of[par]
                den, es, inv = r[:, 4:8], r[:, 12:16], r[:, 16:20]
                p4 = probs_ring[n % 3][:, :, 0:nk]
                ready_ = exped[n]
                if g["sink"] is not None:
                    ready_ = dve.do(lambda e, i: e.tensor_tensor(den, den, es, ALU.add), ready_)
                ready_ = dve.do(lambda e, i: e.reciprocal(inv, den), ready_)
                normed[n] = dve.do(lambda e, i: e.tensor_tensor(p4, p4, spread(inv, [1, 4], [0, nk]), ALU.mult), ready_)

            def turn(n):
                g, par = groups[n], n % 2

                def mm(e, i):
                    for kt in range(g["nk"]):
                        for u in range(4):
                            out = e.transpose(ps[:, 4 + kt, u * P:(u + 1) * P], probs_ring[n % 3][:, u, kt * P:(kt + 1) * P],
                                              ident)
                    return out
                turned[n] = pe.do(mm, normed[n], copied.get(n - 1))
                copied[n] = act.do(lambda e, i: e.activation(
                    probs_t[:, par, 0:g["nk"], :, :].rearrange("p k u n -> p k (u n)"), ps[:, 4:4 + g["nk"], :], ACT.Copy),
                    turned[n], mixed.get(n - 2))

            def mix(n):
                g, par = groups[n], n % 2

                def mm(e, i):
                    for w, u in enumerate(HEADS):
                        base = (u % 2) * HD
                        for kt in range(g["nk"]):
                            v = qkv[:, kt, g["v"](u):g["v"](u) + HD]
                            out = e.matmul(ps[base:base + HD, 6 + par, (u // 2) * P:(u // 2 + 1) * P], v,
                                           probs_t[:, par, kt, w, :], start=kt == 0, stop=kt == g["nk"] - 1)
                    return out
                mixed[n] = pe.do(mm, copied[n], split_.get(n - 2))
                src = ps[:, 6 + par, 0:2 * P].rearrange("p (a n) -> p a n", a=2)
                tiles, tokens = slice(g["out"], g["out"] + 2), slice(g["m"] * P, (g["m"] + 1) * P)
                hi[n] = act.do(lambda e, i: e.activation(mixhi[:, tiles, tokens], src, ACT.Copy), mixed[n])

            def rest(n):
                g, par = groups[n], n % 2
                src = ps[:, 6 + par, 0:2 * P].rearrange("p (a n) -> p a n", a=2)
                tiles, tokens = slice(g["out"], g["out"] + 2), slice(g["m"] * P, (g["m"] + 1) * P)
                split_[n] = dve.do(lambda e, i: e.tensor_tensor(mixlo[:, tiles, tokens], src,
                                                                f32(mixhi[:, tiles, tokens]), ALU.subtract), hi[n])
            hi = {}
            score(0)
            score(1)
            weigh(0)
            for n in range(N):
                if "bias_make" in groups[min(n + 1, N - 1)] and n + 1 < N:
                    groups[n + 1]["bias_make"](biased.get(n - 1))
                weigh(n + 1)
                normalise(n)
                score(n + 2)
                turn(n)
                if n:
                    mix(n - 1)
                if n > 1:
                    rest(n - 2)
            mix(N - 1)
            rest(N - 2)
            rest(N - 1)
            pair_ready.extend(split_[max(n for n in range(N) if groups[n]["out"] == 2 * p)] for p in range(4))
            latest["lnrow"] = split_[N - 1]
            return split_[N - 1]

        def swa_layer(acts):
            sinks_ready.mark = pool.do(lambda e, i: e.tensor_scalar(negated, rows[:, 0:24], -1.0, None, ALU.mult), rows_in)
            w = A["attn_w_qkv"][0]
            copied = {}

            def norm_heads(first, n, is_key=False):
                total = scratch(MT * n)
                v = qkv[:, :, first * HD:(first + n) * HD]
                sq_buf = h[:, :, 0:n * HD]
                sq = act.do(lambda e, i: e.activation(sq_buf, v, ACT.Square), copied[(first + n - 1) // 4], latest.get("squares read"))
                summed = note("squares read", dve.do(lambda e, i: e.tensor_reduce(
                    spread(total, [n, MT], [1, n]), spread(h[:, 0, :], [D, MT], [HD, n], [1, HD]), AX, ALU.add), sq))
                r, r_ready = rsqrt(summed, total, HD, MT * n, EPS)
                for m in range(MT):
                    if is_key:
                        out, src, r_ = (spread(qkv[:, m, QKV1:], [2 * HD, n], [HD, 2], [1, HD]),
                                        spread(qkv[:, m, first * HD:], [HD, n], [0, 2], [1, HD]),
                                        spread(r[:, n * m:], [1, n], [0, 2], [0, HD]))
                    else:
                        out = src = spread(qkv[:, m, first * HD:], [HD, n], [1, HD])
                        r_ = spread(r[:, n * m:], [1, n], [0, HD])
                    normed = dve.do(lambda e, i, out=out, src=src, r_=r_: e.tensor_tensor(out, src, r_, ALU.mult), r_ready)
                return normed

            normed = {}
            for n in range(QKV1 // WIDE):
                done, s = chunk(columns(w, lambda i, n=n: n * WIDE), token_major(acthi, actlo), acts)
                copied[n] = note("qkv", note(f"bank {s}", act.do(lambda e, i, n=n, s=s: e.activation(
                    qkv[:, :, n * WIDE:(n + 1) * WIDE], bank2(s), ACT.Copy), done)))
                if n < 4:
                    normed[n] = norm_heads(4 * n, 4)
                elif n == 4:
                    key_normed = norm_heads(16, 4, True)
            q_cols = lambda p: lambda m: qkv[:, m, p * P:(p + 1) * P]
            k_cols = lambda g: lambda m: qkv[:, m, QKV1 + g * P:QKV1 + (g + 1) * P]
            ready = (key_normed, copied[5])
            turn = lambda n, *args: turn_heads(ready, n, *args)
            q_ready = [turn(0, [q_cols(0), q_cols(1)], q_t, 6, PAR["q_gain"])]
            k_ready = [turn(2 * n, [k_cols(2 * n), k_cols(2 * n + 1)], k_t, 4 + n, PAR["k_gain"]) for n in range(2)]
            q_ready += [turn(2 * n, [q_cols(2 * n), q_cols(2 * n + 1)], q_t, b, PAR["q_gain"]) for n, b in ((1, 7), (2, 2), (3, 3))]
            groups = []
            for m in range(MT):
                for g in range(4):
                    n = len(groups)
                    nk = m + 1
                    sink = rows[:, ROW["sinks1"] + 4 * g:ROW["sinks1"] + 4 * g + 4]
                    msink = negated[:, ROW["sinks1"] + 4 * g:ROW["sinks1"] + 4 * g + 4]

                    def make(free, n=n, m=m, g=g, nk=nk):
                        for w, u in enumerate(HEADS):
                            slope = float(np.exp2(np.float32(-8.0 * (4 * g + u + 1) / 16)))
                            groups[n]["bias_ready"] = pool.do(lambda e, i, w=w, slope=slope: e.tensor_scalar(
                                bias[:, n % 2, w, 0:nk * P], table[:, TAB["dist"] + m * T:TAB["dist"] + m * T + nk * P],
                                -slope, None, ALU.mult), table_in, free)
                    groups.append(dict(m=m, nk=nk, ready=(q_ready[g], k_ready[g // 2]), q=2 * g, k=lambda u, g=g: g, v=lambda u, g=g: D + 256 + g * HD,
                                       out=2 * g, sink=(sink, msink), bias=bias[:, n % 2, :, 0:nk * P], bias_make=make))
            groups[0]["bias_make"](None)
            return attend({1: q_ready[2:]}, groups)

        negated = scratch(24)
        sinks_ready = Later()

        rpb_sem = sem("rpb_landed")

        def rpb_tile(m, g):
            return (bias, bias_more)[m][:, g, :, :]

        def load_rpb(free):
            rpb = A["rpb"]
            (sh, _), (sr, _), _ = rpb.ap
            for m in range(MT):
                for head in range(8):
                    for rr in range(2):
                        off = head * sh + (7 - 2 * m - rr) * sr
                        src = bass.AP(rpb.tensor, off, [[1, 64], [sr, 4], [1, 64]])
                        dst = rpb_tile(m, head // 4)[64 * rr:64 * rr + 64, HEADS.index(head % 4), :].rearrange("p (a n) -> p a n", a=4)
                        pool.add(lambda e, i, dst=dst, src=src: e.dma_start(dst, src), (free,), (rpb_sem, 16))
            return Mark(rpb_sem, 16 * 32)

        biases = {}

        def flip_rpb(m, landed):
            for g in range(2):
                tile = rpb_tile(m, g).rearrange("p u n -> p (u n)")

                def mm(e, i, g=g, tile=tile):
                    for n in range(2):
                        out = e.matmul(ps[:, 2 * g + n, :], table[:, TAB["flip"]:TAB["flip"] + P],
                                       tile[:, 512 * n:512 * n + 512], start=True, stop=True)
                    return out
                flipped = pe.do(mm, landed, biases.get((m - 1, g)))
                near = spread(table[:, TAB["near"] + m * T:], [0, 4], [1, T])
                biases[m, g] = dve.do(lambda e, i, m=m, g=g, near=near: e.tensor_tensor(
                    rpb_tile(m, g), ps[:, 2 * g:2 * g + 2, :].rearrange("p a (b n) -> p (a b) n", b=2), near, ALU.add), flipped)
            for b in range(SLOTS):
                note(f"bank {b}", biases[m, 1])

        def na_layer(acts):
            half = HD // 2
            roped = []

            def rope(ready):
                for m in range(MT):
                    v = qkv[:, m, :]
                    first, second = spread(v, [HD, 10], [1, half]), spread(v[:, half:], [HD, 10], [1, half])
                    both = spread(v, [HD, 10], [1, HD])
                    cos = spread(table[:, TAB["cos"] + m * HD:], [0, 10], [1, HD])
                    minus_sin = spread(table[:, TAB["sin"] + m * HD:], [0, 10], [1, half])
                    plus_sin = spread(table[:, TAB["sin"] + m * HD + half:], [0, 10], [1, half])
                    rot = probs[:, m, 0:3, :].rearrange("p a n -> p (a n)")
                    rot_1, rot_2, rot_all = spread(rot, [HD, 10], [1, half]), spread(rot[:, half:], [HD, 10], [1, half]), \
                        spread(rot, [HD, 10], [1, HD])
                    a = dve.do(lambda e, i, o=rot_1, x_=second, s_=minus_sin: e.tensor_tensor(o, x_, s_, ALU.mult), ready, table_in)
                    b = dve.do(lambda e, i, o=rot_2, x_=first, s_=plus_sin: e.tensor_tensor(o, x_, s_, ALU.mult), ready)
                    c = dve.do(lambda e, i, o=both, s_=cos: e.tensor_tensor(o, o, s_, ALU.mult), a, b)
                    dve.do(lambda e, i, m=m, rot=rot, v=v: e.tensor_tensor(
                        spread(probs[:, m, 3, :], [2 * HD, 2], [HD, 2], [1, HD]), spread(v[:, 512:], [HD, 2], [0, 2], [1, HD]),
                        spread(rot[:, 512:], [HD, 2], [0, 2], [1, HD]), ALU.add), c)
                    roped.append(dve.do(lambda e, i, v=v, rot=rot: e.tensor_tensor(v[:, 0:512], v[:, 0:512], rot[:, 0:512],
                                                                                   ALU.add), c))
            ready = wide_project(A["attn_w_in_2"][0], QKV2, acts, rope)
            cols = lambda c0: lambda m: qkv[:, m, c0:c0 + P]
            twice = lambda g: lambda m: probs[:, m, 3, g * P:(g + 1) * P]
            turn = lambda n, *args: turn_heads((*roped, ready), n, *args)
            q_ready = [turn(0, [cols(0), cols(P)], q_t, 7)]
            k_ready = [turn(0, [twice(0), twice(1)], k_t, 4)]
            q_ready += [turn(2, [cols(2 * P), cols(3 * P)], q_t, 0)]
            k_ready += [turn(2 * n, [cols(1280 + 2 * (n - 1) * P), cols(1280 + (2 * n - 1) * P)], k_t, 4 + n) for n in (1, 2)]
            q_ready += [turn(4 + 2 * n, [cols(768 + 2 * n * P), cols(768 + (2 * n + 1) * P)], q_t, 2 + n) for n in range(2)]
            groups = []
            for m in range(MT):
                window = spread(table[:, TAB["window"] + m * T:], [0, 4], [1, T])
                for g in range(2):
                    c = ROW["sinks2"] + 4 * g
                    groups.append(dict(m=m, nk=2, ready=(q_ready[g], k_ready[0]), q=2 * g, k=lambda u, g=g: g, v=lambda u, g=g: 640 + g * HD, out=2 * g,
                                       sink=(rows[:, c:c + 4], negated[:, c:c + 4]), bias=window, bias_ready=table_in))
                for g in range(2):
                    groups.append(dict(m=m, nk=2, ready=(q_ready[2 + g], k_ready[1 + g]), q=4 + 2 * g, k=lambda u, g=g: 2 + 2 * g + u // 2,
                                       v=lambda u, g=g: 1792 + (4 * g + u) * HD, out=4 + 2 * g, sink=None,
                                       bias=rpb_tile(m, g), bias_ready=biases[m, g]))
            return attend({0: (q_ready[1],), 1: q_ready[2:]}, groups)

        y, _ = place("ssm_y", [P, MT, SSM_INNER], offset=shared)
        z, _ = place("z", [P, 2, MT, 4 * P], offset=shared + 16384)
        ssm_small, _ = place("ssm_small", [P, 5, 128], offset=shared + 24576)
        bc_t, _ = place("bc_t", [P, 4, T], offset=mixhi_at)
        xs_t, _ = place("xs_t", [P, 2, 4, T], offset=mixhi_at + 4096)
        gram_f, _ = place("gram_f", [P, 2, MT, P], offset=mixhi_at + 12288)
        gram_b, _ = place("gram_b", [P, 2, MT, P], offset=mixhi_at + 14336)
        xs, _ = place("xs", [P, 2, MT, 4 * P], offset=mixlo_at)
        gram_x, _ = place("gram_x", [P, 2, MT, P], offset=mixlo_at + 8192)
        xdec, _ = place("xdec", [P, 2, 4, HD], offset=mixlo_at + 10240)
        skipped, _ = place("skipped", [P, 2, 4, HD], offset=mixlo_at + 12288)
        carried, _ = place("carried", [P, 2, 4, HD], offset=mixlo_at + 14336)
        taps, _ = place("ssm_taps", [P, 2, 2, T], offset=hid_at)
        window, _ = place("ssm_window", [P, 2, 2, T + 4], offset=hid_at + 4096)
        cum = [[place(f"cum_{d}{n}", [P, 4, P], F32R, offset=lnrow_at + 4096 * d + 2048 * n)[0] for n in range(2)]
               for d in range(2)]
        decay, _ = place("decay", [P, 2, 4, P], offset=h_at)
        weight, _ = place("weight", [P, 2, 4, P], offset=h_at + 4096)
        rounding, _ = place("rounding", [P, 128], F32R, offset=h_at + 4096)

        def ssm_layer(acts, res):
            w_in = A["ssm_w_in_2"][0]
            le, ge, gt, lt = (table[:, TAB[n]:TAB[n] + P] for n in ("le", "ge", "gt", "lt"))
            def dt_products(e, i, s, hi, lo, ks=None):
                whi_, wlo_ = (w[:, :].rearrange("p (k n) -> p k n", k=KT)[:, :, P:2 * P] for w in (hi, lo))
                for k in ks or range(KT):
                    for q, (w_, a_) in enumerate(((whi_, acthi), (whi_, actlo), (wlo_, acthi))):
                        out = e.matmul(ps[:, s, 0:T], w_[:, k, :], a_[:, k, :], start=k == q == 0, stop=k == KT - 1 and q == 2,
                                       skip_group_check=True)
                return out
            done, s = chunk(columns(w_in, lambda i: SSM_IN - WIDE), dt_products, acts)
            v, (dt, a, a_hi, a_lo, edge) = h[:, 0, 512:640], (ssm_small[:, n, :] for n in range(5))
            two = lambda ap: spread(ap, [64, 2], [1, 64])
            over_m = lambda ap: spread(ap, [0, 2], [1, 64])
            dt_t = h[:, 0, 768:768 + T]
            copied = act.do(lambda e, i: e.activation(dt_t, ps[:, s, 0:T], ACT.Copy), done)

            def turn_dt(e, i):
                for m in range(MT):
                    out = e.transpose(ps[:, s, T + m * P:T + (m + 1) * P], dt_t[:, m * P:(m + 1) * P], ident)
                return out

            def finish_dt():
                turned_dt = pe.do(turn_dt, copied)
                return note(f"bank {s}", dve.do(lambda e, i: e.tensor_tensor(
                    two(v), spread(ps[:, s, T + 64:], [P, 2], [1, 64]), over_m(rows[:, ROW["dt_bias"]:]), ALU.add),
                    turned_dt, rows_in))

            def make_dt():
                m_ = finish_dt()
                e_, u_, ln_, same = (h[:, 0, 128 * n:128 * n + 128] for n in range(4))
                m_ = dve.do(lambda e, i: e.scalar_tensor_tensor(out=e_, in0=v, scalar=-1.0, in1=v, op0=ALU.mult, op1=ALU.min), m_)
                exp_ = act.do(lambda e, i: e.activation(e_, e_, ACT.Exp), m_)
                m_ = dve.do(lambda e, i: e.tensor_scalar(u_, e_, 1.0, None, ALU.add), exp_)
                log = act.do(lambda e, i: e.activation(ln_, u_, ACT.Ln), m_)
                m_ = dve.do(lambda e, i: e.tensor_scalar(same, u_, 1.0, None, ALU.is_equal), m_)
                m_ = dve.do(lambda e, i: e.scalar_tensor_tensor(out=u_, in0=u_, scalar=-1.0, in1=same, op0=ALU.add, op1=ALU.add), m_, log)
                m_ = dve.do(lambda e, i: e.reciprocal(u_, u_), m_)
                m_ = dve.do(lambda e, i: e.tensor_tensor(u_, u_, ln_, ALU.mult), m_)
                m_ = dve.do(lambda e, i: e.tensor_tensor(u_, u_, same, ALU.add), m_)
                m_ = dve.do(lambda e, i: e.tensor_tensor(u_, u_, e_, ALU.mult), m_)
                dt_ready = dve.do(lambda e, i: e.scalar_tensor_tensor(out=dt, in0=v, scalar=0.0, in1=u_, op0=ALU.max, op1=ALU.add), m_)
                rate = scratch(64)
                rated = act.do(lambda e, i: e.activation(rate, rows[:, ROW["a_log"]:ROW["a_log"] + 64], ACT.Exp), rows_in)
                a_ready = dve.do(lambda e, i: e.scalar_tensor_tensor(out=two(a), in0=two(dt), scalar=-1.0, in1=over_m(rate),
                                                                     op0=ALU.mult, op1=ALU.mult), dt_ready, rated)

                act.do(lambda e, i: e.activation(strict[:, 0, :], gt, ACT.Copy), table_in)
                strict_ready = act.do(lambda e, i: e.activation(strict[:, 1, :], lt, ACT.Copy))
                hi = act.do(lambda e, i: e.activation(rounding[:, :], a, ACT.Copy), a_ready)
                dve.do(lambda e, i: e.tensor_copy(a_hi, f32(rounding[:, :])), hi)
                a_split = dve.do(lambda e, i: e.tensor_tensor(a_lo, a, f32(rounding[:, :]), ALU.subtract))
                return dt_ready, a_ready, a_split, strict_ready

            edges = pool.do(lambda e, i: e.memset(window[:, :, :, :], 0.0), acts)
            conved, gated, xs_ready, xs_turned = {}, {}, {}, {}
            ring = [0]

            later = []

            def run_later():
                for op in later:
                    op()
                later.clear()

            def conv_chunk(key, first_tile, dest, free):
                q = ring[0] % 2
                ring[0] += 1
                done, s = chunk(columns(w_in, lambda i: SSM_INNER + first_tile * P), feature_major(acthi, actlo), acts)
                seen = act.do(lambda e, i: e.activation(window[:, q, :, 2:T + 2], bank2(s), ACT.Copy),
                              done, edges, latest.get(f"window {q} read"))
                w = lambda tap, f: params[:, PAR["ssm_conv_w"] + tap * 32 + first_tile + f:][:, 0:1]
                for f in range(2):
                    t = act.do(lambda e, i, f=f: e.activation(taps[:, q, f, :], ps[:, s, f * T:(f + 1) * T], ACT.Copy,
                                                              scale=w(2, f)), latest.get(f"taps {q} read"), params_in)
                note(f"bank {s}", t)
                for tap in (0, 1, 3, 4):
                    prior = t
                    for f in range(2):
                        t = dve.do(lambda e, i, f=f, tap=tap: e.scalar_tensor_tensor(
                            out=taps[:, q, f, :], in0=window[:, q, f, tap:tap + T], scalar=w(tap, f),
                            in1=taps[:, q, f, :], op0=ALU.mult, op1=ALU.add), prior, seen)
                note(f"window {q} read", t)

                def silu():
                    for f in range(2):
                        t2 = act.do(lambda e, i, f=f: e.activation(
                            dest[:, f, :], taps[:, q, f, :], ACT.Silu,
                            bias=params[:, PAR["ssm_conv_b"] + first_tile + f:][:, 0:1]), t, *free())
                    conved[key] = note(f"taps {q} read", t2)
                later.append(silu)

            def z_chunk(n):
                done, s = chunk(columns(w_in, lambda i: n * WIDE), token_major(acthi, actlo), acts)
                gated[n] = note(f"bank {s}", act.do(lambda e, i: e.activation(
                    z[:, n // 2 % 2, :, n % 2 * WIDE:(n % 2 + 1) * WIDE], bank2(s), ACT.Silu), done,
                    gated_read.get((n - 4, 1))))
            gated_read = {}

            def turn_xs(G):
                for m in range(MT):
                    for t in range(4):
                        turned = pe.do(lambda e, i, m=m, t=t: e.transpose(
                            ps[:, 5, t * P:(t + 1) * P], xs_t[:, G % 2, t, m * P:(m + 1) * P], ident),
                            conved[G, 0], conved[G, 1], latest.get("turn bank"))
                    xs_ready[G] = note("turn bank", act.do(lambda e, i, m=m: e.activation(
                        xs[:, G % 2, m, :], ps[:, 5, :], ACT.Copy), turned, skip_made.get(4 * G - 5), multiplied_.get(4 * G - 5)))
                xs_turned[G] = turned

            part = lambda ap, m, d: ap[:, 64 * m + 32 * d:64 * m + 32 * d + 32]
            sums = ((le, 1, 0), (gt, 0, 0), (ge, 0, 1), (lt, 1, 1))

            def make_edge():
                def border(e, i):
                    for n, (mask, m, d) in enumerate(sums):
                        out = e.matmul(ps[:, TOP, 32 * n:32 * n + 32], mask, part(a, m, d), start=True, stop=True)
                    return out
                summed = pe.do(border, a_ready, table_in)
                edged = act.do(lambda e, i: e.activation(edge, ps[:, TOP, 0:128], ACT.Exp), summed)
                out_f = dve.do(lambda e, i: e.tensor_tensor(edge[:, 32:64], edge[:, 32:64], part(dt, 0, 0), ALU.mult), edged)
                out_b = dve.do(lambda e, i: e.tensor_tensor(edge[:, 96:128], edge[:, 96:128], part(dt, 1, 1), ALU.mult), edged)
                return edged, out_f, out_b

            gram, gram_masked, summed_to, exped, made, multiplied_, crossed, summed_y, squared = ({} for _ in range(9))
            summed_over, xd, skip_made = {}, {}, {}
            totals = scratch(16)

            def make_gram(g):
                q = g % 2

                def mm(e, i):
                    for m in range(MT):
                        out = e.matmul(ps[:, TOP, m * T:(m + 1) * T], bc_t[:, q, m * P:(m + 1) * P], bc_t[:, 2 + q, :],
                                       start=True, stop=True)
                    return out
                gram[g] = pe.do(mm, conved[g // 2, 2], conved[g // 2, 3], gram_masked.get(g - 1, edged))
                diag = spread(ps[:, TOP, :], [T + P, 2], [1, P])
                dve.do(lambda e, i: e.tensor_tensor(gram_f[:, q, :, :], diag, spread(le, [0, 2], [1, P]), ALU.mult),
                       gram[g], made.get((g - 2, 1)), crossed.get((g - 2, 1)))
                dve.do(lambda e, i: e.tensor_tensor(gram_b[:, q, :, :], diag, spread(ge, [0, 2], [1, P]), ALU.mult))
                gram_masked[g] = dve.do(lambda e, i: e.tensor_copy(
                    gram_x[:, q, :, :].rearrange("p a n -> p (a n)"), ps[:, TOP, P:3 * P]))

            items = [(g, m) for g in range(SSM_GROUPS) for m in range(MT)]

            def head_cols(ap, m, d, g):
                return part(ap, m, d)[:, 4 * g:4 * g + 4]

            def group_cols(ring_, g, m):
                return spread(ring_[:, g // 2 % 2, m, 4 * HD * (g % 2):], [HD, 4], [1, HD])

            def prepare(n):
                if n >= len(items):
                    return
                g, m = items[n]
                par = n % 2
                for mask, d in ((le, 0), (ge, 1)):
                    for k, v in enumerate((a_hi, a_lo)):
                        summed_over[n] = pool.do(lambda e, i, mask=mask, d=d, k=k, v=v: e.tensor_tensor(
                            cum[d][k][:, :, :], spread(mask, [0, 4], [1, P]), spread(head_cols(v, m, d, g), [1, 4], [0, P]),
                            ALU.mult), a_split, summed_to.get(n - 1), acts)
                src, c = (0, 32) if m == 1 else (1, 96)
                xd[n] = pool.do(lambda e, i: e.tensor_tensor(
                    xdec[:, par, :, :], group_cols(xs, g, src), spread(edge[:, c + 4 * g:], [1, 4], [0, HD]), ALU.mult),
                    out_f, out_b, xs_ready[g // 2], crossed.get(items[n - 2] if n >= 2 else None))
                skip_made[n] = pool.do(lambda e, i: e.tensor_tensor(
                    skipped[:, par, :, :], group_cols(xs, g, m), spread(rows[:, ROW["skip"] + 4 * g:], [1, 4], [0, HD]),
                    ALU.mult), rows_in, summed_y.get(n - 2))

            def decays(n):
                g, m = items[n]
                par, gp = n % 2, g % 2

                def mm(e, i):
                    for d in range(2):
                        for k in range(2):
                            out = e.matmul(ps[:, 4, :], strict[:, d, :], cum[d][k][:, :, :].rearrange("p u n -> p (u n)"),
                                           start=d == k == 0, stop=d == k == 1)
                    return out
                summed_to[n] = pe.do(mm, summed_over[n], exped.get(n - 1), strict_ready)
                for u in range(4):
                    t = act.do(lambda e, i, u=u: e.activation(weight[:, par, u, :], gram_f[:, gp, m, :], ACT.Copy,
                                                              scale=head_cols(dt, m, 0, g)[:, u:u + 1]),
                               gram_masked[g], dt_ready, multiplied_.get(n - 2))
                exped[n] = act.do(lambda e, i: e.activation(decay[:, par, :, :].rearrange("p u n -> p (u n)"), ps[:, 4, :],
                                                            ACT.Exp), summed_to[n], made.get(items[n - 2] if n >= 2 else None))
                for u in range(4):
                    t2 = dve.do(lambda e, i, u=u: e.scalar_tensor_tensor(
                        out=weight[:, par, u, :], in0=gram_b[:, gp, m, :], scalar=head_cols(dt, m, 1, g)[:, u:u + 1],
                        in1=weight[:, par, u, :], op0=ALU.mult, op1=ALU.add), t)
                made[g, m] = dve.do(lambda e, i: e.tensor_tensor(weight[:, par, :, :], weight[:, par, :, :], decay[:, par, :, :],
                                                                 ALU.mult), t2, exped[n])

            def outputs(n):
                g, m = items[n]
                par = n % 2
                bank = 6 + par

                def inner(e, i):
                    for u in range(4):
                        out = e.matmul(ps[:, bank, u * HD:(u + 1) * HD], weight[:, par, u, :],
                                       xs[:, g // 2 % 2, m, (4 * (g % 2) + u) * HD:(4 * (g % 2) + u + 1) * HD],
                                       start=True, stop=True)
                    return out

                def cross(e, i):
                    return e.matmul(ps[:, bank, 4 * HD:8 * HD], gram_x[:, g % 2, 1 - m, :],
                                    xdec[:, par, :, :].rearrange("p u n -> p (u n)"), start=True, stop=True)
                crossed[g, m] = pe.do(cross, xd[n], gram_masked[g], summed_y.get(n - 2))
                multiplied_[n] = pe.do(inner, made[g, m], xs_ready[g // 2])
                c = 0 if m == 1 else 64
                yv = spread(y[:, m, 4 * HD * g:], [HD, 4], [1, HD])
                half = lambda k: spread(ps[:, bank, 4 * HD * k:], [HD, 4], [1, HD])
                t = dve.do(lambda e, i: e.tensor_tensor(carried[:, par, :, :], half(1),
                                                        spread(edge[:, c + 4 * g:], [1, 4], [0, HD]), ALU.mult),
                           multiplied_[n], edged, squared.get(n - 2))
                t = dve.do(lambda e, i: e.tensor_tensor(carried[:, par, :, :], carried[:, par, :, :], skipped[:, par, :, :],
                                                        ALU.add), t, skip_made[n])
                summed_y[n] = dve.do(lambda e, i: e.tensor_tensor(carried[:, par, :, :], half(0),
                                                                  carried[:, par, :, :], ALU.add), t)
                t = gated_read[g, m] = pool.do(lambda e, i: e.tensor_tensor(
                    yv, carried[:, par, :, :], group_cols(z, g, m), ALU.mult), summed_y[n], gated[g], acts)

                def square():
                    squared[n] = act.do(lambda e, i: e.activation(
                        carried[:, par, :, :].rearrange("p u n -> p (u n)"), y[:, m, 4 * HD * g:4 * HD * (g + 1)],
                        ACT.Square, accum_out=totals[:, 2 * g + m:2 * g + m + 1]), t)
                later.append(square)

            scaled = {}

            def norm_pair(G):
                r, r_ready = rsqrt(squared[4 * G + 3], totals[:, 4 * G:4 * G + 4], 4 * HD, 4, 1e-5)
                for m in range(MT):
                    v = spread(y[:, m, 8 * HD * G:], [4 * HD, 2], [1, 4 * HD])
                    scaled[G] = pool.do(lambda e, i, v=v, m=m: e.tensor_tensor(
                        v, v, spread(r[:, m:], [2, 2], [0, 4 * HD]), ALU.mult), r_ready)

            def turn_y(half, hi_part, lo_part, banks, low, *waits):
                for k in range(KT):
                    b = banks[k % 4]
                    for m in range(MT):
                        turned = pe.do(lambda e, i, b=b, m=m, k=k: e.transpose(
                            ps[:, b, m * P:(m + 1) * P], y[:, m, (KT * half + k) * P:(KT * half + k + 1) * P], ident),
                            scaled[2 * half + 1], low.get(k - 4), *waits)
                    g_ = params[:, PAR["ssm_norm"] + KT * half + k:][:, 0:1]
                    hi = act.do(lambda e, i, b=b, k=k, g_=g_: e.activation(hi_part[:, k, :], ps[:, b, 0:T], ACT.Copy, scale=g_),
                                turned)
                    low[k] = dve.do(lambda e, i, b=b, k=k, g_=g_: e.scalar_tensor_tensor(
                        out=lo_part[:, k, :], in0=ps[:, b, 0:T], scalar=g_, in1=f32(hi_part[:, k, :]), op0=ALU.mult,
                        op1=ALU.subtract), hi)
                return low[KT - 1]

            w_out = A["ssm_w_out_2"][0]

            def out_chunk(half, n, hi_part, lo_part, ready, hold=False):
                def src(i, slot):
                    a_ = slot[:, :].rearrange("p (k n) -> p k n", k=KT)
                    b_ = w_out.rearrange("(k p) n -> p k n", p=P)[:, KT * half:KT * (half + 1), n * WIDE:(n + 1) * WIDE]
                    return [(a_[:, 0:4, :], b_[:, 0:4, :]), (a_[:, 4:8, :], b_[:, 4:8, :])]

                def mm(e, i, s, hi, lo):
                    wh, wl = (w[:, :].rearrange("p (k n) -> p k n", k=KT) for w in (hi, lo))
                    for m in range(MT):
                        for k in range(KT):
                            xh, xl = (v[:, k, m * P:(m + 1) * P] for v in (hi_part, lo_part))
                            for q, (p_, w_) in enumerate(((xh, wh), (xh, wl), (xl, wh))):
                                out = e.matmul(ps[:, out_banks[n], m * T:(m + 1) * T], p_, w_[:, k, :],
                                               start=half == m == k == q == 0,
                                               stop=half == 1 and k == KT - 1 and q == 2, skip_group_check=True)
                    return out
                return chunk(src, mm, ready, hold=hold)[0]
            out_banks = (0, 1, 2, 5)

            for G in range(4):
                steps = [lambda: conv_chunk((G, 0), 4 * G, xs_t[:, G % 2, 0:2, :], lambda: (xs_turned.get(G - 2),)),
                         lambda: conv_chunk((G, 1), 4 * G + 2, xs_t[:, G % 2, 2:4, :], lambda: ()),
                         lambda: z_chunk(2 * G),
                         lambda: conv_chunk((G, 2), 16 + 2 * G, bc_t[:, 0:2, :], lambda: (gram.get(2 * G - 1),)),
                         lambda: conv_chunk((G, 3), 24 + 2 * G, bc_t[:, 2:4, :], lambda: (gram.get(2 * G - 1),)),
                         lambda: z_chunk(2 * G + 1)]
                first = 4 * (G - 1)
                for k in range(6):
                    n = first + {1: 0, 2: 1, 4: 2, 5: 3}[k] if G > 0 and k in (1, 2, 4, 5) else None
                    if n is not None:
                        decays(n)
                        prepare(n + 1)
                    if k in (0, 3) and G > 0:
                        make_gram(2 * G - 2 + k // 3)
                    if k == 3 and G > 1:
                        norm_pair(G - 2)
                    former = list(later)
                    later.clear()
                    steps[k]()
                    for op in former:
                        op()
                    if k == 0 and G == 0:
                        dt_ready, a_ready, a_split, strict_ready = make_dt()
                    if n is not None:
                        outputs(n)
                    if k == 3:
                        turn_xs(G)
                        if G == 0:
                            edged, out_f, out_b = make_edge()
                            prepare(0)
            z_read = gated[7]
            run_later()
            make_gram(6)
            for k in range(4):
                decays(12 + k)
                prepare(12 + k + 1)
                if k == 0:
                    norm_pair(2)
                    first_half = turn_y(0, acthi, actlo, out_banks, {}, z_read, xs_ready[3])
                    make_gram(7)
                else:
                    out_chunk(0, k - 1, acthi, actlo, first_half)
                run_later()
                outputs(12 + k)
            out_chunk(0, 3, acthi, actlo, first_half)
            run_later()
            norm_pair(3)
            latest["lnrow"] = summed_to[15]
            second_half = turn_y(1, mixhi, mixlo, (TOP, 4, 6, 7), {})
            for n in range(4):
                done = out_chunk(1, n, mixhi, mixlo, second_half, n == 3)
                for m in range(MT):
                    added = res.add(True, done, bank2(out_banks[n])[:, m, :], m, n)
                if n < SLOTS:
                    note(f"bank {n}", added)
            return res

        def network():
            res = Residual("rms", 1)
            keep_warm(24)
            for m in range(MT):
                res.take(m, 0, x_in[m])
            split_chunk(0, hold=True)
            acts = rms_norm(res, PAR["norm_mixer0"])
            for c in range(1, LEAD):
                split_chunk(c)
            load_later_constants(acts)
            mixed = conv_layer(acts)
            res = project(A["conv_w_out"][0], mixhi, mixlo, mixed, False, Residual("rms", 4))
            yield res.ready
            res = swiglu(0)(rms_norm(res, PAR["norm_ffn0"]), Residual("rms", 2))
            yield res.ready
            mixed = swa_layer(rms_norm(res, PAR["norm_mixer1"]))
            res = project(A["attn_w_o"][0], mixhi, mixlo, mixed, False, Residual("rms", 4))
            yield res.ready
            acts = rms_norm(res, PAR["norm_ffn1"])
            landed = load_rpb(mixed)
            res = swiglu(1)(acts, Residual(None, 2))
            yield res.ready
            for m in range(MT):
                flip_rpb(m, landed)
            acts = to_features(res.ready, rows_=x)
            mixed = na_layer(acts)
            res = project(A["attn_w_out_2"][0], mixhi, mixlo, mixed, True, Residual("ln", 4))
            ready, acts = layer_norm(res, A["ln1_g_2"][0], A["ln1_b_2"][0], PAR["ln1_0"])
            yield ready
            res = squared_relu(0)(acts, Residual("ln", 2))
            ready, acts = layer_norm(res, A["ln2_g_2"][0], A["ln2_b_2"][0], PAR["ln2_0"])
            yield ready
            res = ssm_layer(acts, Residual("ln", 4))
            ready, acts = layer_norm(res, A["ln1_g_2"][1], A["ln1_b_2"][1], PAR["ln1_1"])
            yield ready
            res = squared_relu(1)(acts, Residual("ln", 2))
            yield layer_norm(res, A["ln2_g_2"][1], A["ln2_b_2"][1])[0]

        for n, ready in enumerate(network()):
            if n == stop_after:
                break
        out_landed = sem("out_landed")
        for m in range(MT):
            sp.add(lambda e, i, m=m: e.dma_start(A["out"][0, m * P:(m + 1) * P, :], x[:, m, :]), (ready[m],), (out_landed, 16))

        block = ctx.enter_context(nc.Block())

        @block.sync
        def _(eng):
            sp.emit(eng)
            for landed in consts:
                eng.wait_ge(landed, 16)
            eng.wait_ge(out_landed, 16 * MT)

        @block.scalar
        def _(eng):
            act.emit(eng)

        @block.vector
        def _(eng):
            dve.emit(eng)

        @block.tensor
        def _(eng):
            pe.emit(eng)

        @block.gpsimd
        def _(eng):
            pool.emit(eng)


def spans(sizes):
    out, n = {}, 0
    for name, size in sizes:
        out[name] = n
        n += size
    return out, n


TAB, TAB_N = spans([("ident", P), ("le", P), ("ge", P), ("gt", P), ("lt", P), ("flip", P), ("dist", 2 * T), ("window", 2 * T),
                    ("near", 2 * T), ("cos", 2 * HD), ("sin", 2 * HD)])
PAR, PAR_N = spans([("norm_mixer0", KT), ("norm_ffn0", KT), ("norm_mixer1", KT), ("norm_ffn1", KT),
                    ("conv_w", 3 * KT), ("q_gain", 1), ("k_gain", 1), ("ssm_conv_w", SSM_TAPS * 32),
                    ("ssm_conv_b", 32), ("ssm_norm", 16), ("ln1_0", 2 * KT), ("ln2_0", 2 * KT),
                    ("ln1_1", 2 * KT)])
ROW, ROW_N = spans([("sinks1", 16), ("sinks2", 8), ("dt_bias", 64), ("a_log", 64), ("skip", 32)])

TOTAL_CHUNKS = 202
STOPS = [16, 49, 59, 92, 105, 137, 170, 202]


def shape_tables():
    t = np.arange(T)
    a, b = np.arange(P)[:, None], np.arange(P)[None, :]
    out = np.zeros((P, TAB_N), np.float32)

    def put(name, v):
        out[:, TAB[name]:TAB[name] + v.shape[1]] = v

    put("ident", a == b)
    put("le", a <= b)
    put("ge", a >= b)
    put("gt", a > b)
    put("lt", a < b)
    put("flip", a == b // 64 * 64 + 63 - b % 64)
    far = np.float32(1e30)
    rows = lambda v: v.reshape(MT, P, -1).transpose(1, 0, 2).reshape(P, -1)
    dist = (t[:, None] - t[None, :]).astype(np.float32)
    put("dist", rows(np.where((dist >= 0) & (dist < 128), dist, far)))
    put("window", rows(np.where(np.abs(dist) <= 128, np.float32(0), -far)))
    c = t % 64
    start = np.clip(c - 8, 0, 48)
    near = (c[None, :] >= start[:, None]) & (c[None, :] < start[:, None] + 16)
    put("near", rows(np.where(near, np.float32(0), -far)))
    half = HD // 2
    inv = np.float32(10000.0) ** (-np.arange(half, dtype=np.float32) / np.float32(half))
    ang = t.astype(np.float32)[:, None] * inv[None, :].astype(np.float32)
    cos, sin = np.cos(ang).astype(np.float32), np.sin(ang).astype(np.float32)
    put("cos", rows(np.concatenate([cos, cos], 1)))
    put("sin", rows(np.concatenate([-sin, sin], 1)))
    return out


_WEIGHTS = ["x", "conv_w_in", "conv_w_out", "attn_w_qkv", "attn_w_o", "ffn_w_gate_up", "ffn_w_down", "attn_w_in_2",
            "attn_w_out_2", "ssm_w_in_2", "ssm_w_out_2", "mlp_w1_2", "mlp_w2_2", "ln1_g_2", "ln1_b_2", "ln2_g_2",
            "ln2_b_2"]


def kernel(**inputs):
    import concourse.bacc as bacc
    from concourse.bass_utils import run_bass_kernel_spmd

    get = {k: np.asarray(v) for k, v in inputs.items()}

    def by_feature(v):
        return v.reshape(-1, P).T

    arrays = {name: np.ascontiguousarray(get[name]) for name in _WEIGHTS}
    arrays["table"] = shape_tables()
    arrays["params"] = np.ascontiguousarray(np.concatenate([
        by_feature(get["norm_mixer"][0]), by_feature(get["norm_ffn"][0]), by_feature(get["norm_mixer"][1]),
        by_feature(get["norm_ffn"][1]), by_feature(get["conv_w"][0]), by_feature(np.tile(get["attn_q_gain"][0], 2)),
        by_feature(np.tile(get["attn_k_gain"][0], 2)), by_feature(get["ssm_conv_w_2"][0]),
        by_feature(get["ssm_conv_b_2"][0]), by_feature(get["ssm_norm_w_2"][0]),
        *(by_feature(get[f"{name}_2"][layer]) for name, layer in (
            ("ln1_g", 0), ("ln1_b", 0), ("ln2_g", 0), ("ln2_b", 0), ("ln1_g", 1), ("ln1_b", 1)))], 1))
    arrays["rows"] = np.concatenate([get["attn_sinks"][0], get["attn_sink_2"][0], get["ssm_dt_bias_2"][0],
                                     get["ssm_A_log_2"][0].reshape(-1), get["ssm_D_2"][0]])[None, :]
    rpb = get["attn_rpb_2"][0]
    arrays["rpb"] = np.pad(rpb, ((0, 0), (0, 0), (48, 48)))

    nc = bacc.Bacc("TRN2", target_bir_lowering=False, num_devices=1)
    A = {name: nc.dram_tensor(f"in_{name}", a.shape, mybir.dt.from_np(a.dtype), kind="ExternalInput").ap()
         for name, a in arrays.items()}
    A["out"] = nc.dram_tensor("out", get["x"].shape, F32, kind="ExternalOutput").ap()
    build(nc, A, STOP)
    r = run_bass_kernel_spmd(nc, [{f"in_{n}": a for n, a in arrays.items()}], core_ids=[0])
    return r.results[0]["out"]


STOP = None
```
